# Optimizing a Trainium2 kernel written in Bass

```python
import math
import jax, jax.numpy as jnp
from jax import lax
import numpy as np

D_MODEL = 1024
BATCH = 1
SEQ = 256
DEPTH = 2

D_MIX = D_MODEL
POOL_W = D_MIX // 4
SCONV_W = D_MIX // 4
ATTN_W = D_MIX // 4
CONF_W = D_MIX // 4
POOL_WINDOWS = (2, 4, 8, 16)
N_POOL_GROUPS = len(POOL_WINDOWS)
POOL_GROUP = POOL_W // N_POOL_GROUPS
SCONV_K = 3
N_DIFF_HEADS = 4
DIFF_V_DIM = ATTN_W // N_DIFF_HEADS
DIFF_QK_DIM = DIFF_V_DIM // 2
ROPE_DIM = DIFF_QK_DIM // 4
ROPE_THETA = 500000.0
Q_BLOCK = 128
CONF_K = 31
D_FF = 2816
N_EXPERTS = 8
TOP_K = 2
D_FF_EXPERT = 3584
N_DENSE = (DEPTH + 1) // 2
N_MOE = DEPTH // 2
DN_ALPHA = (2 * DEPTH) ** 0.25
DN_BETA = (8 * DEPTH) ** -0.25
LN_EPS = 1e-5
IN_SIZES = (POOL_W,
            SCONV_W, SCONV_W, SCONV_W,
            ATTN_W, ATTN_W, ATTN_W,
            CONF_W, CONF_W)
IN_COLS = sum(IN_SIZES)

kernel_name = "hybrid_pool_sconv_diffattn_conformer_moe"

def layer_norm(x, g, b):
    xf = x.astype(jnp.float32)
    mu = jnp.mean(xf, axis=-1, keepdims=True)
    xc = xf - mu
    var = jnp.mean(xc * xc, axis=-1, keepdims=True)
    return (xc * lax.rsqrt(var + LN_EPS) * g.astype(jnp.float32) + b.astype(jnp.float32)).astype(x.dtype)

def causal_depthwise_conv(x, w):
    k, c = w.shape
    return lax.conv_general_dilated(
        x, w[:, None, :].astype(x.dtype), window_strides=(1,), padding=[(k - 1, 0)],
        dimension_numbers=('NWC', 'WIO', 'NWC'), feature_group_count=c)

def pool_mixer(h, w_pool, pool_scale):
    b, s, c = h.shape
    hf = h.astype(jnp.float32)
    cs = jnp.cumsum(hf, axis=1)
    tpos = jnp.arange(1, s + 1)
    outs = []
    for gi, w in enumerate(POOL_WINDOWS):
        sl = slice(gi * POOL_GROUP, (gi + 1) * POOL_GROUP)
        csg = cs[..., sl]
        lag = jnp.pad(csg, ((0, 0), (w, 0), (0, 0)))[:, :s]
        cnt = jnp.minimum(tpos, w).astype(jnp.float32)[None, :, None]
        outs.append((csg - lag) / cnt - hf[..., sl])
    d = jnp.stack(outs, axis=2).astype(h.dtype)
    y = jnp.einsum('bsgc,gce->bsge', d, w_pool).reshape(b, s, c)
    return y * pool_scale

def short_conv_mixer(gate_b, gate_c, h, w_conv):
    return gate_b * causal_depthwise_conv(gate_c * h, w_conv)

def rope_tables(positions):
    inv = ROPE_THETA ** (-jnp.arange(0, ROPE_DIM, 2, dtype=jnp.float32) / ROPE_DIM)
    ang = positions.astype(jnp.float32)[..., None] * inv
    return jnp.cos(ang), jnp.sin(ang)

def partial_rope(x, cos, sin):
    half = ROPE_DIM // 2
    xr = x[..., :ROPE_DIM].astype(jnp.float32)
    x1, x2 = xr[..., :half], xr[..., half:]
    c = cos[:, :, None, None, :]
    sn = sin[:, :, None, None, :]
    rot = jnp.concatenate([x1 * c - x2 * sn, x2 * c + x1 * sn], axis=-1)
    return jnp.concatenate([rot.astype(x.dtype), x[..., ROPE_DIM:]], axis=-1)

def diff_attention(q, k, v, lam, lam_init, subln_g):
    b, s = q.shape[:2]
    nb = s // Q_BLOCK
    qt = (q * (DIFF_QK_DIM ** -0.5)).transpose(0, 2, 3, 1, 4)
    kt = k.transpose(0, 2, 3, 1, 4)
    vt = v.transpose(0, 2, 1, 3)
    kpos = jnp.arange(s)

    def block(i):
        q0 = i * Q_BLOCK
        qb = lax.dynamic_slice_in_dim(qt, q0, Q_BLOCK, axis=3)
        sc = jnp.einsum('bhmqd,bhmkd->bhmqk', qb, kt).astype(jnp.float32)
        qpos = q0 + jnp.arange(Q_BLOCK)
        sc = jnp.where(kpos[None, :] <= qpos[:, None], sc, -jnp.inf)
        p = jax.nn.softmax(sc, axis=-1)
        a = p[:, :, 0] - lam * p[:, :, 1]
        return jnp.einsum('bhqk,bhke->bhqe', a.astype(v.dtype), vt)

    o = lax.map(block, jnp.arange(nb))
    o = o.transpose(1, 0, 3, 2, 4).reshape(b, s, N_DIFF_HEADS, DIFF_V_DIM)
    of = o.astype(jnp.float32)
    of = of * lax.rsqrt(jnp.mean(of * of, axis=-1, keepdims=True) + LN_EPS) * subln_g.astype(jnp.float32)
    return (of * (1.0 - lam_init)).reshape(b, s, ATTN_W).astype(v.dtype)

def conformer_conv(a, g, w_dw, ln_g, ln_b):
    u = a * jax.nn.sigmoid(g)
    u = causal_depthwise_conv(u, w_dw)
    u = layer_norm(u, ln_g, ln_b)
    return jax.nn.silu(u)

def hybrid_mixer(x, w_in, w_o, pool_w, pool_scale, sconv_w, lam_params, subln_g,
                 conf_dw, conf_ln_g, conf_ln_b, cos, sin, lam_init):
    b, s, _ = x.shape
    z = x @ w_in
    (p_in, sb, scg, sh, qf, kf, vf, ca, cg) = jnp.split(
        z, np.cumsum(IN_SIZES)[:-1].tolist(), axis=-1)
    y_pool = pool_mixer(p_in, pool_w, pool_scale)
    y_sconv = short_conv_mixer(sb, scg, sh, sconv_w)
    q = partial_rope(qf.reshape(b, s, N_DIFF_HEADS, 2, DIFF_QK_DIM), cos, sin)
    k = partial_rope(kf.reshape(b, s, N_DIFF_HEADS, 2, DIFF_QK_DIM), cos, sin)
    v = vf.reshape(b, s, N_DIFF_HEADS, DIFF_V_DIM)
    lp = lam_params.astype(jnp.float32)
    lam = jnp.exp(jnp.sum(lp[0] * lp[1])) - jnp.exp(jnp.sum(lp[2] * lp[3])) + lam_init
    y_attn = diff_attention(q, k, v, lam, lam_init, subln_g)
    y_conf = conformer_conv(ca, cg, conf_dw, conf_ln_g, conf_ln_b)
    y = jnp.concatenate([y_pool, y_sconv, y_attn, y_conf], axis=-1)
    return y @ w_o

def swiglu(x, wg, wu, wd):
    return (jax.nn.silu(x @ wg) * (x @ wu)) @ wd

def moe_swiglu(x, w_router, wg, wu, wd):
    b, s, d = x.shape
    xt = x.reshape(b * s, d)
    logits = (xt @ w_router).astype(jnp.float32)
    top_v, top_i = lax.top_k(logits, TOP_K)
    top_w = jax.nn.softmax(top_v, axis=-1)
    gates = jnp.sum(jax.nn.one_hot(top_i, N_EXPERTS, dtype=jnp.float32) * top_w[..., None], axis=1)
    out = jnp.zeros_like(xt)
    for e in range(N_EXPERTS):
        out = out + gates[:, e:e + 1].astype(x.dtype) * swiglu(xt, wg[e], wu[e], wd[e])
    return out.reshape(b, s, d)

def setup_inputs(seed: int = 0) -> dict:
    key = jax.random.key(seed)
    ks = jax.random.split(key, 32)
    f32 = jnp.float32
    nrm = lambda k, shape, sc: jax.random.normal(k, shape, f32) * sc
    x = jax.random.normal(ks[0], (BATCH, SEQ, D_MODEL), f32)
    offset = jax.random.randint(ks[1], (BATCH, 1), 0, 4096, dtype=jnp.int32)
    positions = (offset + jnp.arange(SEQ, dtype=jnp.int32)[None, :]).astype(jnp.int32)
    return {
        "x": x,
        "positions": positions,
        "w_in": nrm(ks[2], (DEPTH, D_MODEL, IN_COLS), D_MODEL ** -0.5),
        "w_o": nrm(ks[3], (DEPTH, D_MIX, D_MODEL), DN_BETA * D_MIX ** -0.5),
        "pool_w": nrm(ks[4], (DEPTH, N_POOL_GROUPS, POOL_GROUP, POOL_GROUP), POOL_GROUP ** -0.5),
        "pool_scale": 1.0 + nrm(ks[5], (DEPTH, POOL_W), 0.02),
        "sconv_w": nrm(ks[6], (DEPTH, SCONV_K, SCONV_W), SCONV_K ** -0.5),
        "diff_lambda": nrm(ks[7], (DEPTH, 4, DIFF_QK_DIM), 0.1),
        "diff_subln_g": 1.0 + nrm(ks[8], (DEPTH, DIFF_V_DIM), 0.02),
        "conf_dw": nrm(ks[9], (DEPTH, CONF_K, CONF_W), CONF_K ** -0.5),
        "conf_ln_g": 1.0 + nrm(ks[10], (DEPTH, CONF_W), 0.02),
        "conf_ln_b": nrm(ks[11], (DEPTH, CONF_W), 0.02),
        "ln1_g": 1.0 + nrm(ks[12], (DEPTH, D_MODEL), 0.02),
        "ln1_b": nrm(ks[13], (DEPTH, D_MODEL), 0.02),
        "ln2_g": 1.0 + nrm(ks[14], (DEPTH, D_MODEL), 0.02),
        "ln2_b": nrm(ks[15], (DEPTH, D_MODEL), 0.02),
        "ffn_wg": nrm(ks[16], (N_DENSE, D_MODEL, D_FF), D_MODEL ** -0.5),
        "ffn_wu": nrm(ks[17], (N_DENSE, D_MODEL, D_FF), D_MODEL ** -0.5),
        "ffn_wd": nrm(ks[18], (N_DENSE, D_FF, D_MODEL), DN_BETA * D_FF ** -0.5),
        "router_w": nrm(ks[19], (N_MOE, D_MODEL, N_EXPERTS), D_MODEL ** -0.5),
        "moe_wg": nrm(ks[20], (N_MOE, N_EXPERTS, D_MODEL, D_FF_EXPERT), D_MODEL ** -0.5),
        "moe_wu": nrm(ks[21], (N_MOE, N_EXPERTS, D_MODEL, D_FF_EXPERT), D_MODEL ** -0.5),
        "moe_wd": nrm(ks[22], (N_MOE, N_EXPERTS, D_FF_EXPERT, D_MODEL), DN_BETA * D_FF_EXPERT ** -0.5),
    }

def reference(x, positions, w_in, w_o, pool_w, pool_scale, sconv_w, diff_lambda, diff_subln_g,
              conf_dw, conf_ln_g, conf_ln_b, ln1_g, ln1_b, ln2_g, ln2_b,
              ffn_wg, ffn_wu, ffn_wd, router_w, moe_wg, moe_wu, moe_wd):
    cos, sin = rope_tables(positions)
    for l in range(DEPTH):
        lam_init = 0.8 - 0.6 * math.exp(-0.3 * l)
        y = hybrid_mixer(x, w_in[l], w_o[l], pool_w[l], pool_scale[l], sconv_w[l],
                         diff_lambda[l], diff_subln_g[l], conf_dw[l], conf_ln_g[l], conf_ln_b[l],
                         cos, sin, lam_init)
        x = layer_norm(DN_ALPHA * x + y, ln1_g[l], ln1_b[l])
        j = l // 2
        if l % 2 == 0:
            f = swiglu(x, ffn_wg[j], ffn_wu[j], ffn_wd[j])
        else:
            f = moe_swiglu(x, router_w[j], moe_wg[j], moe_wu[j], moe_wd[j])
        x = layer_norm(DN_ALPHA * x + f, ln2_g[l], ln2_b[l])
    return x


_drawn_inputs = setup_inputs


def setup_inputs(seed=0):
    import zlib

    import numpy as np

    out = dict(_drawn_inputs(seed))
    spreads = {}
    factors = {'pool_scale': 6.519,
     'diff_lambda': 3.384,
     'diff_subln_g': 6.417,
     'conf_ln_g': 8.0,
     'conf_ln_b': 8.0}
    for name, (base, spread) in spreads.items():
        noise = np.random.default_rng([zlib.crc32(name.encode()), seed]).standard_normal(out[name].shape)
        drawn = base * np.exp(spread * noise) if base else spread * noise
        out[name] = __import__('jax').numpy.asarray(drawn.astype(out[name].dtype))
    for name, factor in factors.items():
        out[name] = (out[name] * factor).astype(out[name].dtype)
    return out
```

```python
from contextlib import ExitStack

import numpy as np

import concourse.bass as bass
from concourse import mybir

F32 = mybir.dt.float32
F32R = mybir.dt.float32r
I32 = mybir.dt.int32
ALU = mybir.AluOpType
ACT = mybir.ActivationFunctionType
AX_X = mybir.AxisListType.X

P = 128
D = 1024
SEQ = 256
DEPTH = 2
TT = SEQ // P
KT = D // P
GW = 256
WINDOWS = (2, 4, 8, 16)
SCONV_K = 3
CONF_K = 31
HEADS = 4
MAPS = 2 * HEADS
QK = 32
VD = 64
ROPE_DIM = QK // 4
THETA = 500000.0
D_FF = 2816
NE = 8
FE = 3584
ALPHA = (2 * DEPTH) ** 0.25
EPS = 1e-5
SCALE = float(QK) ** -0.5
LAM_INIT = [0.8 - 0.6 * float(np.exp(-0.3 * l)) for l in range(DEPTH)]

UNIT = 2048
RAW_SLOTS = 7
SPLIT_SLOTS = 3

POOL_G, SB_G, SCG_G, SH_G, Q_G, K_G, V_G, CA_G, CG_G = range(9)
Z_ORDER = [CA_G, CG_G, Q_G, K_G, V_G, POOL_G, SB_G, SCG_G, SH_G]
NZ = len(Z_ORDER)
WO_ORDER = [0, 1, 3, 2]
NWO = len(WO_ORDER)
FP = D_FF // GW
DENSE_ORDER = [("g", 0), ("u", 0)]
for _j in range(1, FP):
    DENSE_ORDER += [("g", _j), ("u", _j), ("d", _j - 1)]
DENSE_ORDER += [("d", FP - 1)]

CW = 512
NC = FE // CW
MOE_ORDER = []
for _c in range(NC):
    MOE_ORDER += [("g", _c, 0), ("g", _c, 1), ("u", _c, 0), ("u", _c, 1)]
    if _c:
        MOE_ORDER += [("d", _c - 1, 0), ("d", _c - 1, 1)]
MOE_ORDER += [("d", NC - 1, 0), ("d", NC - 1, 1)]
NU = len(MOE_ORDER)
assert NU % RAW_SLOTS == 0 and NU % SPLIT_SLOTS == 0
MOE_POS = {u: i for i, u in enumerate(MOE_ORDER)}
COMB_BANKS = (5, 6, 7, 4)
MAX_ITEMS = NE + 3

Z_UNIT = [0, NZ + NWO + len(DENSE_ORDER)]
WO_UNIT = [z + NZ for z in Z_UNIT]
FFN_UNIT = [z + NZ + NWO for z in Z_UNIT]
MOE_UNIT = FFN_UNIT[1]



def dense_unit(kind, j):
    return FFN_UNIT[0] + DENSE_ORDER.index((kind, j))


R_DW, R_SW, R_PS, R_LG, R_LB, R_SG = 0, 62, 68, 70, 72, 74
NR = 75


def _constants():
    at, parts, n = {}, [], 0

    def put(name, a):
        nonlocal n
        a = np.asarray(a, np.float32).reshape(P, -1)
        at[name] = (n, a.shape[1])
        parts.append(a)
        n += a.shape[1]

    i = np.arange(P)
    put("ident", np.eye(P))
    put("tri", (i[:, None] <= i[None, :]))
    put("ones", np.ones((P, P)))
    put("mean", np.full((P, P), 1.0 / GW))
    half = ROPE_DIM // 2
    rot = np.zeros((P, P))
    for c in range(P):
        if c % QK < half:
            rot[c + half, c] = -1.0
        elif c % QK < ROPE_DIM:
            rot[c - half, c] = 1.0
    put("rot", rot)
    put("iota", np.broadcast_to(np.arange(P), (P, P)))
    put("causal", np.concatenate([np.zeros((P, P)), np.where(i[None, :] <= i[:, None], 0.0, -1e30)], 1))
    t = np.arange(1, SEQ + 1)
    counts = np.stack([np.minimum(t[None, :], np.repeat(WINDOWS[2 * h:2 * h + 2], 64)[:, None]) for h in range(2)], 1)
    put("rcount", np.float32(1.0) / counts.astype(np.float32))
    inv = np.float32(THETA) ** (-np.arange(0, ROPE_DIM, 2, dtype=np.float32) / np.float32(ROPE_DIM))
    in_rope = (i % QK < ROPE_DIM)
    put("inv", np.where(in_rope, inv[i % half], 0.0))
    put("roped", in_rope)
    put("unroped", ~in_rope)
    e = np.arange(NE)
    put("before", np.broadcast_to((e[None, :] < e[:, None]).ravel(), (P, NE * NE)))
    put("upto", np.broadcast_to((e[None, :] <= e[:, None]).ravel(), (P, NE * NE)))
    put("experts", np.broadcast_to(e, (P, NE)))
    put("spill", np.broadcast_to(np.repeat(np.arange(1, 4), NE), (P, 3 * NE)))
    put("minus_half", np.full((P, 4), -0.5))
    put("eps", np.full((P, 1), EPS))
    return at, np.ascontiguousarray(np.concatenate(parts, 1))


CONST_AT, CONSTANTS = _constants()

TWO_PI = 2.0 * np.pi
TURN = []
_rest = TWO_PI
for _ in range(3):
    _step = 2.0 ** (np.floor(np.log2(_rest)) - 7)
    TURN.append(float(np.floor(_rest / _step) * _step))
    _rest -= TURN[-1]
TURN.append(float(np.float32(_rest)))
MAGIC = 1.5 * 2.0 ** 23
PI_IN = 3.1415925


def hybrid_trunk(nc, consts, x, positions, w_in, w_o, pool_w, pool_scale, sconv_w, diff_lambda, diff_subln_g,
                 conf_dw, conf_ln_g, conf_ln_b, ln1_g, ln1_b, ln2_g, ln2_b, ffn_wg, ffn_wu, ffn_wd,
                 router_w, moe_wg, moe_wu, moe_wd, out):
    with ExitStack() as ctx:
        def sb(name, shape, dt=F32):
            return ctx.enter_context(nc.sbuf_tensor(name, shape, dt))

        def sem(name):
            return ctx.enter_context(nc.semaphore(name))

        bank = [ctx.enter_context(nc.psum_tensor(f"bank{b}", [P, 512], F32)) for b in range(8)]
        raw = sb("raw", [P, RAW_SLOTS, UNIT])
        w_hi = sb("w_hi", [P, SPLIT_SLOTS, UNIT], F32R)
        w_lo = sb("w_lo", [P, SPLIT_SLOTS, UNIT], F32R)
        a_hi = sb("a_hi", [P, KT, SEQ], F32R)
        a_lo = sb("a_lo", [P, KT, SEQ], F32R)
        h_hi = sb("h_hi", [P, 2, 512], F32R)
        h_lo = sb("h_lo", [P, 2, 512], F32R)
        router_hi = sb("router_hi", [P, KT, NE], F32R)
        router_lo = sb("router_lo", [P, KT, NE], F32R)
        xs = sb("xs", [P, TT, D])
        cst = sb("cst", [P, CONSTANTS.shape[1]])
        ln_gb = sb("ln_gb", [P, 2, D])
        rope_cs = sb("rope_cs", [P, 2, SEQ])
        cols = sb("cols", [P, DEPTH, NR])
        pool_mat = sb("pool_mat", [P, DEPTH, 2, P])
        lam_exp = sb("lam_exp", [P, DEPTH, 2])
        neg_lam = sb("neg_lam", [P, DEPTH])
        stats = sb("stats", [P, TT, 2, 6])
        mean_var = sb("mean_var", [P, TT, 2])
        rstd = sb("rstd", [P, TT])
        row_max = sb("row_max", [P, 2, MAPS])
        row_sum = sb("row_sum", [P, 2, MAPS])
        row_inv = sb("row_inv", [P, 2, MAPS])
        head_ms = sb("head_ms", [P, TT, HEADS])
        slot_of = sb("slot_of", [P, TT, 12])
        gate_of = sb("gate_of", [P, TT, 12])
        item_tab = sb("item_tab", [P, 16])
        item_int = sb("item_int", [P, 16], I32)
        work = sb("work", [P, 12448])

        def c(name, parts=P):
            at, n = CONST_AT[name]
            return cst[0:parts, at:at + n]

        def w(at, n, parts=P):
            return work[0:parts, at:at + n]

        z_at = {CA_G: 0, CG_G: 512, Q_G: 1024, K_G: 1536, SB_G: 2048, SCG_G: 2560, SH_G: 3072, V_G: 3584}
        z = {g: w(at, 512).rearrange("p (h t) -> p h t", h=2) for g, at in z_at.items()}
        CPAD, PPAD, SPAD = CONF_K - 1, 16, SCONV_K - 1
        conf_u = w(4096, 2 * (SEQ + CPAD)).rearrange("p (h t) -> p h t", h=2)
        conf_acc = w(4668, 512).rearrange("p (h t) -> p h t", h=2)
        pool_h = w(5180, 2 * (SEQ + PPAD)).rearrange("p (h t) -> p h t", h=2)
        pool_s = [w(5724 + 544 * b, 544).rearrange("p (h t) -> p h t", h=2) for b in range(2)]
        sconv_u = w(6812, 2 * (SEQ + SPAD)).rearrange("p (h t) -> p h t", h=2)
        sc = w(7328, 2048)
        a_mix = w(9376, 1024)
        y32 = w(10400, 2048).rearrange("p (k t) -> p k t", k=KT)
        xc, xsq = z[CA_G], z[CG_G]
        s_acc, s_tmp = z[SH_G], z[SCG_G]
        rope_rs = sc[:, 0:1024].rearrange("p (g h t) -> p g h t", g=2, h=2)
        rope_qc = sc[:, 1024:2048].rearrange("p (g h t) -> p g h t", g=2, h=2)
        aT = [w(5724, 512), w(1024, 1024)]
        o_sb = sc[:, 0:512].rearrange("p (q h e) -> p q h e", q=2, h=HEADS)
        o_sq = sc[:, 512:1024].rearrange("p (q h e) -> p q h e", q=2, h=HEADS)
        rows = sc[:, 0:DEPTH * P].rearrange("p (l n) -> p l n", l=DEPTH)
        lam_in = a_mix[:, 0:DEPTH * 128].rearrange("p (l a b n) -> p (l a) b n", l=DEPTH, a=2, b=2)
        lam_prod = a_mix[:, 256:384].rearrange("p (l n) -> p l n", n=QK)
        lam_sum = a_mix[:, 384:388]
        pos_int = work[:, 10400:10656].bitcast(I32)
        angle = w(10656, 256)
        trig = w(10912, 512).rearrange("p (h t) -> p h t", h=2)
        turns = w(11424, 512).rearrange("p (h t) -> p h t", h=2)
        part = w(11936, 512).rearrange("p (h t) -> p h t", h=2)
        d_act = w(0, 1024).rearrange("p (b n) -> p b n", b=2)
        d_h = w(1024, 1024).rearrange("p (b n) -> p b n", b=2)
        m_act = w(0, 1024).rearrange("p (b n) -> p b n", b=2)
        m_h = w(1024, 1024).rearrange("p (b n) -> p b n", b=2)
        one_hot = w(2048, 256).rearrange("p (t s) -> p t s", t=TT)
        gated = w(2304, 256).rearrange("p (t s) -> p t s", t=TT)
        gatedT = w(2560, 256)
        y_sb = w(2816, 1024)
        acc = w(3840, 2048).rearrange("p (t n) -> p t n", t=TT)
        router_raw = w(5888, KT * NE).rearrange("p (k e) -> p k e", k=KT)
        logits = w(5952, 16).rearrange("p (t e) -> p t e", t=TT)
        mask = w(5968, 16).rearrange("p (t e) -> p t e", t=TT)
        gates = w(5984, 16).rearrange("p (t e) -> p t e", t=TT)
        expl = w(6000, 16).rearrange("p (t e) -> p t e", t=TT)
        rank = w(6016, 16).rearrange("p (t e) -> p t e", t=TT)
        top = w(6032, 2)
        denom = w(6034, 2)
        rdenom = w(6036, 2)
        slots = w(6040, 16).rearrange("p (t e) -> p t e", t=TT)
        over = w(6056, 8)
        cum_over = w(6064, 8)
        pairs = w(6072, 64)
        pairs2 = w(6200, 64)
        chosen = w(6328, 24).rearrange("p (j e) -> p j e", j=3)
        picked = w(6352, 24).rearrange("p (j e) -> p j e", j=3)

        raw_loaded = [sem(f"raw_loaded{s}") for s in range(RAW_SLOTS)]
        w_hi_ready, w_lo_ready, w_used = sem("w_hi_ready"), sem("w_lo_ready"), sem("w_used")
        consts_loaded, x_loaded, pos_loaded = sem("consts_loaded"), sem("x_loaded"), sem("pos_loaded")
        rows_loaded, lam_loaded, pool_loaded = sem("rows_loaded"), sem("lam_loaded"), sem("pool_loaded")
        router_loaded, ln_loaded, stored = sem("router_loaded"), sem("ln_loaded"), sem("stored")
        cols_psum, cols_ready = sem("cols_psum"), sem("cols_ready")
        pads_zeroed = sem("pads_zeroed")
        lam_summed, lam_exped = sem("lam_summed"), sem("lam_exped")
        angles_ready, sines_ready, rope_ready = sem("angles_ready"), sem("sines_ready"), sem("rope_ready")
        xt_psum, xt_hi, xt_lo = sem("xt_psum"), sem("xt_hi"), sem("xt_lo")
        z_ready = sem("z_ready")
        rot_psum, rope_scaled, roped = sem("rot_psum"), sem("rope_scaled"), sem("roped")
        conf_conv, conf_mean, conf_sq, conf_var = sem("conf_conv"), sem("conf_mean"), sem("conf_sq"), sem("conf_var")
        conf_std, conf_normed, conf_y = sem("conf_std"), sem("conf_normed"), sem("conf_y")
        pool_diff, pool_psum, pool_y, sconv_y = sem("pool_diff"), sem("pool_psum"), sem("pool_y"), sem("sconv_y")
        scores_psum, scores_max, probs_ready = sem("scores_psum"), sem("scores_max"), sem("probs_ready")
        mixed, aT_psum, aT_ready = sem("mixed"), sem("aT_psum"), sem("aT_ready")
        o_psum, o_copied, o_ms, o_rstd = sem("o_psum"), sem("o_copied"), sem("o_ms"), sem("o_rstd")
        o_normed, oT_psum, o_y = sem("o_normed"), sem("oT_psum"), sem("o_y")
        y_hi, y_lo, wo_psum = sem("y_hi"), sem("y_lo"), sem("wo_psum")
        ln_var, ln_rstd, x_ready = sem("ln_var"), sem("ln_rstd"), sem("x_ready")
        g_act, h_ready = sem("g_act"), sem("h_ready")
        h_hi_ready, h_lo_ready, ffn_psum = sem("h_hi_ready"), sem("h_lo_ready"), sem("ffn_psum")
        router_split, logits_psum, logits_off, logits_exp = sem("router_split"), sem("logits_psum"), sem("logits_off"), sem("logits_exp")
        mask_ready, ranks_psum, routed = sem("mask_ready"), sem("ranks_psum"), sem("routed")
        hot_ready, gather_psum, item_hi, item_lo = sem("hot_ready"), sem("gather_psum"), sem("item_hi"), sem("item_lo")
        gated_ready, gT_psum, gT_ready = sem("gated_ready"), sem("gT_psum"), sem("gT_ready")
        mg_act, mh_ready = sem("mg_act"), sem("mh_ready")
        mhT_psum, mh_hi, mh_lo, my_ready = sem("mhT_psum"), sem("mh_hi"), sem("mh_lo"), sem("my_ready")
        comb_psum, acc_ready = sem("comb_psum"), sem("acc_ready")
        dve_step, pool_step = sem("dve_step"), sem("pool_step")

        def z_src(l, g):
            return w_in[l].rearrange("(k p) n -> p k n", p=P)[:, :, g * GW:(g + 1) * GW]

        def wo_src(l, pair):
            return w_o[l].rearrange("(k p) n -> p k n", p=P)[:, 2 * pair:2 * pair + 2, :]

        def dense_src(kind, j):
            if kind == "d":
                return ffn_wd[0].rearrange("(k p) n -> p k n", p=P)[:, 2 * j:2 * j + 2, :]
            m = ffn_wg if kind == "g" else ffn_wu
            return m[0].rearrange("(k p) n -> p k n", p=P)[:, :, j * GW:(j + 1) * GW]

        def moe_src(e, kind, ch, part_):
            if kind == "d":
                m = moe_wd[0, bass.ds(e, 1)].rearrange("a (k p) n -> p (a k) n", p=P)
                k0 = ch * (CW // P) + 2 * part_
                return m[:, k0:k0 + 2, :]
            m = moe_wg if kind == "g" else moe_wu
            m = m[0, bass.ds(e, 1)].rearrange("a (k p) n -> p (a k) n", p=P)
            return m[:, 4 * part_:4 * part_ + 4, ch * CW:(ch + 1) * CW]

        def tiles(slot, k):
            return slot.rearrange("p (k n) -> p k n", k=k)

        def split_pair(n, k):
            s = n % SPLIT_SLOTS
            return tiles(w_hi[:, s, :], k), tiles(w_lo[:, s, :], k)

        FIRST_UNITS = []
        for l in range(DEPTH):
            FIRST_UNITS += [(z_src(l, g), KT) for g in Z_ORDER]
            FIRST_UNITS += [(wo_src(l, pair), 2) for pair in WO_ORDER]
            if l == 0:
                FIRST_UNITS += [(dense_src(kind, j), 2 if kind == "d" else KT) for kind, j in DENSE_ORDER]
        assert len(FIRST_UNITS) == MOE_UNIT

        block = ctx.enter_context(nc.Block())

        @block.sync
        def _(sp):
            for t in range(TT):
                sp.dma_start(xs[:, t, :], x[0, t * P:(t + 1) * P, :]).then_inc(x_loaded, 16)
            for n, (src, k) in enumerate(FIRST_UNITS):
                if n >= RAW_SLOTS:
                    sp.wait_ge(w_lo_ready, n - RAW_SLOTS + 1)
                sp.dma_start(tiles(raw[:, n % RAW_SLOTS, :], k), src).then_inc(raw_loaded[n % RAW_SLOTS], 16)

            def load_item(e, before):
                for i, (kind, ch, half) in enumerate(MOE_ORDER):
                    n = MOE_UNIT + i
                    sp.wait_ge(w_lo_ready, before + (n - RAW_SLOTS + 1))
                    sp.dma_start(tiles(raw[:, n % RAW_SLOTS, :], 2 if kind == "d" else 4),
                                 moe_src(e, kind, ch, half)).then_inc(raw_loaded[n % RAW_SLOTS], 16)

            load_item(0, 0)
            sp.wait_ge(routed, 1)
            items = sp.value_load(item_int[0:1, 12:13], min_val=NE, max_val=MAX_ITEMS)
            with sp.Fori(1, items) as item:
                e = sp.value_load(item_int[0:1, bass.ds(item, 1)], min_val=0, max_val=NE - 1)
                load_item(e, item * NU)
            for t in range(TT):
                sp.wait_ge(x_ready, 3 * TT + t + 1)
                sp.dma_start(out[0, t * P:(t + 1) * P, :], xs[:, t, :]).then_inc(stored, 16)
            sp.wait_ge(stored, 16 * TT)

        @block.gpsimd
        def _(pool):
            steps = [0]

            def step(ins):
                steps[0] += 1
                ins.then_inc(pool_step, 1)
                pool.wait_ge(pool_step, steps[0])

            nc.gpsimd.memset(conf_u[:, :, 0:CPAD], 0.0).then_inc(pads_zeroed, 1)
            nc.gpsimd.memset(pool_h[:, :, 0:PPAD], 0.0).then_inc(pads_zeroed, 1)
            nc.gpsimd.memset(sconv_u[:, :, 0:SPAD], 0.0).then_inc(pads_zeroed, 1)
            step(nc.gpsimd.memset(pool_mat[:], 0.0))
            for l in range(DEPTH):
                for h in range(2):
                    for b in range(2):
                        pool.dma_start(pool_mat[64 * b:64 * b + 64, l, h, 64 * b:64 * b + 64],
                                       pool_w[l, 2 * h + b]).then_inc(pool_loaded, 16)

            pool.wait_ge(consts_loaded, 16)
            pool.wait_ge(pos_loaded, 16)
            step(nc.gpsimd.tensor_copy(angle, pos_int))
            step(nc.gpsimd.tensor_scalar(angle, angle, c("inv"), None, ALU.mult))
            for h in range(2):
                step(nc.gpsimd.tensor_scalar(turns[:, h, :], angle, 1.0 / TWO_PI, 0.25 * h, ALU.mult, ALU.add))
            step(nc.gpsimd.tensor_scalar(turns, turns, MAGIC, -MAGIC, ALU.add, ALU.add))
            for j, piece in enumerate(TURN):
                step(nc.gpsimd.tensor_scalar(part, turns, piece, None, ALU.mult))
                for h in range(2):
                    step(nc.gpsimd.tensor_tensor(trig[:, h, :], angle if j == 0 else trig[:, h, :], part[:, h, :], ALU.subtract))
            step(nc.gpsimd.tensor_scalar(trig[:, 1, :], trig[:, 1, :], 0.5 * np.pi, None, ALU.add))
            nc.gpsimd.tensor_scalar(trig, trig, PI_IN, -PI_IN, ALU.min, ALU.max).then_inc(angles_ready, 1)
            pool.wait_ge(sines_ready, 1)
            nc.gpsimd.tensor_scalar(rope_cs[:, 1, :], rope_cs[:, 1, :], c("roped"), c("unroped"), ALU.mult,
                                    ALU.add).then_inc(rope_ready, 1)

            def short_window(l):
                pool.wait_ge(z_ready, NZ * l + 9)
                step(nc.gpsimd.tensor_tensor(sconv_u[:, :, SPAD:], z[SCG_G], z[SH_G], ALU.mult))
                for h in range(2):
                    for j in range(SCONV_K):
                        to = s_acc if j == 0 else s_tmp
                        tap = cols[:, l, R_SW + 2 * j + h:R_SW + 2 * j + h + 1]
                        step(nc.gpsimd.tensor_scalar(to[:, h, :], sconv_u[:, h, j:j + SEQ], tap, None, ALU.mult))
                        if j:
                            step(nc.gpsimd.tensor_tensor(s_acc[:, h, :], s_acc[:, h, :], s_tmp[:, h, :], ALU.add))
                nc.gpsimd.tensor_tensor(y32[:, 2:4, :], s_acc, z[SB_G], ALU.mult).then_inc(sconv_y, 1)

            def window_sums(l):
                pool.wait_ge(z_ready, NZ * l + Z_ORDER.index(POOL_G) + 1)
                src, first = pool_h, 1
                for n, width in enumerate(WINDOWS):
                    dst = pool_s[n % 2]
                    step(nc.gpsimd.tensor_tensor(dst[:, :, first:], src[:, :, first:],
                                                 src[:, :, first - width // 2:SEQ + PPAD - width // 2], ALU.add))
                    h, lo = n // 2, 64 * (n % 2)
                    step(nc.gpsimd.tensor_tensor(y32[lo:lo + 64, h, :], dst[lo:lo + 64, h, PPAD:],
                                                 c("rcount")[lo:lo + 64, h * SEQ:(h + 1) * SEQ], ALU.mult))
                    src, first = dst, first + width
                nc.gpsimd.tensor_tensor(y32[:, 0:2, :], y32[:, 0:2, :], pool_h[:, :, PPAD:], ALU.subtract).then_inc(pool_diff, 1)

            def inverse_roots(n):
                for t in range(TT):
                    pool.wait_ge(ln_var, TT * n + t + 1)
                    nc.gpsimd.tensor_tensor(rstd[:, t:t + 1], mean_var[:, t, 1:2], c("minus_half")[:, 0:1],
                                            ALU.pow).then_inc(ln_rstd, 1)

            for l in range(DEPTH):
                for n, g in enumerate((Q_G, K_G)):
                    pool.wait_ge(z_ready, NZ * l + Z_ORDER.index(g) + 1)
                    cos = rope_cs[:, 1:2, :].broadcast_to((P, 2, SEQ))
                    if l == 0 and n == 0:
                        pool.wait_ge(rope_ready, 1)
                        pool.wait_ge(cols_ready, DEPTH)
                    nc.gpsimd.tensor_tensor(rope_qc[:, n], z[g], cos, ALU.mult).then_inc(rope_scaled, 1)
                window_sums(l)
                short_window(l)
                for q in range(TT):
                    pool.wait_ge(o_ms, TT * l + q + 1)
                    nc.gpsimd.tensor_tensor(head_ms[:, q, :], head_ms[:, q, :], c("minus_half"), ALU.pow).then_inc(o_rstd, 1)
                inverse_roots(2 * l)
                inverse_roots(2 * l + 1)

        @block.scalar
        def _(act):
            act.dma_start(cst[:], consts).then_inc(consts_loaded, 16)
            for l in range(DEPTH):
                act.dma_start(rows[R_DW:R_DW + 62, l, :], conf_dw[l].rearrange("j (h c) -> (j h) c", h=2)).then_inc(rows_loaded, 16)
                act.dma_start(rows[R_SW:R_SW + 6, l, :], sconv_w[l].rearrange("j (h c) -> (j h) c", h=2)).then_inc(rows_loaded, 16)
                for r, m in ((R_PS, pool_scale), (R_LG, conf_ln_g), (R_LB, conf_ln_b)):
                    act.dma_start(rows[r:r + 2, l, :], m[l].rearrange("(h c) -> h c", h=2)).then_inc(rows_loaded, 16)
                for b in range(2):
                    act.dma_start(rows[R_SG:R_SG + 1, l, 64 * b:64 * b + 64], diff_subln_g[l:l + 1, :]).then_inc(rows_loaded, 16)
            act.dma_start(pos_int, positions[0].partition_broadcast(P)).then_inc(pos_loaded, 16)
            act.dma_start(a_mix[:, 0:DEPTH * 128], diff_lambda.rearrange("l a n -> (l a n)").partition_broadcast(P)).then_inc(lam_loaded, 16)

            units = [0]

            def hi_of_unit(count=1):
                for _ in range(count):
                    n = units[0]
                    units[0] += 1
                    act.wait_ge(raw_loaded[n % RAW_SLOTS], 16 * (n // RAW_SLOTS + 1))
                    if n >= SPLIT_SLOTS:
                        act.wait_ge(w_used, n - SPLIT_SLOTS + 1)
                    nc.scalar.activation(w_hi[:, n % SPLIT_SLOTS, :], raw[:, n % RAW_SLOTS, :], ACT.Copy).then_inc(w_hi_ready, 1)

            def load_ln(n):
                if n:
                    act.wait_ge(x_ready, TT * n)
                g, b = ((ln1_g, ln1_b), (ln2_g, ln2_b))[n % 2]
                for j, m in enumerate((g, b)):
                    act.dma_start(ln_gb[:, j, :], m[n // 2].partition_broadcast(P)).then_inc(ln_loaded, 16)

            def hi_of_x(n):
                for q in range(4):
                    t, k = q // 2, 4 * (q % 2)
                    act.wait_ge(xt_psum, 4 * n + q + 1)
                    nc.scalar.activation(a_hi[:, k:k + 4, t * P:(t + 1) * P], tiles(bank[q][:], 4), ACT.Copy).then_inc(xt_hi, 1)

            def z_out(l, i):
                g = Z_ORDER[i]
                act.wait_ge(w_used, Z_UNIT[l] + i + 1)
                to = pool_h[:, :, PPAD:] if g == POOL_G else z[g]
                nc.scalar.activation(to, tiles(bank[4 + i % 4][:], 2), ACT.Sigmoid if g == CG_G else ACT.Copy).then_inc(z_ready, 1)

            def probs(l, q):
                width = P * (q + 1)
                act.wait_ge(scores_max, 2 * l + q + 1)
                view = sc[:, 0:MAPS * width].rearrange("p (m k) -> p m k", m=MAPS)
                for m in range(MAPS):
                    nc.scalar.activation(view[:, m, :], view[:, m, :], ACT.Exp, bias=row_max[:, q, m:m + 1], scale=SCALE,
                                         accum_out=row_sum[:, q, m:m + 1]).then_inc(probs_ready, 1)

            def aT_out(l, q):
                if q == 0:
                    act.wait_ge(pool_diff, l + 1)
                for n, b in enumerate(([2], [3, 0])[q]):
                    act.wait_ge(aT_psum, 3 * l + q + n + 1)
                    nc.scalar.activation(aT[q][:, 512 * n:512 * n + 512], bank[b][:], ACT.Copy).then_inc(aT_ready, 1)

            def hi_of_y(l, n):
                pair = WO_ORDER[n]
                act.wait_ge((pool_y, sconv_y, o_y, conf_y)[pair], l + 1)
                act.wait_ge(w_used, WO_UNIT[l])
                nc.scalar.activation(a_hi[:, 2 * pair:2 * pair + 2, :], y32[:, 2 * pair:2 * pair + 2, :], ACT.Copy).then_inc(y_hi, 1)

            for l in range(DEPTH):
                if l == 0:
                    load_ln(0)
                    hi_of_unit(2)
                    hi_of_x(0)
                    for k in range(DEPTH):
                        act.wait_ge(cols_psum, k + 1)
                        nc.scalar.activation(cols[:, k, :], bank[4 + k][:, 0:NR], ACT.Copy).then_inc(cols_ready, 1)
                    act.wait_ge(lam_summed, 1)
                    nc.scalar.activation(lam_exp.rearrange("p l n -> p (l n)"), lam_sum, ACT.Exp).then_inc(lam_exped, 1)
                    act.wait_ge(angles_ready, 1)
                    nc.scalar.activation(rope_cs[:], trig, ACT.Sin).then_inc(sines_ready, 1)
                else:
                    hi_of_x(2)
                    load_ln(2)
                hi_of_unit(1)
                for i in range(NZ):
                    z_out(l, i)
                    hi_of_unit(1)
                    if i == 7:
                        probs(l, 0)
                aT_out(l, 0)
                hi_of_y(l, 0)
                hi_of_y(l, 1)
                probs(l, 1)
                act.wait_ge(conf_var, l + 1)
                nc.scalar.activation(xsq[:, 0, :], bank[1][:, 256:512], ACT.Sqrt, bias=c("eps")).then_inc(conf_std, 1)
                act.wait_ge(conf_normed, l + 1)
                for h in range(2):
                    last = nc.scalar.activation(y32[:, 6 + h, :], xc[:, h, :], ACT.Silu, bias=cols[:, l, R_LB + h:R_LB + h + 1],
                                                scale=cols[:, l, R_LG + h:R_LG + h + 1])
                last.then_inc(conf_y, 1)
                hi_of_y(l, 2)
                aT_out(l, 1)
                act.wait_ge(o_psum, l + 1)
                for q in range(TT):
                    nc.scalar.activation(o_sb[:, q].rearrange("p h e -> p (h e)"), bank[1][:, 256 * q:256 * q + 256], ACT.Copy).then_inc(o_copied, 1)
                hi_of_unit(1)
                hi_of_y(l, 3)
                if l == 0:
                    hi_of_unit(2)
                hi_of_x(2 * l + 1)
                load_ln(2 * l + 1)
                if l == 0:
                    hi_of_unit(1)
                    for j in range(FP + 1):
                        if 0 < j < FP:
                            hi_of_unit(1)
                        if j:
                            act.wait_ge(h_ready, j)
                            nc.scalar.activation(h_hi[:, (j - 1) % 2, :], d_h[:, (j - 1) % 2, :], ACT.Copy).then_inc(h_hi_ready, 1)
                        if 0 < j < FP:
                            hi_of_unit(1)
                        if j < FP:
                            act.wait_ge(w_used, dense_unit("g", j) + 1)
                            nc.scalar.activation(d_act[:, j % 2, :], bank[2 * (j % 2)][:], ACT.Silu).then_inc(g_act, 1)
                        if 0 < j < FP:
                            hi_of_unit(1)
                    hi_of_unit(2)
            assert units[0] == MOE_UNIT, (units, MOE_UNIT)

            act.wait_ge(ln_var, 2 * TT + 1)
            act.dma_start(router_raw, router_w[0].rearrange("(k p) e -> p k e", p=P)).then_inc(router_loaded, 16)
            act.wait_ge(router_loaded, 16)
            nc.scalar.activation(router_hi[:], router_raw, ACT.Copy).then_inc(router_split, 1)
            act.wait_ge(logits_off, 1)
            nc.scalar.activation(expl, expl, ACT.Exp).then_inc(logits_exp, 1)

            def hi_of_item(before):
                act.wait_ge(gather_psum, before + 1)
                for h, b in enumerate((1, 3)):
                    last = nc.scalar.activation(a_hi[:, 4 * h:4 * h + 4, 0:P], tiles(bank[b][:], 4), ACT.Copy)
                last.then_inc(item_hi, 1)

            def hi_of_moe(unit, item):
                n = MOE_UNIT + MOE_POS[unit]
                act.wait_ge(raw_loaded[n % RAW_SLOTS], item * (16 * NU // RAW_SLOTS) + 16 * (n // RAW_SLOTS + 1))
                act.wait_ge(w_used, item * NU + (n - SPLIT_SLOTS + 1))
                nc.scalar.activation(w_hi[:, n % SPLIT_SLOTS, :], raw[:, n % RAW_SLOTS, :], ACT.Copy).then_inc(w_hi_ready, 1)

            def y_out(before):
                act.wait_ge(w_used, before * NU + MOE_UNIT)
                for h in range(2):
                    last = nc.scalar.activation(y_sb[:, 512 * h:512 * h + 512], bank[5 + h][:], ACT.Copy)
                last.then_inc(my_ready, 1)

            hi_of_item(0)
            act.wait_ge(routed, 1)
            items = act.value_load(item_int[0:1, 12:13], min_val=NE, max_val=MAX_ITEMS)
            with act.Fori(0, items) as item:
                for ch in range(NC + 1):
                    if ch < NC:
                        hi_of_moe(("g", ch, 0), item)
                        hi_of_moe(("g", ch, 1), item)
                        hi_of_moe(("u", ch, 0), item)
                        if ch == 0:
                            y_out(item)
                        hi_of_moe(("u", ch, 1), item)
                    else:
                        hi_of_item(item + 1)
                    if ch:
                        act.wait_ge(mhT_psum, item * NC + ch)
                        nc.scalar.activation(h_hi[:, 0, :], bank[4][:], ACT.Copy).then_inc(mh_hi, 1)
                    if ch < NC:
                        act.wait_ge(w_used, item * NU + (MOE_UNIT + MOE_POS["g", ch, 1] + 1))
                        nc.scalar.activation(m_act[:, ch % 2, :], bank[ch % 2][:], ACT.Silu).then_inc(mg_act, 1)
                    if ch == 3:
                        act.wait_ge(gT_psum, item + 1)
                        nc.scalar.activation(gatedT, bank[7][:, 0:256], ACT.Copy).then_inc(gT_ready, 1)
                    if ch:
                        hi_of_moe(("d", ch - 1, 0), item)
                        hi_of_moe(("d", ch - 1, 1), item)
            y_out(items)

        @block.vector
        def _(dve):
            steps, units = [0], [0]

            def step(ins):
                steps[0] += 1
                ins.then_inc(dve_step, 1)
                dve.wait_ge(dve_step, steps[0])

            def lo_of_unit(count=1):
                for _ in range(count):
                    n = units[0]
                    units[0] += 1
                    dve.wait_ge(w_hi_ready, n + 1)
                    s = n % SPLIT_SLOTS
                    nc.vector.tensor_tensor(w_lo[:, s, :], raw[:, n % RAW_SLOTS, :], w_hi[:, s, :].bitcast(F32),
                                            ALU.subtract).then_inc(w_lo_ready, 1)

            def lo_of_x(n):
                for q in range(4):
                    t, k = q // 2, 4 * (q % 2)
                    dve.wait_ge(xt_hi, 4 * n + q + 1)
                    at = (slice(None), slice(k, k + 4), slice(t * P, (t + 1) * P))
                    nc.vector.tensor_tensor(a_lo[at], tiles(bank[q][:], 4), a_hi[at].bitcast(F32), ALU.subtract).then_inc(xt_lo, 1)

            def lo_of_y(l, n):
                pair = WO_ORDER[n]
                dve.wait_ge(y_hi, NWO * l + n + 1)
                at = (slice(None), slice(2 * pair, 2 * pair + 2))
                nc.vector.tensor_tensor(a_lo[at], y32[at], a_hi[at].bitcast(F32), ALU.subtract).then_inc(y_lo, 1)

            def layer_norm(n, ready, source):
                for t in range(TT):
                    ready(t)
                    for h in range(2):
                        xh = xs[:, t, 512 * h:512 * h + 512]
                        step(nc.vector.scalar_tensor_tensor(xh, xh, ALPHA, source(t, h), ALU.mult, ALU.add))
                        step(nc.vector.bn_stats(stats[:, t, h, :], xh))
                    step(nc.vector.bn_aggr(mean_var[:, t, :], stats[:, t].rearrange("p h n -> p (h n)")))
                    nc.vector.tensor_scalar(mean_var[:, t, 1:2], mean_var[:, t, 1:2], EPS, None, ALU.add).then_inc(ln_var, 1)
                    dve.wait_ge(ln_rstd, TT * n + t + 1)
                    step(nc.vector.tensor_scalar(xs[:, t, :], xs[:, t, :], mean_var[:, t, 0:1], rstd[:, t:t + 1],
                                                 ALU.subtract, ALU.mult))
                    dve.wait_ge(ln_loaded, 32 * (n + 1))
                    step(nc.vector.tensor_tensor(xs[:, t, :], xs[:, t, :], ln_gb[:, 0, :], ALU.mult))
                    nc.vector.tensor_tensor(xs[:, t, :], xs[:, t, :], ln_gb[:, 1, :], ALU.add).then_inc(x_ready, 1)

            taps = [(h, j) for j in range(CONF_K) for h in range(2)]
            tap_at = [0]

            def conv_taps(l, count):
                for _ in range(count):
                    h, j = taps[tap_at[0] % len(taps)]
                    tap_at[0] += 1
                    tap = cols[:, l, R_DW + 2 * j + h:R_DW + 2 * j + h + 1]
                    window = conf_u[:, h, j:j + SEQ]
                    if j == 0:
                        ins = nc.vector.tensor_scalar(conf_acc[:, h, :], window, tap, None, ALU.mult)
                    else:
                        dve.wait_ge(conf_conv, tap_at[0] - 2)
                        ins = nc.vector.scalar_tensor_tensor(conf_acc[:, h, :], window, tap, conf_acc[:, h, :], ALU.mult, ALU.add)
                    ins.then_inc(conf_conv, 1)

            def rope(l):
                for n, g in enumerate((Q_G, K_G)):
                    dve.wait_ge(rot_psum, 2 * l + n + 1)
                    if l == 0 and n == 0:
                        dve.wait_ge(rope_ready, 1)
                    sin = rope_cs[:, 0:1, :].broadcast_to((P, 2, SEQ))
                    step(nc.vector.tensor_tensor(rope_rs[:, n], tiles(bank[n][:], 2), sin, ALU.mult))
                    dve.wait_ge(rope_scaled, 2 * l + n + 1)
                    nc.vector.tensor_tensor(z[g], rope_rs[:, n], rope_qc[:, n], ALU.add).then_inc(roped, 1)

            def score_rows(l, q):
                width = P * (q + 1)
                view = sc[:, 0:MAPS * width].rearrange("p (t j k) -> p t j k", t=2, j=4)
                causal = c("causal")[:, SEQ - width:].rearrange("p (a k) -> p a k", a=1).broadcast_to((P, 2, width))
                dve.wait_ge(scores_psum, 2 * l + q + 1)
                if l or q:
                    dve.wait_ge(mixed, 2 * l + q)
                for j in range(4):
                    ins = nc.vector.tensor_tensor(view[:, :, j, :], bank[j][:, 0:2 * width].rearrange("p (t k) -> p t k", t=2),
                                                  causal, ALU.add)
                step(ins)
                maps = sc[:, 0:MAPS * width].rearrange("p (m k) -> p m k", m=MAPS)
                step(nc.vector.tensor_reduce(row_max[:, q, :], maps, AX_X, ALU.max))
                nc.vector.tensor_scalar(row_max[:, q, :], row_max[:, q, :], -SCALE, None, ALU.mult).then_inc(scores_max, 1)

            def mix_maps(l, q):
                width = P * (q + 1)
                maps = sc[:, 0:MAPS * width].rearrange("p (m k) -> p m k", m=MAPS)
                dve.wait_ge(probs_ready, MAPS * (2 * l + q + 1))
                step(nc.vector.reciprocal(row_inv[:, q, :], row_sum[:, q, :]))
                second = row_inv[:, q, :].rearrange("p (h m) -> p h m", m=2)[:, :, 1]
                step(nc.vector.tensor_scalar(second, second, neg_lam[:, l:l + 1], None, ALU.mult))
                if q:
                    dve.wait_ge(aT_psum, 3 * l + 1)
                for hd in range(HEADS):
                    m = 2 * hd + 1
                    ins = nc.vector.tensor_scalar(maps[:, m, :], maps[:, m, :], row_inv[:, q, m:m + 1], None, ALU.mult)
                step(ins)
                for hd in range(HEADS):
                    m = 2 * hd
                    ins = nc.vector.scalar_tensor_tensor(a_mix[:, hd * width:(hd + 1) * width], maps[:, m, :], row_inv[:, q, m:m + 1],
                                                         maps[:, m + 1, :], ALU.mult, ALU.add)
                ins.then_inc(mixed, 1)

            for l in range(DEPTH):
                if l == 0:
                    lo_of_unit(2)
                    lo_of_x(0)
                    dve.wait_ge(lam_loaded, 16)
                    step(nc.vector.tensor_tensor(lam_prod, lam_in[:, :, 0, :], lam_in[:, :, 1, :], ALU.mult))
                    nc.vector.tensor_reduce(lam_sum, lam_prod, AX_X, ALU.add).then_inc(lam_summed, 1)
                    dve.wait_ge(lam_exped, 1)
                    step(nc.vector.tensor_tensor(neg_lam[:], lam_exp[:, :, 1], lam_exp[:, :, 0], ALU.subtract))
                    for k in range(DEPTH):
                        ins = nc.vector.tensor_scalar(neg_lam[:, k:k + 1], neg_lam[:, k:k + 1], -LAM_INIT[k], None, ALU.add)
                    step(ins)
                    dve.wait_ge(cols_ready, DEPTH)
                    for k in range(DEPTH):
                        ins = nc.vector.tensor_scalar(cols[:, k, R_SG:R_SG + 1], cols[:, k, R_SG:R_SG + 1], 1.0 - LAM_INIT[k],
                                                      None, ALU.mult)
                    step(ins)
                    dve.wait_ge(pads_zeroed, 3)
                else:
                    lo_of_x(2)
                lo_of_unit(1)
                for i in range(NZ):
                    if i == 1:
                        dve.wait_ge(z_ready, NZ * l + 2)
                        step(nc.vector.tensor_tensor(conf_u[:, :, CPAD:], z[CA_G], z[CG_G], ALU.mult))
                    lo_of_unit(1)
                    if i == 5:
                        rope(l)
                    if i == 7:
                        score_rows(l, 0)
                    if 1 <= i < 8:
                        conv_taps(l, 8)
                conv_taps(l, len(taps) - 56)
                mix_maps(l, 0)
                score_rows(l, 1)
                dve.wait_ge(pool_psum, l + 1)
                for h in range(2):
                    ins = nc.vector.tensor_scalar(y32[:, h, :], bank[0][:, 256 * h:256 * h + 256],
                                                  cols[:, l, R_PS + h:R_PS + h + 1], None, ALU.mult)
                ins.then_inc(pool_y, 1)
                dve.wait_ge(conf_mean, l + 1)
                mean = bank[1][:, 0:256].rearrange("p (a t) -> p a t", a=1).broadcast_to((P, 2, SEQ))
                step(nc.vector.tensor_tensor(xc, conf_acc, mean, ALU.subtract))
                nc.vector.tensor_tensor(xsq, xc, xc, ALU.mult).then_inc(conf_sq, 1)
                lo_of_y(l, 0)
                lo_of_y(l, 1)
                mix_maps(l, 1)
                dve.wait_ge(conf_std, l + 1)
                step(nc.vector.reciprocal(xsq[:, 1, :], xsq[:, 0, :]))
                inv_std = xsq[:, 1:2, :].broadcast_to((P, 2, SEQ))
                nc.vector.tensor_tensor(xc, xc, inv_std, ALU.mult).then_inc(conf_normed, 1)
                lo_of_y(l, 2)
                for q in range(TT):
                    dve.wait_ge(o_copied, 2 * l + q + 1)
                    step(nc.vector.tensor_tensor(o_sq[:, q], o_sb[:, q], o_sb[:, q], ALU.mult))
                    step(nc.vector.tensor_reduce(head_ms[:, q, :], o_sq[:, q], AX_X, ALU.add))
                    nc.vector.tensor_scalar(head_ms[:, q, :], head_ms[:, q, :], 1.0 / VD, EPS, ALU.mult, ALU.add).then_inc(o_ms, 1)
                for q in range(TT):
                    dve.wait_ge(o_rstd, 2 * l + q + 1)
                    scale = head_ms[:, q, :].rearrange("p (h a) -> p h a", a=1).broadcast_to((P, HEADS, VD))
                    nc.vector.tensor_tensor(o_sq[:, q], o_sb[:, q], scale, ALU.mult).then_inc(o_normed, 1)
                lo_of_unit(1)
                dve.wait_ge(oT_psum, l + 1)
                nc.vector.tensor_scalar(y32[:, 4:6, :], tiles(bank[2][:], 2), cols[:, l, R_SG:R_SG + 1], None, ALU.mult).then_inc(o_y, 1)
                lo_of_y(l, 3)
                if l == 0:
                    lo_of_unit(2)

                def mixers_ready(t):
                    if t == 0:
                        dve.wait_ge(wo_psum, l + 1)
                    else:
                        dve.wait_ge(w_used, WO_UNIT[l] + NWO)

                layer_norm(2 * l, mixers_ready, lambda t, h: bank[4 + 2 * t + h][:])
                lo_of_x(2 * l + 1)
                if l == 0:
                    lo_of_unit(1)
                    for j in range(1, FP + 1):
                        b = 2 * ((j - 1) % 2)
                        dve.wait_ge(g_act, j)
                        dve.wait_ge(w_used, dense_unit("u", j - 1) + 1)
                        nc.vector.tensor_tensor(d_h[:, (j - 1) % 2, :], d_act[:, (j - 1) % 2, :], bank[b + 1][:],
                                                ALU.mult).then_inc(h_ready, 1)
                        if j < FP:
                            lo_of_unit(1)
                        dve.wait_ge(h_hi_ready, j)
                        nc.vector.tensor_tensor(h_lo[:, (j - 1) % 2, :], d_h[:, (j - 1) % 2, :],
                                                h_hi[:, (j - 1) % 2, :].bitcast(F32), ALU.subtract).then_inc(h_lo_ready, 1)
                        if j < FP:
                            lo_of_unit(2)
                    lo_of_unit(2)

                    def dense_ready(t):
                        if t == 0:
                            dve.wait_ge(ffn_psum, 1)
                        else:
                            dve.wait_ge(w_used, Z_UNIT[1])

                    layer_norm(1, dense_ready, lambda t, h: bank[4 + 2 * t + h][:])
            assert units[0] == MOE_UNIT, (units, MOE_UNIT)

            dve.wait_ge(router_split, 1)
            nc.vector.tensor_tensor(router_lo[:], router_raw, router_hi[:].bitcast(F32), ALU.subtract).then_inc(router_split, 1)
            nc.vector.memset(acc, 0.0).then_inc(acc_ready, 1)
            nc.vector.memset(gatedT, 0.0).then_inc(gT_ready, 1)
            nc.vector.memset(bank[5][:], 0.0)
            nc.vector.memset(bank[6][:], 0.0)
            nc.vector.memset(slot_of[:], -1.0)
            nc.vector.memset(gate_of[:], 0.0)
            dve.wait_ge(logits_psum, 1)
            step(nc.vector.tensor_copy(logits, tiles(bank[7][:, 0:16], 2)))
            step(nc.vector.tensor_reduce(top, logits, AX_X, ALU.max))

            def over_experts(v):
                return v.rearrange("p (t a) -> p t a", a=1).broadcast_to((P, TT, NE))

            nc.vector.tensor_tensor(expl, logits, over_experts(top), ALU.subtract).then_inc(logits_off, 1)
            above = pairs.rearrange("p (e f) -> p e f", e=NE)
            level = pairs2.rearrange("p (e f) -> p e f", e=NE)
            for t in range(TT):
                other = logits[:, t:t + 1, :].broadcast_to((P, NE, NE))
                own = logits[:, t, :].rearrange("p (e a) -> p e a", a=1).broadcast_to((P, NE, NE))
                nc.vector.tensor_tensor(above, other, own, ALU.is_gt)
                step(nc.vector.tensor_tensor(level, other, own, ALU.is_equal))
                step(nc.vector.tensor_tensor(pairs2, pairs2, c("before"), ALU.mult))
                step(nc.vector.tensor_tensor(pairs, pairs, pairs2, ALU.add))
                step(nc.vector.tensor_reduce(rank[:, t, :], above, AX_X, ALU.add))
            nc.vector.tensor_scalar(mask, rank, 1.5, None, ALU.is_lt).then_inc(mask_ready, 1)
            dve.wait_ge(logits_exp, 1)
            dve.wait_ge(mask_ready, 1)
            step(nc.vector.tensor_tensor(expl, expl, mask, ALU.mult))
            step(nc.vector.tensor_reduce(denom, expl, AX_X, ALU.add))
            step(nc.vector.reciprocal(rdenom, denom))
            step(nc.vector.tensor_tensor(gates, expl, over_experts(rdenom), ALU.mult))
            dve.wait_ge(ranks_psum, 1)
            step(nc.vector.tensor_tensor(slots, tiles(bank[7][:, 64:80], 2), mask, ALU.mult))
            step(nc.vector.tensor_scalar(slots, slots, -1.0, None, ALU.add))
            nc.vector.tensor_copy(slot_of[:, :, 0:NE], slots)
            nc.vector.tensor_copy(gate_of[:, :, 0:NE], gates)
            step(nc.vector.tensor_scalar(over, bank[7][:, 80:88], P + 0.5, None, ALU.is_gt))
            over_all = over.rearrange("p (a e) -> p a e", a=1).broadcast_to((P, NE, NE))
            step(nc.vector.tensor_tensor(above, over_all, c("upto").rearrange("p (e f) -> p e f", e=NE), ALU.mult))
            step(nc.vector.tensor_reduce(cum_over, above, AX_X, ALU.add))

            def thrice(v):
                return v.rearrange("p (a e) -> p a e", a=1).broadcast_to((P, 3, NE))

            step(nc.vector.tensor_tensor(chosen, thrice(cum_over), c("spill").rearrange("p (j e) -> p j e", j=3), ALU.is_equal))
            step(nc.vector.tensor_tensor(chosen, chosen, thrice(over), ALU.mult))
            for t in range(TT):
                step(nc.vector.tensor_tensor(picked, chosen, thrice(slots[:, t, :]), ALU.mult))
                step(nc.vector.tensor_reduce(slot_of[:, t, NE:NE + 3], picked, AX_X, ALU.add))
                step(nc.vector.tensor_scalar(slot_of[:, t, NE:NE + 3], slot_of[:, t, NE:NE + 3], -float(P), None, ALU.add))
                step(nc.vector.tensor_tensor(picked, chosen, thrice(gates[:, t, :]), ALU.mult))
                step(nc.vector.tensor_reduce(gate_of[:, t, NE:NE + 3], picked, AX_X, ALU.add))
            step(nc.vector.tensor_copy(item_tab[:, 0:NE], c("experts")))
            step(nc.vector.tensor_tensor(picked, chosen, thrice(c("experts")), ALU.mult))
            step(nc.vector.tensor_reduce(item_tab[:, NE:NE + 3], picked, AX_X, ALU.add))
            step(nc.vector.tensor_reduce(item_tab[:, 12:13], over, AX_X, ALU.add))
            step(nc.vector.tensor_scalar(item_tab[:, 12:13], item_tab[:, 12:13], float(NE), None, ALU.add))
            step(nc.vector.tensor_copy(item_int[:, 0:11], item_tab[:, 0:11]))
            nc.vector.tensor_copy(item_int[:, 12:13], item_tab[:, 12:13]).then_inc(routed, 1)

            def hot(column):
                for t in range(TT):
                    ins = nc.vector.tensor_scalar(one_hot[:, t, :], c("iota"), slot_of[:, t, column], None, ALU.is_equal)
                ins.then_inc(hot_ready, 1)

            def lo_of_item(before):
                dve.wait_ge(item_hi, before + 1)
                for h, b in enumerate((1, 3)):
                    at = (slice(None), slice(4 * h, 4 * h + 4), slice(0, P))
                    ins = nc.vector.tensor_tensor(a_lo[at], tiles(bank[b][:], 4), a_hi[at].bitcast(F32), ALU.subtract)
                ins.then_inc(item_lo, 1)

            def lo_of_moe(unit, item):
                n = MOE_UNIT + MOE_POS[unit]
                s = n % SPLIT_SLOTS
                dve.wait_ge(w_hi_ready, item * NU + (n + 1))
                nc.vector.tensor_tensor(w_lo[:, s, :], raw[:, n % RAW_SLOTS, :], w_hi[:, s, :].bitcast(F32),
                                        ALU.subtract).then_inc(w_lo_ready, 1)

            def add_up(before):
                dve.wait_ge(acc_ready, before * 4 + 1)
                for q in range(4):
                    t, h = q // 2, q % 2
                    dve.wait_ge(comb_psum, before * 4 + (q + 1))
                    ah = acc[:, t, 512 * h:512 * h + 512]
                    nc.vector.tensor_tensor(ah, ah, bank[COMB_BANKS[q]][:], ALU.add).then_inc(acc_ready, 1)

            hot(slice(0, 1))
            lo_of_item(0)
            dve.wait_ge(routed, 1)
            items = dve.value_load(item_int[0:1, 12:13], min_val=NE, max_val=MAX_ITEMS)
            with dve.Fori(0, items) as item:
                for ch in range(NC + 1):
                    if ch:
                        dve.wait_ge(mg_act, item * NC + ch)
                        dve.wait_ge(w_used, item * NU + (MOE_UNIT + MOE_POS["u", ch - 1, 1] + 1))
                        nc.vector.tensor_tensor(m_h[:, (ch - 1) % 2, :], m_act[:, (ch - 1) % 2, :], bank[2 + (ch - 1) % 2][:],
                                                ALU.mult).then_inc(mh_ready, 1)
                    if ch < NC:
                        lo_of_moe(("g", ch, 0), item)
                        lo_of_moe(("g", ch, 1), item)
                        if ch == 1:
                            add_up(item)
                        lo_of_moe(("u", ch, 0), item)
                        lo_of_moe(("u", ch, 1), item)
                    else:
                        lo_of_item(item + 1)
                    if ch:
                        dve.wait_ge(mh_hi, item * NC + ch)
                        nc.vector.tensor_tensor(h_lo[:, 0, :], bank[4][:], h_hi[:, 0, :].bitcast(F32), ALU.subtract).then_inc(mh_lo, 1)
                        lo_of_moe(("d", ch - 1, 0), item)
                        lo_of_moe(("d", ch - 1, 1), item)
                    if ch == 1:
                        for t in range(TT):
                            ins = nc.vector.tensor_scalar(gated[:, t, :], c("iota"), slot_of[:, t, bass.ds(item, 1)],
                                                          gate_of[:, t, bass.ds(item, 1)], ALU.is_equal, ALU.mult)
                        ins.then_inc(gated_ready, 1)
                    if ch == 3:
                        hot(bass.ds(item + 1, 1))
            add_up(items)

            def sums_ready(t):
                dve.wait_ge(acc_ready, items * 4 + 5)

            layer_norm(3, sums_ready, lambda t, h: acc[:, t, 512 * h:512 * h + 512])

        @block.tensor
        def _(pe):
            units = [0]
            ident = c("ident")

            def product(target, stationary, moving, first, last):
                (s_hi, s_lo), (m_hi, m_lo) = stationary, moving
                nc.tensor.matmul(target, s_hi, m_hi, start=first, stop=False)
                nc.tensor.matmul(target, s_hi, m_lo, start=False, stop=False)
                return nc.tensor.matmul(target, s_lo, m_hi, start=False, stop=last)

            def next_unit(k):
                n = units[0]
                units[0] += 1
                pe.wait_ge(w_lo_ready, n + 1)
                return split_pair(n, k)

            def transpose_x(n):
                for q in range(4):
                    t, k0 = q // 2, 4 * (q % 2)
                    if n:
                        pe.wait_ge(x_ready, TT * (n - 1) + t + 1)
                    for k in range(k0, k0 + 4):
                        last = nc.tensor.transpose(bank[q][:, (k - k0) * P:(k - k0 + 1) * P], xs[:, t, k * P:(k + 1) * P], ident)
                    last.then_inc(xt_psum, 1)

            def project(l, i):
                if i == 0:
                    pe.wait_ge(xt_lo, 4 * (2 * l + 1))
                if i >= 4:
                    pe.wait_ge(z_ready, NZ * l + i - 3)
                m_hi, m_lo = next_unit(KT)
                for h in range(2):
                    to = bank[4 + i % 4][:, 256 * h:256 * h + 256]
                    for k in range(KT):
                        if Z_ORDER[i] == V_G:
                            tokens = slice(h * P, (h + 1) * P)
                            last = product(to, (a_hi[:, k, tokens], a_lo[:, k, tokens]), (m_hi[:, k, :], m_lo[:, k, :]),
                                           k == 0, k == KT - 1)
                        else:
                            channels = slice(h * P, (h + 1) * P)
                            last = product(to, (m_hi[:, k, channels], m_lo[:, k, channels]), (a_hi[:, k, :], a_lo[:, k, :]),
                                           k == 0, k == KT - 1)
                last.then_inc(w_used, 1)

            def scores(l, q):
                width = P * (q + 1)
                pe.wait_ge(roped, 2 * l + 2)
                if q:
                    pe.wait_ge(scores_max, 2 * l + 1)
                for t in range(2):
                    for j in range(4):
                        last = nc.tensor.matmul(bank[j][:, t * width:(t + 1) * width], z[Q_G][32 * j:32 * j + 32, t, q * P:(q + 1) * P],
                                                z[K_G][32 * j:32 * j + 32, t, 0:width], start=True, stop=True)
                last.then_inc(scores_psum, 1)

            def transpose_probs(l, q):
                pe.wait_ge(mixed, 2 * l + q + 1)
                if q == 0:
                    pe.wait_ge(scores_max, 2 * l + 2)
                else:
                    pe.wait_ge(pool_y, l + 1)
                for n, b in enumerate(([2], [3, 0])[q]):
                    for k in range(4):
                        at = (4 * n + k) * P
                        last = nc.tensor.transpose(bank[b][:, k * P:(k + 1) * P], a_mix[:, at:at + P], ident)
                    last.then_inc(aT_psum, 1)

            def attend(l, q):
                pe.wait_ge(aT_ready, 3 * l + 1 + 2 * q)
                if q == 0:
                    pe.wait_ge(conf_std, l + 1)
                for hd in range(HEADS):
                    for kb in range(q + 1):
                        at = (hd * (q + 1) + kb) * P
                        last = nc.tensor.matmul(bank[1][:, 256 * q + VD * hd:256 * q + VD * hd + VD], aT[q][:, at:at + P],
                                                z[V_G][:, kb, VD * hd:VD * hd + VD], start=(kb == 0), stop=(kb == q))
                if q:
                    last.then_inc(o_psum, 1)

            def down(k0, hi, lo, first, final, tile0_done):
                m_hi, m_lo = next_unit(2)
                for t in range(TT):
                    tokens = slice(t * P, (t + 1) * P)
                    for k in range(2):
                        for h in range(2):
                            half = slice(512 * h, 512 * h + 512)
                            last = product(bank[4 + 2 * t + h][:], (hi[:, k0 + k, tokens], lo[:, k0 + k, tokens]),
                                           (m_hi[:, k, half], m_lo[:, k, half]), first and k == 0, final and k == 1)
                    if final and t == 0:
                        last.then_inc(tile0_done, 1)
                last.then_inc(w_used, 1)

            def mix_out(l, n):
                if n == 0:
                    pe.wait_ge(z_ready, NZ * (l + 1))
                pe.wait_ge(y_lo, NWO * l + n + 1)
                down(2 * WO_ORDER[n], a_hi, a_lo, n == 0, n == NWO - 1, wo_psum)

            def dense_in(kind, j):
                b = 2 * (j % 2) + (kind == "u")
                if j == 0:
                    pe.wait_ge(xt_lo, 8)
                if j > 1:
                    pe.wait_ge(h_ready, j - 1)
                m_hi, m_lo = next_unit(KT)
                for f in range(2):
                    hidden = slice(f * P, (f + 1) * P)
                    for k in range(KT):
                        last = product(bank[b][:, 256 * f:256 * f + 256], (m_hi[:, k, hidden], m_lo[:, k, hidden]),
                                       (a_hi[:, k, :], a_lo[:, k, :]), k == 0, k == KT - 1)
                last.then_inc(w_used, 1)

            h_hi_t = h_hi[:].rearrange("p b (f t) -> p (b f) t", f=2)
            h_lo_t = h_lo[:].rearrange("p b (f t) -> p (b f) t", f=2)

            pe.wait_ge(consts_loaded, 16)
            pe.wait_ge(x_loaded, 16 * TT)
            for l in range(DEPTH):
                transpose_x(2 * l)
                if l == 0:
                    pe.wait_ge(rows_loaded, 16 * DEPTH * 7)
                    for k in range(DEPTH):
                        nc.tensor.transpose(bank[4 + k][:, 0:NR], rows[0:NR, k, :], ident[0:NR, 0:NR]).then_inc(cols_psum, 1)
                    pe.wait_ge(cols_ready, DEPTH)
                for i in range(NZ):
                    project(l, i)
                    if i == 4:
                        pe.wait_ge(z_ready, NZ * l + 4)
                        for n, g in enumerate((Q_G, K_G)):
                            nc.tensor.matmul(bank[n][:], c("rot"), z[g].rearrange("p h t -> p (h t)"), start=True, stop=True).then_inc(rot_psum, 1)
                    if i == 6:
                        scores(l, 0)
                scores(l, 1)
                transpose_probs(l, 0)
                pe.wait_ge(pool_diff, l + 1)
                pe.wait_ge(pool_loaded, 16 * 4 * DEPTH)
                for h in range(2):
                    last = nc.tensor.matmul(bank[0][:, 256 * h:256 * h + 256], pool_mat[:, l, h, :], y32[:, h, :], start=True, stop=True)
                last.then_inc(pool_psum, 1)
                pe.wait_ge(conf_conv, (l + 1) * 2 * CONF_K)
                for h in range(2):
                    last = nc.tensor.matmul(bank[1][:, 0:256], c("mean"), conf_acc[:, h, :], start=(h == 0), stop=(h == 1))
                last.then_inc(conf_mean, 1)
                mix_out(l, 0)
                pe.wait_ge(conf_sq, l + 1)
                for h in range(2):
                    last = nc.tensor.matmul(bank[1][:, 256:512], c("mean"), xsq[:, h, :], start=(h == 0), stop=(h == 1))
                last.then_inc(conf_var, 1)
                mix_out(l, 1)
                transpose_probs(l, 1)
                attend(l, 0)
                attend(l, 1)
                mix_out(l, 2)
                pe.wait_ge(o_normed, 2 * (l + 1))
                for ct in range(2):
                    for q in range(TT):
                        last = nc.tensor.transpose(bank[2][:, ct * SEQ + q * P:ct * SEQ + (q + 1) * P],
                                                   o_sq[:, q].rearrange("p h e -> p (h e)")[:, ct * P:(ct + 1) * P], ident)
                last.then_inc(oT_psum, 1)
                mix_out(l, 3)
                transpose_x(2 * l + 1)
                if l == 0:
                    for kind, j in DENSE_ORDER:
                        if kind == "d":
                            pe.wait_ge(h_lo_ready, j + 1)
                            down(2 * (j % 2), h_hi_t, h_lo_t, j == 0, j == FP - 1, ffn_psum)
                        else:
                            dense_in(kind, j)
            assert units[0] == MOE_UNIT, (units, MOE_UNIT)

            pe.wait_ge(xt_lo, 16)
            pe.wait_ge(router_split, 2)
            for t in range(TT):
                tokens = slice(t * P, (t + 1) * P)
                for k in range(KT):
                    last = product(bank[7][:, NE * t:NE * t + NE], (a_hi[:, k, tokens], a_lo[:, k, tokens]),
                                   (router_hi[:, k, :], router_lo[:, k, :]), k == 0, k == KT - 1)
            last.then_inc(logits_psum, 1)
            pe.wait_ge(mask_ready, 1)
            for at, pieces in ((64, (("tri", 0),)), (72, (("ones", 0), ("tri", 1))), (80, (("ones", 0), ("ones", 1)))):
                for n, (table, t) in enumerate(pieces):
                    last = nc.tensor.matmul(bank[7][:, at:at + NE], c(table), mask[:, t, :], start=(n == 0), stop=(n == len(pieces) - 1))
            last.then_inc(ranks_psum, 1)

            def gather(before):
                pe.wait_ge(hot_ready, before + 1)
                for k in range(KT):
                    for t in range(TT):
                        last = nc.tensor.matmul(bank[1 + 2 * (k // 4)][:, (k % 4) * P:(k % 4 + 1) * P], xs[:, t, k * P:(k + 1) * P],
                                                one_hot[:, t, :], start=(t == 0), stop=(t == TT - 1))
                last.then_inc(gather_psum, 1)

            def moe_unit(unit, item):
                kind, ch, half = unit
                n = MOE_UNIT + MOE_POS[unit]
                pe.wait_ge(w_lo_ready, item * NU + (n + 1))
                if kind == "d":
                    m_hi, m_lo = split_pair(n, 2)
                    for k in range(2):
                        tile = slice((2 * half + k) * P, (2 * half + k + 1) * P)
                        for h in range(2):
                            cols_ = slice(512 * h, 512 * h + 512)
                            last = product(bank[5 + h][:], (h_hi[:, 0, tile], h_lo[:, 0, tile]), (m_hi[:, k, cols_], m_lo[:, k, cols_]),
                                           ch == 0 and half == 0 and k == 0, ch == NC - 1 and half == 1 and k == 1)
                else:
                    m_hi, m_lo = split_pair(n, 4)
                    b = ch % 2 + 2 * (kind == "u")
                    for k in range(4):
                        last = product(bank[b][:], (a_hi[:, 4 * half + k, 0:P], a_lo[:, 4 * half + k, 0:P]), (m_hi[:, k, :], m_lo[:, k, :]),
                                       half == 0 and k == 0, half == 1 and k == 3)
                last.then_inc(w_used, 1)

            def transpose_h(ch, item):
                pe.wait_ge(mh_ready, item * NC + (ch + 1))
                for f in range(4):
                    last = nc.tensor.transpose(bank[4][:, f * P:(f + 1) * P], m_h[:, ch % 2, f * P:(f + 1) * P], ident)
                last.then_inc(mhT_psum, 1)

            def combine(before):
                pe.wait_ge(my_ready, before + 1)
                pe.wait_ge(gT_ready, before + 1)
                for q in range(4):
                    t, h = q // 2, q % 2
                    nc.tensor.matmul(bank[COMB_BANKS[q]][:], gatedT[:, t * P:(t + 1) * P], y_sb[:, 512 * h:512 * h + 512],
                                     start=True, stop=True).then_inc(comb_psum, 1)

            gather(0)
            pe.wait_ge(routed, 1)
            items = pe.value_load(item_int[0:1, 12:13], min_val=NE, max_val=MAX_ITEMS)
            with pe.Fori(0, items) as item:
                pe.wait_ge(item_lo, item + 1)
                for ch in range(NC + 1):
                    if ch < NC:
                        moe_unit(("g", ch, 0), item)
                        moe_unit(("g", ch, 1), item)
                    else:
                        gather(item + 1)
                    if ch:
                        if ch == 1:
                            pe.wait_ge(acc_ready, item * 4 + 5)
                        transpose_h(ch - 1, item)
                    if ch < NC:
                        moe_unit(("u", ch, 0), item)
                        moe_unit(("u", ch, 1), item)
                    if ch == 0:
                        combine(item)
                    if ch == 2:
                        pe.wait_ge(gated_ready, item + 1)
                        for t in range(TT):
                            last = nc.tensor.transpose(bank[7][:, t * P:(t + 1) * P], gated[:, t, :], ident)
                        last.then_inc(gT_psum, 1)
                    if ch:
                        pe.wait_ge(mh_lo, item * NC + ch)
                        moe_unit(("d", ch - 1, 0), item)
                        moe_unit(("d", ch - 1, 1), item)
            combine(items)


_INS = ["x", "positions", "w_in", "w_o", "pool_w", "pool_scale", "sconv_w", "diff_lambda", "diff_subln_g",
        "conf_dw", "conf_ln_g", "conf_ln_b", "ln1_g", "ln1_b", "ln2_g", "ln2_b", "ffn_wg", "ffn_wu", "ffn_wd",
        "router_w", "moe_wg", "moe_wu", "moe_wd"]


def kernel(**inputs):
    import concourse.bacc as _bacc
    from concourse.bass_utils import run_bass_kernel_spmd as _run

    nc = _bacc.Bacc("TRN2", target_bir_lowering=False, num_devices=1)
    arrays, args = {}, []
    for name, a in [("constants", CONSTANTS)] + [(n, np.ascontiguousarray(inputs[n])) for n in _INS]:
        arrays[f"in_{name}_dram"] = a
        args.append(nc.dram_tensor(f"in_{name}_dram", a.shape, mybir.dt.from_np(a.dtype), kind="ExternalInput").ap())
    args.append(nc.dram_tensor("out_0_dram", (1, SEQ, D), F32, kind="ExternalOutput").ap())
    hybrid_trunk(nc, *args)
    r = _run(nc, [arrays], core_ids=[0])
    return r.results[0]["out_0_dram"]
```

```python
from contextlib import ExitStack

import numpy as np

import concourse.bass as bass
from concourse import mybir

F32 = mybir.dt.float32
F32R = mybir.dt.float32r
BF16 = mybir.dt.bfloat16
I32 = mybir.dt.int32
ALU = mybir.AluOpType
ACT = mybir.ActivationFunctionType
AX_X = mybir.AxisListType.X

P = 128
D = 1024
SEQ = 256
DEPTH = 2
TT = SEQ // P
KT = D // P
GW = 256
WINDOWS = (2, 4, 8, 16)
SCONV_K = 3
CONF_K = 31
HEADS = 4
MAPS = 2 * HEADS
QK = 32
VD = 64
ROPE_DIM = QK // 4
THETA = 500000.0
D_FF = 2816
NE = 8
FE = 3584
ALPHA = (2 * DEPTH) ** 0.25
EPS = 1e-5
SCALE = float(QK) ** -0.5
LAM_INIT = [0.8 - 0.6 * float(np.exp(-0.3 * l)) for l in range(DEPTH)]

UNIT = 2048
RAW_SLOTS = 7
SPLIT_SLOTS = 3

POOL_G, SB_G, SCG_G, SH_G, Q_G, K_G, V_G, CA_G, CG_G = range(9)
Z_ORDER = [CA_G, CG_G, Q_G, K_G, SCG_G, SH_G, SB_G, POOL_G, V_G]
NZ = len(Z_ORDER)
Z_BANKS = (4, 5, 6)
WO_ORDER = [1, 0, 2, 3]
NWO = len(WO_ORDER)
FP = D_FF // GW
DENSE_ORDER = [("g", 0), ("u", 0)]
for _j in range(1, FP):
    DENSE_ORDER += [("g", _j), ("u", _j), ("d", _j - 1)]
DENSE_ORDER += [("d", FP - 1)]

CW = 512
NC = FE // CW
MOE_ORDER = []
for _c in range(NC):
    MOE_ORDER += [("g", _c, 0), ("g", _c, 1), ("u", _c, 0), ("u", _c, 1)]
    if _c:
        MOE_ORDER += [("d", _c - 1, 0), ("d", _c - 1, 1)]
MOE_ORDER += [("d", NC - 1, 0), ("d", NC - 1, 1)]
NU = len(MOE_ORDER)
assert NU % RAW_SLOTS == 0 and NU % SPLIT_SLOTS == 0
MOE_POS = {u: i for i, u in enumerate(MOE_ORDER)}
COMB_BANKS = (5, 6, 7, 4)
MAX_ITEMS = NE + 3

Z_UNIT = [0, NZ + NWO + len(DENSE_ORDER)]
WO_UNIT = [z + NZ for z in Z_UNIT]
FFN_UNIT = [z + NZ + NWO for z in Z_UNIT]
MOE_UNIT = FFN_UNIT[1]



def dense_unit(kind, j):
    return FFN_UNIT[0] + DENSE_ORDER.index((kind, j))


R_DW, R_SW, R_PS, R_LG, R_LB, R_SG = 0, 62, 68, 70, 72, 74
NR = 75


def _constants():
    at, parts, n = {}, [], 0

    def put(name, a):
        nonlocal n
        a = np.asarray(a, np.float32).reshape(P, -1)
        at[name] = (n, a.shape[1])
        parts.append(a)
        n += a.shape[1]

    i = np.arange(P)
    half = ROPE_DIM // 2
    inv = np.float32(THETA) ** (-np.arange(0, ROPE_DIM, 2, dtype=np.float32) / np.float32(ROPE_DIM))
    in_rope = (i % QK < ROPE_DIM)
    put("ident", np.eye(P))
    put("inv", np.where(in_rope, inv[i % half], 0.0))
    put("roped", in_rope)
    put("unroped", ~in_rope)
    put("minus_half", np.full((P, 4), -0.5))
    put("eps", np.full((P, 1), EPS))
    at["first"] = (0, n)
    put("alpha", ALPHA * np.eye(P))
    put("tri", (i[:, None] <= i[None, :]))
    put("ones", np.ones((P, P)))
    put("mean", np.full((P, P), 1.0 / GW))
    rot = np.zeros((P, P))
    for c in range(P):
        if c % QK < half:
            rot[c + half, c] = -1.0
        elif c % QK < ROPE_DIM:
            rot[c - half, c] = 1.0
    put("rot", rot)
    put("iota", np.broadcast_to(np.arange(P), (P, P)))
    put("causal", np.concatenate([np.zeros((P, P)), np.where(i[None, :] <= i[:, None], 0.0, -1e30)], 1))
    t = np.arange(1, SEQ + 1)
    counts = np.stack([np.minimum(t[None, :], np.repeat(WINDOWS[2 * h:2 * h + 2], 64)[:, None]) for h in range(2)], 1)
    put("rcount", np.float32(1.0) / counts.astype(np.float32))
    e = np.arange(NE)
    put("before", np.broadcast_to((e[None, :] < e[:, None]).ravel(), (P, NE * NE)))
    put("upto", np.broadcast_to((e[None, :] <= e[:, None]).ravel(), (P, NE * NE)))
    put("experts", np.broadcast_to(e, (P, NE)))
    put("spill", np.broadcast_to(np.repeat(np.arange(1, 4), NE), (P, 3 * NE)))
    return at, np.ascontiguousarray(np.concatenate(parts, 1))


CONST_AT, CONSTANTS = _constants()

TWO_PI = 2.0 * np.pi
TURN = []
_rest = TWO_PI
for _ in range(3):
    _step = 2.0 ** (np.floor(np.log2(_rest)) - 7)
    TURN.append(float(np.floor(_rest / _step) * _step))
    _rest -= TURN[-1]
TURN.append(float(np.float32(_rest)))
MAGIC = 1.5 * 2.0 ** 23
PI_IN = 3.1415925


def hybrid_trunk(nc, consts, x, positions, w_in, w_o, pool_w, pool_scale, sconv_w, diff_lambda, diff_subln_g,
                 conf_dw, conf_ln_g, conf_ln_b, ln1_g, ln1_b, ln2_g, ln2_b, ffn_wg, ffn_wu, ffn_wd,
                 router_w, moe_wg, moe_wu, moe_wd, out):
    with ExitStack() as ctx:
        def sb(name, shape, dt=F32):
            return ctx.enter_context(nc.sbuf_tensor(name, shape, dt))

        def sem(name):
            return ctx.enter_context(nc.semaphore(name))

        bank = [ctx.enter_context(nc.psum_tensor(f"bank{b}", [P, 512], F32)) for b in range(8)]
        raw = sb("raw", [P, RAW_SLOTS, UNIT])
        w_hi = sb("w_hi", [P, SPLIT_SLOTS, UNIT], F32R)
        w_lo = sb("w_lo", [P, SPLIT_SLOTS, UNIT], F32R)
        a_hi = sb("a_hi", [P, KT, SEQ], F32R)
        a_lo = sb("a_lo", [P, KT, SEQ], F32R)
        h_hi = sb("h_hi", [P, 2, 512], F32R)
        h_lo = sb("h_lo", [P, 2, 512], F32R)
        router_raw = sb("router_raw", [P, KT, NE])
        router_hi = sb("router_hi", [P, KT, NE], F32R)
        router_lo = sb("router_lo", [P, KT, NE], F32R)
        xs = sb("xs", [P, TT, D])
        cst = sb("cst", [P, CONSTANTS.shape[1]])
        ln_gb = sb("ln_gb", [P, 2, D])
        rope_cs = sb("rope_cs", [P, 2, SEQ])
        cols = sb("cols", [P, DEPTH, NR])
        pool_mat = sb("pool_mat", [P, DEPTH, 2, P])
        ident_b = sb("ident_b", [P, P], BF16)
        causal_b = sb("causal_b", [P, SEQ], BF16)
        lam_exp = sb("lam_exp", [P, DEPTH, 2])
        neg_lam = sb("neg_lam", [P, DEPTH])
        stats = sb("stats", [P, TT, 2, 6])
        mean_var = sb("mean_var", [P, TT, 2])
        rstd = sb("rstd", [P, TT])
        row_max = sb("row_max", [P, 2, MAPS])
        row_sum = sb("row_sum", [P, 2, MAPS])
        row_inv = sb("row_inv", [P, 2, MAPS])
        head_ms = sb("head_ms", [P, TT, HEADS])
        slot_of = sb("slot_of", [P, TT, 12])
        gate_of = sb("gate_of", [P, TT, 12])
        item_tab = sb("item_tab", [P, 16])
        item_int = sb("item_int", [P, 16], I32)
        work = sb("work", [P, 12448])

        def c(name, parts=P):
            at, n = CONST_AT[name]
            return cst[0:parts, at:at + n]

        def w(at, n, parts=P):
            return work[0:parts, at:at + n]

        z_at = {CA_G: 0, CG_G: 512, Q_G: 1024, K_G: 1536, SB_G: 2048, SCG_G: 2560, SH_G: 3072, V_G: 3584}
        z = {g: w(at, 512).rearrange("p (h t) -> p h t", h=2) for g, at in z_at.items()}
        CPAD, PPAD, SPAD = CONF_K - 1, 16, SCONV_K - 1
        conf_u = w(4096, 2 * (SEQ + CPAD)).rearrange("p (h t) -> p h t", h=2)
        conf_acc = w(4668, 512).rearrange("p (h t) -> p h t", h=2)
        pool_h = w(5180, 2 * (SEQ + PPAD)).rearrange("p (h t) -> p h t", h=2)
        pool_s = [w(5724 + 544 * b, 544).rearrange("p (h t) -> p h t", h=2) for b in range(2)]
        sconv_u = w(6812, 2 * (SEQ + SPAD)).rearrange("p (h t) -> p h t", h=2)
        sc = w(7328, 2048)
        a_mix = w(9376, 1024)
        y32 = w(10400, 2048).rearrange("p (k t) -> p k t", k=KT)
        xc, xsq = z[CA_G], z[SB_G]
        s_acc, s_tmp = z[SH_G], z[SCG_G]
        rope_rs = sc[:, 0:1024].rearrange("p (g h t) -> p g h t", g=2, h=2)
        rope_qc = sc[:, 1024:2048].rearrange("p (g h t) -> p g h t", g=2, h=2)
        aT = [w(512, 512), w(1024, 1024)]
        o_sb = sc[:, 0:512].rearrange("p (q h e) -> p q h e", q=2, h=HEADS)
        o_sq = sc[:, 512:1024].rearrange("p (q h e) -> p q h e", q=2, h=HEADS)
        rows = sc[:, 0:DEPTH * P].rearrange("p (l n) -> p l n", l=DEPTH)
        lam_in = a_mix[:, 0:DEPTH * 128].rearrange("p (l a b n) -> p (l a) b n", l=DEPTH, a=2, b=2)
        lam_prod = a_mix[:, 256:384].rearrange("p (l n) -> p l n", n=QK)
        lam_sum = a_mix[:, 384:388]
        pos_int = work[:, 10400:10656].bitcast(I32)
        angle = w(10656, 256)
        trig = w(10912, 512).rearrange("p (h t) -> p h t", h=2)
        turns = w(11424, 512).rearrange("p (h t) -> p h t", h=2)
        d_act = w(0, 1024).rearrange("p (b n) -> p b n", b=2)
        d_h = w(1024, 1024).rearrange("p (b n) -> p b n", b=2)
        m_act = w(0, 1024).rearrange("p (b n) -> p b n", b=2)
        m_h = w(1024, 1024).rearrange("p (b n) -> p b n", b=2)
        one_hot = w(2048, 256).rearrange("p (t s) -> p t s", t=TT)
        gated = w(2304, 256).rearrange("p (t s) -> p t s", t=TT)
        gatedT = w(2560, 256)
        y_sb = w(2816, 1024)
        acc = w(3840, 2048).rearrange("p (t n) -> p t n", t=TT)
        logitsT = w(6400, SEQ, NE)
        logits = w(5952, 16).rearrange("p (t e) -> p t e", t=TT)
        mask = w(5968, 16).rearrange("p (t e) -> p t e", t=TT)
        gates = w(5984, 16).rearrange("p (t e) -> p t e", t=TT)
        expl = w(6000, 16).rearrange("p (t e) -> p t e", t=TT)
        rank = w(6016, 16).rearrange("p (t e) -> p t e", t=TT)
        top = w(6032, 2)
        denom = w(6034, 2)
        rdenom = w(6036, 2)
        slots = w(6040, 16).rearrange("p (t e) -> p t e", t=TT)
        over = w(6056, 8)
        cum_over = w(6064, 8)
        pairs = w(6072, 128)
        pairs2 = w(6200, 128)
        chosen = w(6328, 24).rearrange("p (j e) -> p j e", j=3)
        picked = w(6656, 48).rearrange("p (t j e) -> p t j e", t=TT, j=3)
        picked_gate = w(6704, 48).rearrange("p (t j e) -> p t j e", t=TT, j=3)
        picked_expert = w(6352, 24).rearrange("p (j e) -> p j e", j=3)

        raw_loaded = [sem(f"raw_loaded{s}") for s in range(RAW_SLOTS)]
        w_hi_ready, w_lo_ready, w_used = sem("w_hi_ready"), sem("w_lo_ready"), sem("w_used")
        first_loaded, consts_loaded, x_loaded, pos_loaded = sem("first_loaded"), sem("consts_loaded"), sem("x_loaded"), sem("pos_loaded")
        rows_loaded, lam_loaded, pool_loaded = sem("rows_loaded"), sem("lam_loaded"), sem("pool_loaded")
        router_loaded, ln_loaded, stored = sem("router_loaded"), sem("ln_loaded"), sem("stored")
        cols_psum, cols_ready = sem("cols_psum"), sem("cols_ready")
        pads_zeroed = sem("pads_zeroed")
        lam_summed, lam_exped = sem("lam_summed"), sem("lam_exped")
        angles_ready, sines_ready, rope_ready = sem("angles_ready"), sem("sines_ready"), sem("rope_ready")
        xt_psum, xt_hi, xt_lo = sem("xt_psum"), sem("xt_hi"), sem("xt_lo")
        z_ready = sem("z_ready")
        rot_psum, rope_scaled, roped = sem("rot_psum"), sem("rope_scaled"), sem("roped")
        conf_conv, conf_mean, conf_sq, conf_var = sem("conf_conv"), sem("conf_mean"), sem("conf_sq"), sem("conf_var")
        conf_std, conf_normed, conf_y = sem("conf_std"), sem("conf_normed"), sem("conf_y")
        pool_diff, pool_psum, pool_y, sconv_y = sem("pool_diff"), sem("pool_psum"), sem("pool_y"), sem("sconv_y")
        tables_ready, scores_psum, scores_max, probs_ready = sem("tables_ready"), sem("scores_psum"), sem("scores_max"), sem("probs_ready")
        mixed, aT_psum, aT_ready = sem("mixed"), sem("aT_psum"), sem("aT_ready")
        o_psum, o_copied, o_ms, o_rstd = sem("o_psum"), sem("o_copied"), sem("o_ms"), sem("o_rstd")
        o_normed, oT_psum, o_y = sem("o_normed"), sem("oT_psum"), sem("o_y")
        y_hi, y_lo, wo_psum = sem("y_hi"), sem("y_lo"), sem("wo_psum")
        ln_var, ln_rstd, x_ready = sem("ln_var"), sem("ln_rstd"), sem("x_ready")
        g_act, h_ready = sem("g_act"), sem("h_ready")
        h_hi_ready, h_lo_ready, ffn_psum = sem("h_hi_ready"), sem("h_lo_ready"), sem("ffn_psum")
        router_split, logitsT_ready, logits_psum, logits_off, logits_exp = sem("router_split"), sem("logitsT_ready"), sem("logits_psum"), sem("logits_off"), sem("logits_exp")
        mask_ready, ranks_psum, routed = sem("mask_ready"), sem("ranks_psum"), sem("routed")
        hot_ready, gather_psum, item_hi, item_lo = sem("hot_ready"), sem("gather_psum"), sem("item_hi"), sem("item_lo")
        gated_ready, gT_psum, gT_ready = sem("gated_ready"), sem("gT_psum"), sem("gT_ready")
        mg_act, mh_ready = sem("mg_act"), sem("mh_ready")
        mhT_psum, mh_hi, mh_lo, my_ready = sem("mhT_psum"), sem("mh_hi"), sem("mh_lo"), sem("my_ready")
        comb_psum, acc_ready = sem("comb_psum"), sem("acc_ready")
        dve_step, pool_step = sem("dve_step"), sem("pool_step")

        def z_src(l, g):
            return w_in[l].rearrange("(k p) n -> p k n", p=P)[:, :, g * GW:(g + 1) * GW]

        def wo_src(l, pair):
            return w_o[l].rearrange("(k p) n -> p k n", p=P)[:, 2 * pair:2 * pair + 2, :]

        def dense_src(kind, j):
            if kind == "d":
                return ffn_wd[0].rearrange("(k p) n -> p k n", p=P)[:, 2 * j:2 * j + 2, :]
            m = ffn_wg if kind == "g" else ffn_wu
            return m[0].rearrange("(k p) n -> p k n", p=P)[:, :, j * GW:(j + 1) * GW]

        def moe_src(e, kind, ch, part_):
            if kind == "d":
                m = moe_wd[0, bass.ds(e, 1)].rearrange("a (k p) n -> p (a k) n", p=P)
                k0 = ch * (CW // P) + 2 * part_
                return m[:, k0:k0 + 2, :]
            m = moe_wg if kind == "g" else moe_wu
            m = m[0, bass.ds(e, 1)].rearrange("a (k p) n -> p (a k) n", p=P)
            return m[:, 4 * part_:4 * part_ + 4, ch * CW:(ch + 1) * CW]

        def tiles(slot, k):
            return slot.rearrange("p (k n) -> p k n", k=k)

        def split_pair(n, k):
            s = n % SPLIT_SLOTS
            return tiles(w_hi[:, s, :], k), tiles(w_lo[:, s, :], k)

        FIRST_UNITS = []
        for l in range(DEPTH):
            FIRST_UNITS += [(z_src(l, g), KT) for g in Z_ORDER]
            FIRST_UNITS += [(wo_src(l, pair), 2) for pair in WO_ORDER]
            if l == 0:
                FIRST_UNITS += [(dense_src(kind, j), 2 if kind == "d" else KT) for kind, j in DENSE_ORDER]
        assert len(FIRST_UNITS) == MOE_UNIT

        block = ctx.enter_context(nc.Block())

        @block.sync
        def _(sp):
            def load_small():
                sp.dma_start(rows[R_DW:R_DW + 62], conf_dw.rearrange("l j (h c) -> (j h) l c", h=2)).then_inc(rows_loaded, 16)
                sp.dma_start(rows[R_SW:R_SW + 6], sconv_w.rearrange("l j (h c) -> (j h) l c", h=2)).then_inc(rows_loaded, 16)
                for r, m in ((R_PS, pool_scale), (R_LG, conf_ln_g), (R_LB, conf_ln_b)):
                    sp.dma_start(rows[r:r + 2], m.rearrange("l (h c) -> h l c", h=2)).then_inc(rows_loaded, 16)
                for b in range(2):
                    sp.dma_start(rows[R_SG:R_SG + 1, :, 64 * b:64 * b + 64], diff_subln_g.rearrange("(a l) n -> a l n", a=1)).then_inc(rows_loaded, 16)
                sp.dma_start(a_mix[:, 0:DEPTH * 128], diff_lambda.rearrange("l a n -> (l a n)").partition_broadcast(P)).then_inc(lam_loaded, 16)
                sp.dma_start(router_raw[:], router_w[0].rearrange("(k p) e -> p k e", p=P)).then_inc(router_loaded, 16)

            first = CONST_AT["first"][1]
            sp.dma_start(cst[:, 0:first], consts[:, 0:first]).then_inc(first_loaded, 16)
            for t in range(TT):
                sp.dma_start(xs[:, t, :], x[0, t * P:(t + 1) * P, :]).then_inc(x_loaded, 16)
            for n, (src, k) in enumerate(FIRST_UNITS):
                if n == SPLIT_SLOTS:
                    load_small()
                if n >= RAW_SLOTS:
                    sp.wait_ge(w_lo_ready, n - RAW_SLOTS + 1)
                sp.dma_start(tiles(raw[:, n % RAW_SLOTS, :], k), src).then_inc(raw_loaded[n % RAW_SLOTS], 16)

            def load_item(e, before, count=NU):
                for i, (kind, ch, half) in enumerate(MOE_ORDER[:count]):
                    n = MOE_UNIT + i
                    sp.wait_ge(w_lo_ready, before + (n - RAW_SLOTS + 1))
                    sp.dma_start(tiles(raw[:, n % RAW_SLOTS, :], 2 if kind == "d" else 4),
                                 moe_src(e, kind, ch, half)).then_inc(raw_loaded[n % RAW_SLOTS], 16)

            load_item(0, 0)
            sp.wait_ge(routed, 1)
            items = sp.value_load(item_int[0:1, 12:13], min_val=NE, max_val=MAX_ITEMS)
            with sp.Fori(1, items) as item:
                e = sp.value_load(item_int[0:1, bass.ds(item, 1)], min_val=0, max_val=NE - 1)
                load_item(e, item * NU)
            load_item(0, items * NU, 2)
            for t in range(TT):
                sp.wait_ge(x_ready, 3 * TT + t + 1)
                sp.dma_start(out[0, t * P:(t + 1) * P, :], xs[:, t, :]).then_inc(stored, 16)
            sp.wait_ge(stored, 16 * TT)

        @block.gpsimd
        def _(pool):
            steps = [0]

            def step(ins):
                steps[0] += 1
                ins.then_inc(pool_step, 1)
                pool.wait_ge(pool_step, steps[0])

            nc.gpsimd.memset(conf_u[:, :, 0:CPAD], 0.0).then_inc(pads_zeroed, 1)
            nc.gpsimd.memset(pool_h[:, :, 0:PPAD], 0.0).then_inc(pads_zeroed, 1)
            nc.gpsimd.memset(sconv_u[:, :, 0:SPAD], 0.0).then_inc(pads_zeroed, 1)
            step(nc.gpsimd.memset(pool_mat[:], 0.0))
            for l in range(DEPTH):
                for h in range(2):
                    for b in range(2):
                        pool.dma_start(pool_mat[64 * b:64 * b + 64, l, h, 64 * b:64 * b + 64],
                                       pool_w[l, 2 * h + b]).then_inc(pool_loaded, 16)

            def short_window(l):
                pool.wait_ge(z_ready, NZ * l + Z_ORDER.index(SH_G) + 1)
                step(nc.gpsimd.tensor_tensor(sconv_u[:, :, SPAD:], z[SCG_G], z[SH_G], ALU.mult))
                for h in range(2):
                    for j in range(SCONV_K):
                        to = s_acc if j == 0 else s_tmp
                        tap = cols[:, l, R_SW + 2 * j + h:R_SW + 2 * j + h + 1]
                        step(nc.gpsimd.tensor_scalar(to[:, h, :], sconv_u[:, h, j:j + SEQ], tap, None, ALU.mult))
                        if j:
                            step(nc.gpsimd.tensor_tensor(s_acc[:, h, :], s_acc[:, h, :], s_tmp[:, h, :], ALU.add))
                pool.wait_ge(z_ready, NZ * l + Z_ORDER.index(SB_G) + 1)
                nc.gpsimd.tensor_tensor(y32[:, 2:4, :], s_acc, z[SB_G], ALU.mult).then_inc(sconv_y, 1)

            def window_sums(l):
                pool.wait_ge(z_ready, NZ * l + Z_ORDER.index(POOL_G) + 1)
                src, first = pool_h, 1
                for n, width in enumerate(WINDOWS):
                    dst = pool_s[n % 2]
                    step(nc.gpsimd.tensor_tensor(dst[:, :, first:], src[:, :, first:],
                                                 src[:, :, first - width // 2:SEQ + PPAD - width // 2], ALU.add))
                    h, lo = n // 2, 64 * (n % 2)
                    step(nc.gpsimd.tensor_tensor(y32[lo:lo + 64, h, :], dst[lo:lo + 64, h, PPAD:],
                                                 c("rcount")[lo:lo + 64, h * SEQ:(h + 1) * SEQ], ALU.mult))
                    src, first = dst, first + width
                nc.gpsimd.tensor_tensor(y32[:, 0:2, :], y32[:, 0:2, :], pool_h[:, :, PPAD:], ALU.subtract).then_inc(pool_diff, 1)

            def inverse_roots(n):
                for t in range(TT):
                    pool.wait_ge(ln_var, TT * n + t + 1)
                    nc.gpsimd.tensor_tensor(rstd[:, t:t + 1], mean_var[:, t, 1:2], c("minus_half")[:, 0:1],
                                            ALU.pow).then_inc(ln_rstd, 1)

            for l in range(DEPTH):
                for n, g in enumerate((Q_G, K_G)):
                    pool.wait_ge(z_ready, NZ * l + Z_ORDER.index(g) + 1)
                    cos = rope_cs[:, 1:2, :].broadcast_to((P, 2, SEQ))
                    if l == 0 and n == 0:
                        pool.wait_ge(rope_ready, 1)
                        pool.wait_ge(cols_ready, DEPTH)
                    nc.gpsimd.tensor_tensor(rope_qc[:, n], z[g], cos, ALU.mult).then_inc(rope_scaled, 1)
                short_window(l)
                window_sums(l)
                for q in range(TT):
                    pool.wait_ge(o_ms, TT * l + q + 1)
                    nc.gpsimd.tensor_tensor(head_ms[:, q, :], head_ms[:, q, :], c("minus_half"), ALU.pow).then_inc(o_rstd, 1)
                inverse_roots(2 * l)
                if l == DEPTH - 1:
                    pool.wait_ge(x_ready, TT * 3)
                    nc.gpsimd.tensor_scalar(acc, xs[:], ALPHA, None, ALU.mult).then_inc(acc_ready, 1)
                inverse_roots(2 * l + 1)

        @block.scalar
        def _(act):
            act.dma_start(pos_int, positions[0].partition_broadcast(P)).then_inc(pos_loaded, 16)
            first = CONST_AT["first"][1]
            act.dma_start(cst[:, first:], consts[:, first:]).then_inc(consts_loaded, 16)

            units = [0]

            def hi_of_unit(count=1):
                for _ in range(count):
                    n = units[0]
                    units[0] += 1
                    act.wait_ge(raw_loaded[n % RAW_SLOTS], 16 * (n // RAW_SLOTS + 1))
                    if n >= SPLIT_SLOTS:
                        act.wait_ge(w_used, n - SPLIT_SLOTS + 1)
                    nc.scalar.activation(w_hi[:, n % SPLIT_SLOTS, :], raw[:, n % RAW_SLOTS, :], ACT.Copy).then_inc(w_hi_ready, 1)

            def hi_of_moe(unit, item):
                n = MOE_UNIT + MOE_POS[unit]
                act.wait_ge(raw_loaded[n % RAW_SLOTS], item * (16 * NU // RAW_SLOTS) + 16 * (n // RAW_SLOTS + 1))
                act.wait_ge(w_used, item * NU + (n - SPLIT_SLOTS + 1))
                nc.scalar.activation(w_hi[:, n % SPLIT_SLOTS, :], raw[:, n % RAW_SLOTS, :], ACT.Copy).then_inc(w_hi_ready, 1)

            def load_ln(n):
                if n:
                    act.wait_ge(x_ready, TT * n)
                g, b = ((ln1_g, ln1_b), (ln2_g, ln2_b))[n % 2]
                for j, m in enumerate((g, b)):
                    act.dma_start(ln_gb[:, j, :], m[n // 2].partition_broadcast(P)).then_inc(ln_loaded, 16)

            def hi_of_x(n):
                for q in range(4):
                    t, k = q // 2, 4 * (q % 2)
                    act.wait_ge(xt_psum, 4 * n + q + 1)
                    nc.scalar.activation(a_hi[:, k:k + 4, t * P:(t + 1) * P], tiles(bank[q][:], 4), ACT.Copy).then_inc(xt_hi, 1)

            def z_out(l, i):
                g = Z_ORDER[i]
                act.wait_ge(w_used, Z_UNIT[l] + i + 1)
                to = pool_h[:, :, PPAD:] if g == POOL_G else z[g]
                nc.scalar.activation(to, tiles(bank[Z_BANKS[i % 3]][:], 2), ACT.Sigmoid if g == CG_G else ACT.Copy).then_inc(z_ready, 1)

            def probs(l, q):
                width = P * (q + 1)
                act.wait_ge(scores_max, 2 * l + q + 1)
                if l or q:
                    act.wait_ge(mixed, 2 * l + q)
                view = sc[:, 0:MAPS * width].rearrange("p (m k) -> p m k", m=MAPS)
                for m in range(MAPS):
                    nc.scalar.activation(view[:, m, :], bank[m % 4][:, (m // 4) * width:(m // 4 + 1) * width], ACT.Exp,
                                         bias=row_max[:, q, m:m + 1], scale=SCALE,
                                         accum_out=row_sum[:, q, m:m + 1]).then_inc(probs_ready, 1)

            def aT_out(l, q):
                for n, b in enumerate(([7], [0, 1])[q]):
                    act.wait_ge(aT_psum, 3 * l + q + n + 1)
                    nc.scalar.activation(aT[q][:, 512 * n:512 * n + 512], bank[b][:], ACT.Copy).then_inc(aT_ready, 1)

            def hi_of_y(l, n):
                pair = WO_ORDER[n]
                act.wait_ge((pool_y, sconv_y, o_y, conf_y)[pair], l + 1)
                act.wait_ge(w_used, WO_UNIT[l])
                nc.scalar.activation(a_hi[:, 2 * pair:2 * pair + 2, :], y32[:, 2 * pair:2 * pair + 2, :], ACT.Copy).then_inc(y_hi, 1)

            for l in range(DEPTH):
                if l == 0:
                    hi_of_unit(1)
                    hi_of_x(0)
                    hi_of_unit(2)
                    act.wait_ge(angles_ready, 1)
                    nc.scalar.activation(rope_cs[:], trig, ACT.Sin).then_inc(sines_ready, 1)
                else:
                    hi_of_x(2)
                    load_ln(2)
                    hi_of_unit(1)
                for i in range(NZ):
                    z_out(l, i)
                    hi_of_unit(1)
                    if l == 0 and i == 0:
                        load_ln(0)
                    if l == 0 and i == 1:
                        for k in range(DEPTH):
                            act.wait_ge(cols_psum, k + 1)
                            nc.scalar.activation(cols[:, k, :], bank[2 + k][:, 0:NR], ACT.Copy).then_inc(cols_ready, 1)
                        act.wait_ge(lam_summed, 1)
                        nc.scalar.activation(lam_exp.rearrange("p l n -> p (l n)"), lam_sum, ACT.Exp).then_inc(lam_exped, 1)
                        act.wait_ge(router_loaded, 16)
                        nc.scalar.activation(router_hi[:], router_raw[:], ACT.Copy).then_inc(router_split, 1)
                    if i == 5:
                        probs(l, 0)
                    if i == 6:
                        probs(l, 1)
                    if i == 7:
                        aT_out(l, 0)
                aT_out(l, 1)
                hi_of_y(l, 0)
                act.wait_ge(o_psum, l + 1)
                for q in range(TT):
                    nc.scalar.activation(o_sb[:, q].rearrange("p h e -> p (h e)"), bank[2][:, 256 * q:256 * q + 256], ACT.Copy).then_inc(o_copied, 1)
                hi_of_y(l, 1)
                hi_of_unit(1)
                hi_of_y(l, 2)
                act.wait_ge(conf_var, l + 1)
                nc.scalar.activation(xsq[:, 0, :], bank[1][:, 256:512], ACT.Sqrt, bias=c("eps")).then_inc(conf_std, 1)
                act.wait_ge(conf_normed, l + 1)
                for h in range(2):
                    last = nc.scalar.activation(y32[:, 6 + h, :], xc[:, h, :], ACT.Silu, bias=cols[:, l, R_LB + h:R_LB + h + 1],
                                                scale=cols[:, l, R_LG + h:R_LG + h + 1])
                last.then_inc(conf_y, 1)
                hi_of_y(l, 3)
                if l == 0:
                    hi_of_unit(2)
                else:
                    hi_of_moe(MOE_ORDER[0], 0)
                    hi_of_moe(MOE_ORDER[1], 0)
                hi_of_x(2 * l + 1)
                load_ln(2 * l + 1)
                if l == 0:
                    hi_of_unit(1)
                    for j in range(FP + 1):
                        if 0 < j < FP:
                            hi_of_unit(1)
                        if j:
                            act.wait_ge(h_ready, j)
                            nc.scalar.activation(h_hi[:, (j - 1) % 2, :], d_h[:, (j - 1) % 2, :], ACT.Copy).then_inc(h_hi_ready, 1)
                        if 0 < j < FP:
                            hi_of_unit(1)
                        if j < FP:
                            act.wait_ge(w_used, dense_unit("g", j) + 1)
                            nc.scalar.activation(d_act[:, j % 2, :], bank[2 * (j % 2)][:], ACT.Silu).then_inc(g_act, 1)
                        if 0 < j < FP:
                            hi_of_unit(1)
                    hi_of_unit(2)
            assert units[0] == MOE_UNIT, (units, MOE_UNIT)

            act.wait_ge(logits_off, 1)
            nc.scalar.activation(expl, expl, ACT.Exp).then_inc(logits_exp, 1)

            def hi_of_item(before):
                act.wait_ge(gather_psum, before + 1)
                for h, b in enumerate((1, 3)):
                    last = nc.scalar.activation(a_hi[:, 4 * h:4 * h + 4, 0:P], tiles(bank[b][:], 4), ACT.Copy)
                last.then_inc(item_hi, 1)

            def y_out(before):
                act.wait_ge(w_used, before * NU + MOE_UNIT)
                for h in range(2):
                    last = nc.scalar.activation(y_sb[:, 512 * h:512 * h + 512], bank[5 + h][:], ACT.Copy)
                last.then_inc(my_ready, 1)

            y_out(0)
            hi_of_item(0)
            act.wait_ge(routed, 1)
            items = act.value_load(item_int[0:1, 12:13], min_val=NE, max_val=MAX_ITEMS)
            with act.Fori(0, items) as item:
                for ch in range(NC + 1):
                    if ch < NC:
                        if ch:
                            hi_of_moe(("g", ch, 0), item)
                            hi_of_moe(("g", ch, 1), item)
                        hi_of_moe(("u", ch, 0), item)
                        hi_of_moe(("u", ch, 1), item)
                    else:
                        hi_of_moe(("d", ch - 1, 0), item)
                        hi_of_moe(("d", ch - 1, 1), item)
                    if ch:
                        act.wait_ge(mhT_psum, item * NC + ch)
                        nc.scalar.activation(h_hi[:, 0, :], bank[4][:], ACT.Copy).then_inc(mh_hi, 1)
                    if ch < NC:
                        act.wait_ge(w_used, item * NU + (MOE_UNIT + MOE_POS["g", ch, 1] + 1))
                        nc.scalar.activation(m_act[:, ch % 2, :], bank[ch % 2][:], ACT.Silu).then_inc(mg_act, 1)
                    if ch == 3:
                        act.wait_ge(gT_psum, item + 1)
                        nc.scalar.activation(gatedT, bank[7][:, 0:256], ACT.Copy).then_inc(gT_ready, 1)
                    if 0 < ch < NC:
                        hi_of_moe(("d", ch - 1, 0), item)
                        hi_of_moe(("d", ch - 1, 1), item)
                hi_of_moe(MOE_ORDER[0], item + 1)
                hi_of_item(item + 1)
                hi_of_moe(MOE_ORDER[1], item + 1)
                y_out(item + 1)

        @block.vector
        def _(dve):
            steps, units = [0], [0]
            ident = c("ident")

            def step(ins):
                steps[0] += 1
                ins.then_inc(dve_step, 1)
                dve.wait_ge(dve_step, steps[0])

            def lo_of_unit(count=1):
                for _ in range(count):
                    n = units[0]
                    units[0] += 1
                    dve.wait_ge(w_hi_ready, n + 1)
                    s = n % SPLIT_SLOTS
                    nc.vector.tensor_tensor(w_lo[:, s, :], raw[:, n % RAW_SLOTS, :], w_hi[:, s, :].bitcast(F32),
                                            ALU.subtract).then_inc(w_lo_ready, 1)

            def lo_of_moe(unit, item):
                n = MOE_UNIT + MOE_POS[unit]
                s = n % SPLIT_SLOTS
                dve.wait_ge(w_hi_ready, item * NU + (n + 1))
                nc.vector.tensor_tensor(w_lo[:, s, :], raw[:, n % RAW_SLOTS, :], w_hi[:, s, :].bitcast(F32),
                                        ALU.subtract).then_inc(w_lo_ready, 1)

            def lo_of_x(n):
                for q in range(4):
                    t, k = q // 2, 4 * (q % 2)
                    dve.wait_ge(xt_hi, 4 * n + q + 1)
                    at = (slice(None), slice(k, k + 4), slice(t * P, (t + 1) * P))
                    nc.vector.tensor_tensor(a_lo[at], tiles(bank[q][:], 4), a_hi[at].bitcast(F32), ALU.subtract).then_inc(xt_lo, 1)

            def lo_of_y(l, n):
                pair = WO_ORDER[n]
                dve.wait_ge(y_hi, NWO * l + n + 1)
                at = (slice(None), slice(2 * pair, 2 * pair + 2))
                nc.vector.tensor_tensor(a_lo[at], y32[at], a_hi[at].bitcast(F32), ALU.subtract).then_inc(y_lo, 1)

            def layer_norm(n, ready, source):
                dve.wait_ge(ln_loaded, 32 * (n + 1))
                for t in range(TT):
                    ready(t)
                    for h in range(2):
                        ins = nc.vector.bn_stats(stats[:, t, h, :], source(t, h))
                    step(ins)
                    step(nc.vector.bn_aggr(mean_var[:, t, :], stats[:, t].rearrange("p h n -> p (h n)")))
                    nc.vector.tensor_scalar(mean_var[:, t, 1:2], mean_var[:, t, 1:2], EPS, None, ALU.add).then_inc(ln_var, 1)
                    for h in range(2):
                        half = slice(512 * h, 512 * h + 512)
                        ins = nc.vector.scalar_tensor_tensor(xs[:, t, half], source(t, h), mean_var[:, t, 0:1], ln_gb[:, 0, half],
                                                             ALU.subtract, ALU.mult)
                    step(ins)
                    dve.wait_ge(ln_rstd, TT * n + t + 1)
                    nc.vector.scalar_tensor_tensor(xs[:, t, :], xs[:, t, :], rstd[:, t:t + 1], ln_gb[:, 1, :],
                                                   ALU.mult, ALU.add).then_inc(x_ready, 1)

            taps = [(h, j) for j in range(CONF_K) for h in range(2)]
            tap_at = [0]

            def conv_taps(l, count):
                for _ in range(count):
                    h, j = taps[tap_at[0] % len(taps)]
                    tap_at[0] += 1
                    tap = cols[:, l, R_DW + 2 * j + h:R_DW + 2 * j + h + 1]
                    window = conf_u[:, h, j:j + SEQ]
                    if j == 0:
                        ins = nc.vector.tensor_scalar(conf_acc[:, h, :], window, tap, None, ALU.mult)
                    else:
                        dve.wait_ge(conf_conv, tap_at[0] - 2)
                        ins = nc.vector.scalar_tensor_tensor(conf_acc[:, h, :], window, tap, conf_acc[:, h, :], ALU.mult, ALU.add)
                    ins.then_inc(conf_conv, 1)

            def rope(l, n):
                dve.wait_ge(rot_psum, 2 * l + n + 1)
                if l == 0 and n == 0:
                    dve.wait_ge(rope_ready, 1)
                sin = rope_cs[:, 0:1, :].broadcast_to((P, 2, SEQ))
                step(nc.vector.tensor_tensor(rope_rs[:, n], tiles(bank[n][:], 2), sin, ALU.mult))
                dve.wait_ge(rope_scaled, 2 * l + n + 1)
                nc.vector.tensor_tensor(z[(Q_G, K_G)[n]], rope_rs[:, n], rope_qc[:, n], ALU.add).then_inc(roped, 1)

            def score_rows(l, q):
                width = P * (q + 1)
                maxima = row_max[:, q, :].rearrange("p (t j) -> p t j", t=2)
                dve.wait_ge(scores_psum, 2 * l + q + 1)
                for j in range(4):
                    ins = nc.vector.tensor_reduce(maxima[:, :, j], bank[j][:, 0:2 * width].rearrange("p (t k) -> p t k", t=2),
                                                  AX_X, ALU.max)
                step(ins)
                nc.vector.tensor_scalar(row_max[:, q, :], row_max[:, q, :], -SCALE, None, ALU.mult).then_inc(scores_max, 1)

            def mix_maps(l, q):
                width = P * (q + 1)
                maps = sc[:, 0:MAPS * width].rearrange("p (m k) -> p m k", m=MAPS)
                dve.wait_ge(probs_ready, MAPS * (2 * l + q + 1))
                step(nc.vector.reciprocal(row_inv[:, q, :], row_sum[:, q, :]))
                second = row_inv[:, q, :].rearrange("p (h m) -> p h m", m=2)[:, :, 1]
                step(nc.vector.tensor_scalar(second, second, neg_lam[:, l:l + 1], None, ALU.mult))
                if q:
                    dve.wait_ge(aT_psum, 3 * l + 1)
                for hd in range(HEADS):
                    m = 2 * hd + 1
                    ins = nc.vector.tensor_scalar(maps[:, m, :], maps[:, m, :], row_inv[:, q, m:m + 1], None, ALU.mult)
                step(ins)
                for hd in range(HEADS):
                    m = 2 * hd
                    ins = nc.vector.scalar_tensor_tensor(a_mix[:, hd * width:(hd + 1) * width], maps[:, m, :], row_inv[:, q, m:m + 1],
                                                         maps[:, m + 1, :], ALU.mult, ALU.add)
                ins.then_inc(mixed, 1)

            for l in range(DEPTH):
                if l == 0:
                    dve.wait_ge(first_loaded, 16)
                    dve.wait_ge(pos_loaded, 16)
                    step(nc.vector.tensor_copy(angle, pos_int))
                    step(nc.vector.tensor_scalar(angle, angle, c("inv"), None, ALU.mult))
                    for h in range(2):
                        ins = nc.vector.tensor_scalar(turns[:, h, :], angle, 1.0 / TWO_PI, 0.25 * h, ALU.mult, ALU.add)
                    step(ins)
                    step(nc.vector.tensor_scalar(turns, turns, MAGIC, -MAGIC, ALU.add, ALU.add))
                    for j, piece in enumerate(TURN):
                        source = angle.rearrange("p (a t) -> p a t", a=1).broadcast_to((P, 2, SEQ)) if j == 0 else trig
                        step(nc.vector.scalar_tensor_tensor(trig, turns, -piece, source, ALU.mult, ALU.add))
                    step(nc.vector.tensor_scalar(trig[:, 1, :], trig[:, 1, :], 0.5 * np.pi, None, ALU.add))
                    nc.vector.tensor_scalar(trig, trig, PI_IN, -PI_IN, ALU.min, ALU.max).then_inc(angles_ready, 1)
                    lo_of_unit(1)
                    lo_of_x(0)
                    lo_of_unit(2)
                    dve.wait_ge(sines_ready, 1)
                    nc.vector.tensor_scalar(rope_cs[:, 1, :], rope_cs[:, 1, :], c("roped"), c("unroped"), ALU.mult,
                                            ALU.add).then_inc(rope_ready, 1)
                    dve.wait_ge(consts_loaded, 16)
                    nc.vector.tensor_copy(ident_b[:], ident)
                    nc.vector.tensor_copy(causal_b[:], c("causal")).then_inc(tables_ready, 1)
                    dve.wait_ge(lam_loaded, 16)
                    step(nc.vector.tensor_tensor(lam_prod, lam_in[:, :, 0, :], lam_in[:, :, 1, :], ALU.mult))
                    nc.vector.tensor_reduce(lam_sum, lam_prod, AX_X, ALU.add).then_inc(lam_summed, 1)
                else:
                    lo_of_x(2)
                    lo_of_unit(2)
                for i in range(NZ):
                    if l == 0 and i == 1:
                        lo_of_unit(1)
                        dve.wait_ge(lam_exped, 1)
                        step(nc.vector.tensor_tensor(neg_lam[:], lam_exp[:, :, 1], lam_exp[:, :, 0], ALU.subtract))
                        for k in range(DEPTH):
                            ins = nc.vector.tensor_scalar(neg_lam[:, k:k + 1], neg_lam[:, k:k + 1], -LAM_INIT[k], None, ALU.add)
                        step(ins)
                        dve.wait_ge(cols_ready, DEPTH)
                        for k in range(DEPTH):
                            ins = nc.vector.tensor_scalar(cols[:, k, R_SG:R_SG + 1], cols[:, k, R_SG:R_SG + 1], 1.0 - LAM_INIT[k],
                                                          None, ALU.mult)
                        step(ins)
                        dve.wait_ge(router_split, 1)
                        nc.vector.tensor_tensor(router_lo[:], router_raw[:], router_hi[:].bitcast(F32),
                                                ALU.subtract).then_inc(router_split, 1)
                        dve.wait_ge(pads_zeroed, 3)
                    if i == 1:
                        dve.wait_ge(z_ready, NZ * l + 2)
                        step(nc.vector.tensor_tensor(conf_u[:, :, CPAD:], z[CA_G], z[CG_G], ALU.mult))
                    if i == 3:
                        rope(l, 0)
                    if i == 4:
                        rope(l, 1)
                    if i == 5:
                        score_rows(l, 0)
                    if i == 6:
                        mix_maps(l, 0)
                    if not (l == 0 and i == 1):
                        lo_of_unit(1)
                    if i == 6:
                        score_rows(l, 1)
                    if i == 7:
                        mix_maps(l, 1)
                    conv_taps(l, (0, 6, 4, 3, 8, 4, 10, 0, 0)[i])
                lo_of_y(l, 0)
                conv_taps(l, 14)
                dve.wait_ge(pool_psum, l + 1)
                for h in range(2):
                    ins = nc.vector.tensor_scalar(y32[:, h, :], bank[3][:, 256 * h:256 * h + 256],
                                                  cols[:, l, R_PS + h:R_PS + h + 1], None, ALU.mult)
                ins.then_inc(pool_y, 1)
                lo_of_y(l, 1)
                conv_taps(l, len(taps) - 35 - 14)
                for q in range(TT):
                    dve.wait_ge(o_copied, 2 * l + q + 1)
                    step(nc.vector.tensor_tensor(o_sq[:, q], o_sb[:, q], o_sb[:, q], ALU.mult))
                    step(nc.vector.tensor_reduce(head_ms[:, q, :], o_sq[:, q], AX_X, ALU.add))
                    nc.vector.tensor_scalar(head_ms[:, q, :], head_ms[:, q, :], 1.0 / VD, EPS, ALU.mult, ALU.add).then_inc(o_ms, 1)
                dve.wait_ge(conf_mean, l + 1)
                mean = bank[1][:, 0:256].rearrange("p (a t) -> p a t", a=1).broadcast_to((P, 2, SEQ))
                step(nc.vector.tensor_tensor(xc, conf_acc, mean, ALU.subtract))
                nc.vector.tensor_tensor(xsq, xc, xc, ALU.mult).then_inc(conf_sq, 1)
                for q in range(TT):
                    dve.wait_ge(o_rstd, 2 * l + q + 1)
                    scale = head_ms[:, q, :].rearrange("p (h a) -> p h a", a=1).broadcast_to((P, HEADS, VD))
                    nc.vector.tensor_tensor(o_sq[:, q], o_sb[:, q], scale, ALU.mult).then_inc(o_normed, 1)
                lo_of_unit(1)
                dve.wait_ge(oT_psum, l + 1)
                nc.vector.tensor_scalar(y32[:, 4:6, :], tiles(bank[0][:], 2), cols[:, l, R_SG:R_SG + 1], None, ALU.mult).then_inc(o_y, 1)
                lo_of_y(l, 2)
                dve.wait_ge(conf_std, l + 1)
                step(nc.vector.reciprocal(xsq[:, 1, :], xsq[:, 0, :]))
                inv_std = xsq[:, 1:2, :].broadcast_to((P, 2, SEQ))
                nc.vector.tensor_tensor(xc, xc, inv_std, ALU.mult).then_inc(conf_normed, 1)
                lo_of_y(l, 3)
                if l == 0:
                    lo_of_unit(1)
                else:
                    lo_of_moe(MOE_ORDER[0], 0)

                def mixers_ready(t):
                    if t == 0:
                        dve.wait_ge(wo_psum, l + 1)
                    else:
                        dve.wait_ge(w_used, WO_UNIT[l] + NWO)

                layer_norm(2 * l, mixers_ready, lambda t, h: bank[4 + 2 * t + h][:])
                lo_of_x(2 * l + 1)
                if l == 0:
                    lo_of_unit(2)
                    for j in range(1, FP + 1):
                        b = 2 * ((j - 1) % 2)
                        dve.wait_ge(g_act, j)
                        dve.wait_ge(w_used, dense_unit("u", j - 1) + 1)
                        nc.vector.tensor_tensor(d_h[:, (j - 1) % 2, :], d_act[:, (j - 1) % 2, :], bank[b + 1][:],
                                                ALU.mult).then_inc(h_ready, 1)
                        if j < FP:
                            lo_of_unit(1)
                        dve.wait_ge(h_hi_ready, j)
                        nc.vector.tensor_tensor(h_lo[:, (j - 1) % 2, :], d_h[:, (j - 1) % 2, :],
                                                h_hi[:, (j - 1) % 2, :].bitcast(F32), ALU.subtract).then_inc(h_lo_ready, 1)
                        if j < FP:
                            lo_of_unit(2)
                    lo_of_unit(1)

                    def dense_ready(t):
                        if t == 0:
                            dve.wait_ge(ffn_psum, 1)
                        else:
                            dve.wait_ge(w_used, Z_UNIT[1])

                    layer_norm(1, dense_ready, lambda t, h: bank[4 + 2 * t + h][:])
            assert units[0] == MOE_UNIT, (units, MOE_UNIT)

            def hot(column):
                for t in range(TT):
                    ins = nc.vector.tensor_scalar(one_hot[:, t, :], c("iota"), slot_of[:, t, column], None, ALU.is_equal)
                ins.then_inc(hot_ready, 1)

            nc.vector.memset(gatedT, 0.0).then_inc(gT_ready, 1)
            nc.vector.memset(bank[5][:], 0.0)
            nc.vector.memset(bank[6][:], 0.0)
            nc.vector.memset(slot_of[:], -1.0)
            nc.vector.memset(gate_of[:], 0.0)
            step(nc.vector.memset(item_tab[:], 0.0))
            step(nc.vector.tensor_copy(item_tab[:, 0:NE], c("experts")))
            dve.wait_ge(logits_psum, 1)
            nc.vector.tensor_copy(logitsT, bank[7][0:NE, 256:512]).then_inc(logitsT_ready, 1)
            dve.wait_ge(logits_psum, 2)
            step(nc.vector.tensor_copy(logits, tiles(bank[7][:, 0:16], 2)))
            step(nc.vector.tensor_reduce(top, logits, AX_X, ALU.max))

            def over_experts(v):
                return v.rearrange("p (t a) -> p t a", a=1).broadcast_to((P, TT, NE))

            nc.vector.tensor_tensor(expl, logits, over_experts(top), ALU.subtract).then_inc(logits_off, 1)
            above = pairs.rearrange("p (t e f) -> p t e f", t=TT, e=NE)
            level = pairs2.rearrange("p (t e f) -> p t e f", t=TT, e=NE)
            other = logits.rearrange("p t (a e) -> p t a e", a=1).broadcast_to((P, TT, NE, NE))
            own = logits.rearrange("p t (e a) -> p t e a", a=1).broadcast_to((P, TT, NE, NE))
            nc.vector.tensor_tensor(above, other, own, ALU.is_gt)
            step(nc.vector.tensor_tensor(level, other, own, ALU.is_equal))
            before = c("before").rearrange("p (a n) -> p a n", a=1).broadcast_to((P, TT, NE * NE))
            step(nc.vector.tensor_tensor(tiles(pairs2, TT), tiles(pairs2, TT), before, ALU.mult))
            step(nc.vector.tensor_tensor(pairs, pairs, pairs2, ALU.add))
            step(nc.vector.tensor_reduce(rank, above, AX_X, ALU.add))
            nc.vector.tensor_scalar(mask, rank, 1.5, None, ALU.is_lt).then_inc(mask_ready, 1)
            dve.wait_ge(logits_exp, 1)
            dve.wait_ge(mask_ready, 1)
            step(nc.vector.tensor_tensor(expl, expl, mask, ALU.mult))
            step(nc.vector.tensor_reduce(denom, expl, AX_X, ALU.add))
            step(nc.vector.reciprocal(rdenom, denom))
            step(nc.vector.tensor_tensor(gates, expl, over_experts(rdenom), ALU.mult))
            dve.wait_ge(ranks_psum, 1)
            step(nc.vector.tensor_tensor(slots, tiles(bank[7][:, 64:80], 2), mask, ALU.mult))
            step(nc.vector.tensor_scalar(slots, slots, -1.0, None, ALU.add))
            step(nc.vector.tensor_copy(slot_of[:, :, 0:NE], slots))
            hot(slice(0, 1))
            lo_of_moe(MOE_ORDER[1], 0)
            nc.vector.tensor_copy(gate_of[:, :, 0:NE], gates)
            step(nc.vector.tensor_scalar(over, bank[7][:, 80:88], P + 0.5, None, ALU.is_gt))
            over_all = over.rearrange("p (a e) -> p a e", a=1).broadcast_to((P, NE, NE))
            step(nc.vector.tensor_tensor(above[:, 0], over_all, c("upto").rearrange("p (e f) -> p e f", e=NE), ALU.mult))
            step(nc.vector.tensor_reduce(cum_over, above[:, 0], AX_X, ALU.add))

            def thrice(v):
                return v.rearrange("p (a e) -> p a e", a=1).broadcast_to((P, 3, NE))

            step(nc.vector.tensor_tensor(chosen, thrice(cum_over), c("spill").rearrange("p (j e) -> p j e", j=3), ALU.is_equal))
            step(nc.vector.tensor_tensor(chosen, chosen, thrice(over), ALU.mult))
            chosen_t = chosen.rearrange("p (a j) e -> p a j e", a=1).broadcast_to((P, TT, 3, NE))

            def over_items(v):
                return v.rearrange("p t (a e) -> p t a e", a=1).broadcast_to((P, TT, 3, NE))

            nc.vector.tensor_tensor(picked, chosen_t, over_items(slots), ALU.mult)
            nc.vector.tensor_tensor(picked_gate, chosen_t, over_items(gates), ALU.mult)
            nc.vector.tensor_tensor(picked_expert, chosen, thrice(c("experts")), ALU.mult)
            step(nc.vector.tensor_reduce(item_tab[:, 12:13], over, AX_X, ALU.add))
            nc.vector.tensor_reduce(slot_of[:, :, NE:NE + 3], picked, AX_X, ALU.add)
            nc.vector.tensor_reduce(gate_of[:, :, NE:NE + 3], picked_gate, AX_X, ALU.add)
            nc.vector.tensor_reduce(item_tab[:, NE:NE + 3], picked_expert, AX_X, ALU.add)
            step(nc.vector.tensor_scalar(item_tab[:, 12:13], item_tab[:, 12:13], float(NE), None, ALU.add))
            nc.vector.tensor_scalar(slot_of[:, :, NE:NE + 3], slot_of[:, :, NE:NE + 3], -float(P), None, ALU.add)
            nc.vector.tensor_copy(item_int[:, 0:13], item_tab[:, 0:13]).then_inc(routed, 1)

            def lo_of_item(before):
                dve.wait_ge(item_hi, before + 1)
                for h, b in enumerate((1, 3)):
                    at = (slice(None), slice(4 * h, 4 * h + 4), slice(0, P))
                    ins = nc.vector.tensor_tensor(a_lo[at], tiles(bank[b][:], 4), a_hi[at].bitcast(F32), ALU.subtract)
                ins.then_inc(item_lo, 1)

            def add_up(before):
                dve.wait_ge(acc_ready, before * 4 + 1)
                for q in range(4):
                    t, h = q // 2, q % 2
                    dve.wait_ge(comb_psum, before * 4 + (q + 1))
                    ah = acc[:, t, 512 * h:512 * h + 512]
                    nc.vector.tensor_tensor(ah, ah, bank[COMB_BANKS[q]][:], ALU.add).then_inc(acc_ready, 1)

            lo_of_item(0)
            dve.wait_ge(routed, 1)
            items = dve.value_load(item_int[0:1, 12:13], min_val=NE, max_val=MAX_ITEMS)
            with dve.Fori(0, items) as item:
                for ch in range(NC + 1):
                    if ch:
                        dve.wait_ge(mg_act, item * NC + ch)
                        dve.wait_ge(w_used, item * NU + (MOE_UNIT + MOE_POS["u", ch - 1, 1] + 1))
                        nc.vector.tensor_tensor(m_h[:, (ch - 1) % 2, :], m_act[:, (ch - 1) % 2, :], bank[2 + (ch - 1) % 2][:],
                                                ALU.mult).then_inc(mh_ready, 1)
                    if ch < NC:
                        if ch:
                            lo_of_moe(("g", ch, 0), item)
                            lo_of_moe(("g", ch, 1), item)
                        if ch == 1:
                            add_up(item)
                        lo_of_moe(("u", ch, 0), item)
                        lo_of_moe(("u", ch, 1), item)
                    else:
                        lo_of_moe(("d", ch - 1, 0), item)
                        lo_of_moe(("d", ch - 1, 1), item)
                    if ch:
                        dve.wait_ge(mh_hi, item * NC + ch)
                        nc.vector.tensor_tensor(h_lo[:, 0, :], bank[4][:], h_hi[:, 0, :].bitcast(F32), ALU.subtract).then_inc(mh_lo, 1)
                    if 0 < ch < NC:
                        lo_of_moe(("d", ch - 1, 0), item)
                        lo_of_moe(("d", ch - 1, 1), item)
                    if ch == 1:
                        for t in range(TT):
                            ins = nc.vector.tensor_scalar(gated[:, t, :], c("iota"), slot_of[:, t, bass.ds(item, 1)],
                                                          gate_of[:, t, bass.ds(item, 1)], ALU.is_equal, ALU.mult)
                        ins.then_inc(gated_ready, 1)
                    if ch == 3:
                        hot(bass.ds(item + 1, 1))
                lo_of_moe(MOE_ORDER[0], item + 1)
                lo_of_item(item + 1)
                lo_of_moe(MOE_ORDER[1], item + 1)
            add_up(items)

            def sums_ready(t):
                dve.wait_ge(acc_ready, items * 4 + (2 * t + 3))

            layer_norm(3, sums_ready, lambda t, h: acc[:, t, 512 * h:512 * h + 512])

        @block.tensor
        def _(pe):
            units = [0]
            ident = c("ident")

            def product(target, stationary, moving, first, last):
                (s_hi, s_lo), (m_hi, m_lo) = stationary, moving
                nc.tensor.matmul(target, s_hi, m_hi, start=first, stop=False)
                nc.tensor.matmul(target, s_hi, m_lo, start=False, stop=False)
                return nc.tensor.matmul(target, s_lo, m_hi, start=False, stop=last)

            def next_unit(k):
                n = units[0]
                units[0] += 1
                pe.wait_ge(w_lo_ready, n + 1)
                return split_pair(n, k)

            def transpose_x(n):
                for q in range(4):
                    t, k0 = q // 2, 4 * (q % 2)
                    if n:
                        pe.wait_ge(x_ready, TT * (n - 1) + t + 1)
                    for k in range(k0, k0 + 4):
                        last = nc.tensor.transpose(bank[q][:, (k - k0) * P:(k - k0 + 1) * P], xs[:, t, k * P:(k + 1) * P], ident)
                    last.then_inc(xt_psum, 1)

            def project(l, i):
                if i == 0:
                    pe.wait_ge(xt_lo, 4 * (2 * l + 1))
                if i >= 3:
                    pe.wait_ge(z_ready, NZ * l + i - 2)
                m_hi, m_lo = next_unit(KT)
                for h in range(2):
                    to = bank[Z_BANKS[i % 3]][:, 256 * h:256 * h + 256]
                    for k in range(KT):
                        if Z_ORDER[i] == V_G:
                            tokens = slice(h * P, (h + 1) * P)
                            last = product(to, (a_hi[:, k, tokens], a_lo[:, k, tokens]), (m_hi[:, k, :], m_lo[:, k, :]),
                                           k == 0, k == KT - 1)
                        else:
                            channels = slice(h * P, (h + 1) * P)
                            last = product(to, (m_hi[:, k, channels], m_lo[:, k, channels]), (a_hi[:, k, :], a_lo[:, k, :]),
                                           k == 0, k == KT - 1)
                last.then_inc(w_used, 1)

            def scores(l, q):
                width = P * (q + 1)
                pe.wait_ge(roped, 2 * l + 2)
                pe.wait_ge(tables_ready, 1)
                if q:
                    pe.wait_ge(probs_ready, MAPS * (2 * l + 1))
                for t in range(2):
                    for j in range(4):
                        to = bank[j][:, t * width:(t + 1) * width]
                        nc.tensor.matmul(to, ident_b[:], causal_b[:, SEQ - width:], start=True, stop=False)
                        last = nc.tensor.matmul(to, z[Q_G][32 * j:32 * j + 32, t, q * P:(q + 1) * P],
                                                z[K_G][32 * j:32 * j + 32, t, 0:width], start=False, stop=True)
                last.then_inc(scores_psum, 1)

            def transpose_probs(l, q):
                pe.wait_ge(mixed, 2 * l + q + 1)
                if q:
                    pe.wait_ge(probs_ready, MAPS * (2 * l + 2))
                for n, b in enumerate(([7], [0, 1])[q]):
                    for k in range(4):
                        at = (4 * n + k) * P
                        last = nc.tensor.transpose(bank[b][:, k * P:(k + 1) * P], a_mix[:, at:at + P], ident)
                    last.then_inc(aT_psum, 1)

            def attend(l, q):
                pe.wait_ge(aT_ready, 3 * l + 1 + 2 * q)
                for hd in range(HEADS):
                    for kb in range(q + 1):
                        at = (hd * (q + 1) + kb) * P
                        last = nc.tensor.matmul(bank[2][:, 256 * q + VD * hd:256 * q + VD * hd + VD], aT[q][:, at:at + P],
                                                z[V_G][:, kb, VD * hd:VD * hd + VD], start=(kb == 0), stop=(kb == q))
                if q:
                    last.then_inc(o_psum, 1)

            def residual(n):
                if n:
                    pe.wait_ge(x_ready, TT * n)
                for t in range(TT):
                    for h in range(2):
                        nc.tensor.matmul(bank[4 + 2 * t + h][:], c("alpha"), xs[:, t, 512 * h:512 * h + 512], start=True, stop=False)

            def down(k0, hi, lo, final, tile0_done):
                m_hi, m_lo = next_unit(2)
                for t in range(TT):
                    tokens = slice(t * P, (t + 1) * P)
                    for k in range(2):
                        for h in range(2):
                            half = slice(512 * h, 512 * h + 512)
                            last = product(bank[4 + 2 * t + h][:], (hi[:, k0 + k, tokens], lo[:, k0 + k, tokens]),
                                           (m_hi[:, k, half], m_lo[:, k, half]), False, final and k == 1)
                    if final and t == 0:
                        last.then_inc(tile0_done, 1)
                last.then_inc(w_used, 1)

            def mix_out(l, n):
                pe.wait_ge(y_lo, NWO * l + n + 1)
                down(2 * WO_ORDER[n], a_hi, a_lo, n == NWO - 1, wo_psum)

            def dense_in(kind, j):
                b = 2 * (j % 2) + (kind == "u")
                if j == 0:
                    pe.wait_ge(xt_lo, 8)
                if j > 1:
                    pe.wait_ge(h_ready, j - 1)
                m_hi, m_lo = next_unit(KT)
                for f in range(2):
                    hidden = slice(f * P, (f + 1) * P)
                    for k in range(KT):
                        last = product(bank[b][:, 256 * f:256 * f + 256], (m_hi[:, k, hidden], m_lo[:, k, hidden]),
                                       (a_hi[:, k, :], a_lo[:, k, :]), k == 0, k == KT - 1)
                last.then_inc(w_used, 1)

            h_hi_t = h_hi[:].rearrange("p b (f t) -> p (b f) t", f=2)
            h_lo_t = h_lo[:].rearrange("p b (f t) -> p (b f) t", f=2)

            pe.wait_ge(first_loaded, 16)
            pe.wait_ge(x_loaded, 16 * TT)
            for l in range(DEPTH):
                transpose_x(2 * l)
                for i in range(NZ):
                    project(l, i)
                    if l == 0 and i == 1:
                        pe.wait_ge(rows_loaded, 16 * 7)
                        for k in range(DEPTH):
                            nc.tensor.transpose(bank[2 + k][:, 0:NR], rows[0:NR, k, :], ident[0:NR, 0:NR]).then_inc(cols_psum, 1)
                    if i in (3, 4):
                        if i == 3:
                            pe.wait_ge(consts_loaded, 16)
                        n, g = ((0, Q_G), (1, K_G))[i - 3]
                        pe.wait_ge(z_ready, NZ * l + i)
                        nc.tensor.matmul(bank[n][:], c("rot"), z[g].rearrange("p h t -> p (h t)"), start=True, stop=True).then_inc(rot_psum, 1)
                    if i == 5:
                        if l == 0:
                            pe.wait_ge(cols_ready, DEPTH)
                        scores(l, 0)
                    if i == 6:
                        scores(l, 1)
                    if i == 7:
                        transpose_probs(l, 0)
                transpose_probs(l, 1)
                pe.wait_ge(aT_ready, 3 * l + 1)
                pe.wait_ge(z_ready, NZ * (l + 1))
                residual(2 * l)
                attend(l, 0)
                attend(l, 1)
                pe.wait_ge(pool_diff, l + 1)
                pe.wait_ge(pool_loaded, 16 * 4 * DEPTH)
                for h in range(2):
                    last = nc.tensor.matmul(bank[3][:, 256 * h:256 * h + 256], pool_mat[:, l, h, :], y32[:, h, :], start=True, stop=True)
                last.then_inc(pool_psum, 1)
                mix_out(l, 0)
                pe.wait_ge(conf_conv, (l + 1) * 2 * CONF_K)
                for h in range(2):
                    last = nc.tensor.matmul(bank[1][:, 0:256], c("mean"), conf_acc[:, h, :], start=(h == 0), stop=(h == 1))
                last.then_inc(conf_mean, 1)
                mix_out(l, 1)
                pe.wait_ge(o_normed, 2 * (l + 1))
                for ct in range(2):
                    for q in range(TT):
                        last = nc.tensor.transpose(bank[0][:, ct * SEQ + q * P:ct * SEQ + (q + 1) * P],
                                                   o_sq[:, q].rearrange("p h e -> p (h e)")[:, ct * P:(ct + 1) * P], ident)
                last.then_inc(oT_psum, 1)
                pe.wait_ge(conf_sq, l + 1)
                for h in range(2):
                    last = nc.tensor.matmul(bank[1][:, 256:512], c("mean"), xsq[:, h, :], start=(h == 0), stop=(h == 1))
                last.then_inc(conf_var, 1)
                mix_out(l, 2)
                mix_out(l, 3)
                transpose_x(2 * l + 1)
                if l == 0:
                    residual(1)
                if l == 0:
                    for kind, j in DENSE_ORDER:
                        if kind == "d":
                            pe.wait_ge(h_lo_ready, j + 1)
                            down(2 * (j % 2), h_hi_t, h_lo_t, j == FP - 1, ffn_psum)
                        else:
                            dense_in(kind, j)
            assert units[0] == MOE_UNIT, (units, MOE_UNIT)

            pe.wait_ge(xt_lo, 16)
            pe.wait_ge(router_split, 2)
            for k in range(KT):
                last = product(bank[7][0:NE, 256:512], (router_hi[:, k, :], router_lo[:, k, :]), (a_hi[:, k, :], a_lo[:, k, :]),
                               k == 0, k == KT - 1)
            last.then_inc(logits_psum, 1)
            pe.wait_ge(logitsT_ready, 1)
            for t in range(TT):
                last = nc.tensor.transpose(bank[7][:, NE * t:NE * t + NE], logitsT[:, t * P:(t + 1) * P], ident[0:NE, 0:NE])
            last.then_inc(logits_psum, 1)
            pe.wait_ge(mask_ready, 1)
            for at, pieces in ((64, (("tri", 0),)), (72, (("ones", 0), ("tri", 1))), (80, (("ones", 0), ("ones", 1)))):
                for n, (table, t) in enumerate(pieces):
                    last = nc.tensor.matmul(bank[7][:, at:at + NE], c(table), mask[:, t, :], start=(n == 0), stop=(n == len(pieces) - 1))
            last.then_inc(ranks_psum, 1)

            def gather(before):
                pe.wait_ge(hot_ready, before + 1)
                for k in range(KT):
                    for t in range(TT):
                        last = nc.tensor.matmul(bank[1 + 2 * (k // 4)][:, (k % 4) * P:(k % 4 + 1) * P], xs[:, t, k * P:(k + 1) * P],
                                                one_hot[:, t, :], start=(t == 0), stop=(t == TT - 1))
                last.then_inc(gather_psum, 1)

            def moe_unit(unit, item):
                kind, ch, half = unit
                n = MOE_UNIT + MOE_POS[unit]
                pe.wait_ge(w_lo_ready, item * NU + (n + 1))
                if kind == "d":
                    m_hi, m_lo = split_pair(n, 2)
                    for k in range(2):
                        tile = slice((2 * half + k) * P, (2 * half + k + 1) * P)
                        for h in range(2):
                            cols_ = slice(512 * h, 512 * h + 512)
                            last = product(bank[5 + h][:], (h_hi[:, 0, tile], h_lo[:, 0, tile]), (m_hi[:, k, cols_], m_lo[:, k, cols_]),
                                           ch == 0 and half == 0 and k == 0, ch == NC - 1 and half == 1 and k == 1)
                else:
                    m_hi, m_lo = split_pair(n, 4)
                    b = ch % 2 + 2 * (kind == "u")
                    for k in range(4):
                        last = product(bank[b][:], (a_hi[:, 4 * half + k, 0:P], a_lo[:, 4 * half + k, 0:P]), (m_hi[:, k, :], m_lo[:, k, :]),
                                       half == 0 and k == 0, half == 1 and k == 3)
                last.then_inc(w_used, 1)

            def transpose_h(ch, item):
                pe.wait_ge(mh_ready, item * NC + (ch + 1))
                for f in range(4):
                    last = nc.tensor.transpose(bank[4][:, f * P:(f + 1) * P], m_h[:, ch % 2, f * P:(f + 1) * P], ident)
                last.then_inc(mhT_psum, 1)

            def combine(before):
                pe.wait_ge(my_ready, before + 1)
                pe.wait_ge(gT_ready, before + 1)
                for q in range(4):
                    t, h = q // 2, q % 2
                    nc.tensor.matmul(bank[COMB_BANKS[q]][:], gatedT[:, t * P:(t + 1) * P], y_sb[:, 512 * h:512 * h + 512],
                                     start=True, stop=True).then_inc(comb_psum, 1)

            gather(0)
            pe.wait_ge(routed, 1)
            items = pe.value_load(item_int[0:1, 12:13], min_val=NE, max_val=MAX_ITEMS)
            with pe.Fori(0, items) as item:
                pe.wait_ge(item_lo, item + 1)
                for ch in range(NC + 1):
                    if ch < NC:
                        moe_unit(("g", ch, 0), item)
                        moe_unit(("g", ch, 1), item)
                    if ch:
                        if ch == 1:
                            pe.wait_ge(acc_ready, item * 4 + 5)
                        transpose_h(ch - 1, item)
                    if ch < NC:
                        moe_unit(("u", ch, 0), item)
                        moe_unit(("u", ch, 1), item)
                    if ch == 0:
                        combine(item)
                    if ch == 2:
                        pe.wait_ge(gated_ready, item + 1)
                        for t in range(TT):
                            last = nc.tensor.transpose(bank[7][:, t * P:(t + 1) * P], gated[:, t, :], ident)
                        last.then_inc(gT_psum, 1)
                    if ch == NC:
                        gather(item + 1)
                    if ch:
                        pe.wait_ge(mh_lo, item * NC + ch)
                        moe_unit(("d", ch - 1, 0), item)
                        moe_unit(("d", ch - 1, 1), item)
            combine(items)


_INS = ["x", "positions", "w_in", "w_o", "pool_w", "pool_scale", "sconv_w", "diff_lambda", "diff_subln_g",
        "conf_dw", "conf_ln_g", "conf_ln_b", "ln1_g", "ln1_b", "ln2_g", "ln2_b", "ffn_wg", "ffn_wu", "ffn_wd",
        "router_w", "moe_wg", "moe_wu", "moe_wd"]


def kernel(**inputs):
    import concourse.bacc as _bacc
    from concourse.bass_utils import run_bass_kernel_spmd as _run

    nc = _bacc.Bacc("TRN2", target_bir_lowering=False, num_devices=1)
    arrays, args = {}, []
    for name, a in [("constants", CONSTANTS)] + [(n, np.ascontiguousarray(inputs[n])) for n in _INS]:
        arrays[f"in_{name}_dram"] = a
        args.append(nc.dram_tensor(f"in_{name}_dram", a.shape, mybir.dt.from_np(a.dtype), kind="ExternalInput").ap())
    args.append(nc.dram_tensor("out_0_dram", (1, SEQ, D), F32, kind="ExternalOutput").ap())
    hybrid_trunk(nc, *args)
    r = _run(nc, [arrays], core_ids=[0])
    return r.results[0]["out_0_dram"]
```

```python
from contextlib import ExitStack

import numpy as np

import concourse.bass as bass
from concourse import mybir

F32 = mybir.dt.float32
F32R = mybir.dt.float32r
BF16 = mybir.dt.bfloat16
I32 = mybir.dt.int32
ALU = mybir.AluOpType
ACT = mybir.ActivationFunctionType
AX_X = mybir.AxisListType.X

P = 128
D = 1024
SEQ = 256
DEPTH = 2
TT = SEQ // P
XQ = 2 * TT
KT = D // P
GW = 256
WINDOWS = (2, 4, 8, 16)
SCONV_K = 3
CONF_K = 31
HEADS = 4
MAPS = 2 * HEADS
QK = 32
VD = 64
ROPE_DIM = QK // 4
THETA = 500000.0
D_FF = 2816
NE = 8
FE = 3584
ALPHA = (2 * DEPTH) ** 0.25
EPS = 1e-5
SCALE = float(QK) ** -0.5
LAM_INIT = [0.8 - 0.6 * float(np.exp(-0.3 * l)) for l in range(DEPTH)]

UNIT = 2048
RAW_SLOTS = 7
SPLIT_SLOTS = 3

POOL_G, SB_G, SCG_G, SH_G, Q_G, K_G, V_G, CA_G, CG_G = range(9)
Z_ORDER = [CA_G, CG_G, Q_G, K_G, SCG_G, SH_G, SB_G, POOL_G, V_G]
NZ = len(Z_ORDER)
Z_BANKS = (4, 5, 6)
WO_ORDER = [1, 0, 2, 3]
NWO = len(WO_ORDER)
FP = D_FF // GW
DENSE_ORDER = [("g", 0), ("u", 0)]
for _j in range(1, FP):
    DENSE_ORDER += [("g", _j), ("u", _j), ("d", _j - 1)]
DENSE_ORDER += [("d", FP - 1)]

CW = 512
NC = FE // CW
MOE_ORDER = []
for _c in range(NC):
    MOE_ORDER += [("g", _c, 0), ("g", _c, 1), ("u", _c, 0), ("u", _c, 1)]
    if _c:
        MOE_ORDER += [("d", _c - 1, 0), ("d", _c - 1, 1)]
MOE_ORDER += [("d", NC - 1, 0), ("d", NC - 1, 1)]
NU = len(MOE_ORDER)
assert NU % RAW_SLOTS == 0 and NU % SPLIT_SLOTS == 0
MOE_POS = {u: i for i, u in enumerate(MOE_ORDER)}
PARTS = 2
PART = UNIT // PARTS
AHEAD = SPLIT_SLOTS
COMB_BANKS = (4, 5, 6, 7)
MAX_ITEMS = NE + 3

Z_UNIT = [0, NZ + NWO + len(DENSE_ORDER)]
WO_UNIT = [z + NZ for z in Z_UNIT]
FFN_UNIT = [z + NZ + NWO for z in Z_UNIT]
MOE_UNIT = FFN_UNIT[1]



def dense_unit(kind, j):
    return FFN_UNIT[0] + DENSE_ORDER.index((kind, j))


POOL_UNITS = [z + i for z in Z_UNIT for i in (5, 7, NZ + NWO - 1)]


def lo_counts(n):
    by_pool = sum(u <= n for u in POOL_UNITS)
    return n + 1 - by_pool, by_pool


LO_BASE = MOE_UNIT - len(POOL_UNITS)

SPARE_ITEMS = range(3, 6)
SPARE_POS = 9
assert max(SPARE_ITEMS) < NE

R_DW, R_SW, R_PS, R_LG, R_LB, R_SG = 0, 62, 68, 70, 72, 74
NR = 75


def _constants():
    at, parts, n = {}, [], 0

    def put(name, a):
        nonlocal n
        a = np.asarray(a, np.float32).reshape(P, -1)
        at[name] = (n, a.shape[1])
        parts.append(a)
        n += a.shape[1]

    i = np.arange(P)
    half = ROPE_DIM // 2
    inv = np.float32(THETA) ** (-np.arange(0, ROPE_DIM, 2, dtype=np.float32) / np.float32(ROPE_DIM))
    in_rope = (i % QK < ROPE_DIM)
    put("ident", np.eye(P))
    put("inv", np.where(in_rope, inv[i % half], 0.0))
    put("roped", in_rope)
    put("unroped", ~in_rope)
    put("minus_half", np.full((P, 4), -0.5))
    put("eps", np.full((P, 1), EPS))
    at["first"] = (0, n)
    put("alpha", ALPHA * np.eye(P))
    put("tri", (i[:, None] <= i[None, :]))
    put("ones", np.ones((P, P)))
    put("mean", np.full((P, P), 1.0 / GW))
    rot = np.zeros((P, P))
    for c in range(P):
        if c % QK < half:
            rot[c + half, c] = -1.0
        elif c % QK < ROPE_DIM:
            rot[c - half, c] = 1.0
    put("rot", rot)
    put("iota", np.broadcast_to(np.arange(P), (P, P)))
    put("causal", np.concatenate([np.zeros((P, P)), np.where(i[None, :] <= i[:, None], 0.0, -1e30)], 1))
    t = np.arange(1, SEQ + 1)
    counts = np.stack([np.minimum(t[None, :], np.repeat(WINDOWS[2 * h:2 * h + 2], 64)[:, None]) for h in range(2)], 1)
    put("rcount", np.float32(1.0) / counts.astype(np.float32))
    e = np.arange(NE)
    put("before", np.broadcast_to((e[None, :] < e[:, None]).ravel(), (P, NE * NE)))
    put("upto", np.broadcast_to((e[None, :] <= e[:, None]).ravel(), (P, NE * NE)))
    put("experts", np.broadcast_to(e, (P, NE)))
    put("spill", np.broadcast_to(np.repeat(np.arange(1, 4), NE), (P, 3 * NE)))
    return at, np.ascontiguousarray(np.concatenate(parts, 1))


CONST_AT, CONSTANTS = _constants()

TWO_PI = 2.0 * np.pi
TURN = []
_rest = TWO_PI
for _ in range(3):
    _step = 2.0 ** (np.floor(np.log2(_rest)) - 7)
    TURN.append(float(np.floor(_rest / _step) * _step))
    _rest -= TURN[-1]
TURN.append(float(np.float32(_rest)))
MAGIC = 1.5 * 2.0 ** 23
PI_IN = 3.1415925


def hybrid_trunk(nc, consts, x, positions, w_in, w_o, pool_w, pool_scale, sconv_w, diff_lambda, diff_subln_g,
                 conf_dw, conf_ln_g, conf_ln_b, ln1_g, ln1_b, ln2_g, ln2_b, ffn_wg, ffn_wu, ffn_wd,
                 router_w, moe_wg, moe_wu, moe_wd, out):
    with ExitStack() as ctx:
        def sb(name, shape, dt=F32):
            return ctx.enter_context(nc.sbuf_tensor(name, shape, dt))

        def sem(name):
            return ctx.enter_context(nc.semaphore(name))

        bank = [ctx.enter_context(nc.psum_tensor(f"bank{b}", [P, 512], F32)) for b in range(8)]
        raw = sb("raw", [P, RAW_SLOTS, UNIT])
        w_hi = sb("w_hi", [P, SPLIT_SLOTS, UNIT], F32R)
        w_lo = sb("w_lo", [P, SPLIT_SLOTS, UNIT], F32R)
        a_hi = sb("a_hi", [P, KT, SEQ], F32R)
        a_lo = sb("a_lo", [P, KT, SEQ], F32R)
        h_hi = sb("h_hi", [P, 2, 512], F32R)
        h_lo = sb("h_lo", [P, 2, 512], F32R)
        router_raw = sb("router_raw", [P, KT, NE])
        router_hi = sb("router_hi", [P, KT, NE], F32R)
        router_lo = sb("router_lo", [P, KT, NE], F32R)
        xs = sb("xs", [P, TT, D])
        cst = sb("cst", [P, CONSTANTS.shape[1]])
        ln_gb = sb("ln_gb", [P, 2, D])
        rope_cs = sb("rope_cs", [P, 2, SEQ])
        cols = sb("cols", [P, DEPTH, NR])
        pool_mat = sb("pool_mat", [P, DEPTH, 2, P])
        ident_b = sb("ident_b", [P, P], BF16)
        causal_b = sb("causal_b", [P, SEQ], BF16)
        lam_exp = sb("lam_exp", [P, DEPTH, 2])
        neg_lam = sb("neg_lam", [P, DEPTH])
        stats = sb("stats", [P, TT, 2, 6])
        mean_var = sb("mean_var", [P, TT, 2])
        rstd = sb("rstd", [P, TT])
        row_max = sb("row_max", [P, 2, MAPS])
        row_sum = sb("row_sum", [P, 2, MAPS])
        row_inv = sb("row_inv", [P, 2, MAPS])
        head_ms = sb("head_ms", [P, TT, HEADS])
        slot_of = sb("slot_of", [P, TT, 12])
        gate_of = sb("gate_of", [P, TT, 12])
        item_tab = sb("item_tab", [P, 16])
        item_int = sb("item_int", [P, 16], I32)
        work = sb("work", [P, 12448])

        def c(name, parts=P):
            at, n = CONST_AT[name]
            return cst[0:parts, at:at + n]

        def w(at, n, parts=P):
            return work[0:parts, at:at + n]

        z_at = {CA_G: 0, CG_G: 512, Q_G: 1024, K_G: 1536, SB_G: 2048, SCG_G: 2560, SH_G: 3072, V_G: 3584}
        z = {g: w(at, 512).rearrange("p (h t) -> p h t", h=2) for g, at in z_at.items()}
        CPAD, PPAD, SPAD = CONF_K - 1, 16, SCONV_K - 1
        conf_u = w(4096, 2 * (SEQ + CPAD)).rearrange("p (h t) -> p h t", h=2)
        conf_acc = w(4668, 512).rearrange("p (h t) -> p h t", h=2)
        pool_h = w(5180, 2 * (SEQ + PPAD)).rearrange("p (h t) -> p h t", h=2)
        pool_s = [w(5724 + 544 * b, 544).rearrange("p (h t) -> p h t", h=2) for b in range(2)]
        sconv_u = w(6812, 2 * (SEQ + SPAD)).rearrange("p (h t) -> p h t", h=2)
        sc = w(7328, 2048)
        a_mix = w(9376, 1024)
        y32 = w(10400, 2048).rearrange("p (k t) -> p k t", k=KT)
        xc, xsq = z[CA_G], z[SB_G]
        s_acc, s_tmp = z[SH_G], z[SCG_G]
        rope_rs = sc[:, 0:1024].rearrange("p (g h t) -> p g h t", g=2, h=2)
        rope_qc = sc[:, 1024:2048].rearrange("p (g h t) -> p g h t", g=2, h=2)
        aT = [w(512, 512), w(1024, 1024)]
        o_sb = sc[:, 0:512].rearrange("p (q h e) -> p q h e", q=2, h=HEADS)
        o_sq = sc[:, 512:1024].rearrange("p (q h e) -> p q h e", q=2, h=HEADS)
        rows = sc[:, 0:DEPTH * P].rearrange("p (l n) -> p l n", l=DEPTH)
        lam_in = a_mix[:, 0:DEPTH * 128].rearrange("p (l a b n) -> p (l a) b n", l=DEPTH, a=2, b=2)
        lam_prod = a_mix[:, 256:384].rearrange("p (l n) -> p l n", n=QK)
        lam_sum = a_mix[:, 384:388]
        pos_int = work[:, 10400:10656].bitcast(I32)
        angle = w(10656, 256)
        trig = w(10912, 512).rearrange("p (h t) -> p h t", h=2)
        turns = w(11424, 512).rearrange("p (h t) -> p h t", h=2)
        d_act = w(0, 1024).rearrange("p (b n) -> p b n", b=2)
        d_h = w(1024, 1024).rearrange("p (b n) -> p b n", b=2)
        m_act = w(0, 1024).rearrange("p (b n) -> p b n", b=2)
        m_h = w(1024, 1024).rearrange("p (b n) -> p b n", b=2)
        one_hot = w(2048, 256).rearrange("p (t s) -> p t s", t=TT)
        gated = w(2304, 256).rearrange("p (t s) -> p t s", t=TT)
        gatedT = w(2560, 256)
        y_sb = w(2816, 1024)
        acc = w(3840, 2048).rearrange("p (t n) -> p t n", t=TT)
        logitsT = w(0, SEQ, NE)
        logits = w(5952, 16).rearrange("p (t e) -> p t e", t=TT)
        mask = w(5968, 16).rearrange("p (t e) -> p t e", t=TT)
        expl = w(6000, 16).rearrange("p (t e) -> p t e", t=TT)
        rank = w(6016, 16).rearrange("p (t e) -> p t e", t=TT)
        count_b = {"tri": work[:, 400:464].bitcast(BF16), "ones": work[:, 464:528].bitcast(BF16)}
        mask_b = work[:, 528:536].bitcast(BF16).rearrange("p (t e) -> p t e", t=TT)
        top = w(6032, 2)
        denom = w(6034, 2)
        rdenom = w(6036, 2)
        rank_in = w(6040, 16).rearrange("p (t e) -> p t e", t=TT)
        over = w(6056, 8)
        cum_over = w(6064, 8)
        pairs = w(544, 128)
        pairs2 = w(672, 128)
        chosen = w(376, 24).rearrange("p (j e) -> p j e", j=3)
        picked = w(256, 48).rearrange("p (t j e) -> p t j e", t=TT, j=3)
        picked_gate = w(304, 48).rearrange("p (t j e) -> p t j e", t=TT, j=3)
        picked_expert = w(352, 24).rearrange("p (j e) -> p j e", j=3)

        spare = w(work.shape[1] - len(SPARE_ITEMS) * UNIT, len(SPARE_ITEMS) * UNIT).rearrange("p (u n) -> p u n", n=UNIT)

        raw_loaded = [sem(f"raw_loaded{s}") for s in range(RAW_SLOTS)]
        w_hi_ready, w_lo_ready, w_used = sem("w_hi_ready"), sem("w_lo_ready"), sem("w_used")
        spare_loaded = sem("spare_loaded")
        w_lo_by_pool = sem("w_lo_by_pool")
        first_loaded, consts_loaded, x_loaded, pos_loaded = sem("first_loaded"), sem("consts_loaded"), [sem(f"x_loaded{t}") for t in range(TT)], sem("pos_loaded")
        rows_loaded, lam_loaded, pool_loaded = sem("rows_loaded"), sem("lam_loaded"), sem("pool_loaded")
        router_loaded, ln_loaded, stored = sem("router_loaded"), sem("ln_loaded"), sem("stored")
        cols_psum, cols_ready = sem("cols_psum"), sem("cols_ready")
        pads_zeroed = sem("pads_zeroed")
        lam_summed, lam_exped = sem("lam_summed"), sem("lam_exped")
        angles_ready, sines_ready, rope_ready = sem("angles_ready"), sem("sines_ready"), sem("rope_ready")
        xt_psum, xt_hi, xt_lo = sem("xt_psum"), sem("xt_hi"), sem("xt_lo")
        z_ready = sem("z_ready")
        rot_psum, rope_scaled, roped = sem("rot_psum"), sem("rope_scaled"), sem("roped")
        conf_conv, conf_mean, conf_sq, conf_var = sem("conf_conv"), sem("conf_mean"), sem("conf_sq"), sem("conf_var")
        conf_std, conf_normed, conf_y = sem("conf_std"), sem("conf_normed"), sem("conf_y")
        pool_diff, pool_psum, pool_y, sconv_y = sem("pool_diff"), sem("pool_psum"), sem("pool_y"), sem("sconv_y")
        tables_ready, scores_psum, scores_max, probs_ready = sem("tables_ready"), sem("scores_psum"), sem("scores_max"), sem("probs_ready")
        mixed, aT_psum, aT_ready = sem("mixed"), sem("aT_psum"), sem("aT_ready")
        o_psum, o_ms, o_rstd = sem("o_psum"), sem("o_ms"), sem("o_rstd")
        o_normed, oT_psum, o_y = sem("o_normed"), sem("oT_psum"), sem("o_y")
        y_hi, y_lo, wo_psum = sem("y_hi"), sem("y_lo"), sem("wo_psum")
        ln_var, ln_rstd, x_ready = sem("ln_var"), sem("ln_rstd"), sem("x_ready")
        g_act, h_ready = sem("g_act"), sem("h_ready")
        h_hi_ready, h_lo_ready, ffn_psum = sem("h_hi_ready"), sem("h_lo_ready"), sem("ffn_psum")
        router_split, logitsT_ready, logits_psum, logits_off, logits_exp = sem("router_split"), sem("logitsT_ready"), sem("logits_psum"), sem("logits_off"), sem("logits_exp")
        mask_ready, ranks_psum, routed = sem("mask_ready"), sem("ranks_psum"), sem("routed")
        hot_ready, gather_psum, item_hi, item_lo = sem("hot_ready"), sem("gather_psum"), sem("item_hi"), sem("item_lo")
        gated_ready, gT_psum, gT_ready = sem("gated_ready"), sem("gT_psum"), sem("gT_ready")
        mg_act, mh_ready = sem("mg_act"), sem("mh_ready")
        mhT_psum, mh_hi, mh_lo, my_ready = sem("mhT_psum"), sem("mh_hi"), sem("mh_lo"), sem("my_ready")
        comb_psum, acc_ready = sem("comb_psum"), sem("acc_ready")
        dve_step, pool_step = sem("dve_step"), sem("pool_step")

        def z_src(l, g):
            return w_in[l].rearrange("(k p) n -> p k n", p=P)[:, :, g * GW:(g + 1) * GW]

        def wo_src(l, pair):
            return w_o[l].rearrange("(k p) n -> p k n", p=P)[:, 2 * pair:2 * pair + 2, :]

        def dense_src(kind, j):
            if kind == "d":
                return ffn_wd[0].rearrange("(k p) n -> p k n", p=P)[:, 2 * j:2 * j + 2, :]
            m = ffn_wg if kind == "g" else ffn_wu
            return m[0].rearrange("(k p) n -> p k n", p=P)[:, :, j * GW:(j + 1) * GW]

        def moe_src(e, kind, ch, part_):
            if kind == "d":
                m = moe_wd[0, bass.ds(e, 1)].rearrange("a (k p) n -> p (a k) n", p=P)
                k0 = ch * (CW // P) + 2 * part_
                return m[:, k0:k0 + 2, :]
            m = moe_wg if kind == "g" else moe_wu
            m = m[0, bass.ds(e, 1)].rearrange("a (k p) n -> p (a k) n", p=P)
            return m[:, 4 * part_:4 * part_ + 4, ch * CW:(ch + 1) * CW]

        def tiles(slot, k):
            return slot.rearrange("p (k n) -> p k n", k=k)

        def split_pair(n, k):
            s = n % SPLIT_SLOTS
            return tiles(w_hi[:, s, :], k), tiles(w_lo[:, s, :], k)

        FIRST_UNITS = []
        for l in range(DEPTH):
            FIRST_UNITS += [(z_src(l, g), KT) for g in Z_ORDER]
            FIRST_UNITS += [(wo_src(l, pair), 2) for pair in WO_ORDER]
            if l == 0:
                FIRST_UNITS += [(dense_src(kind, j), 2 if kind == "d" else KT) for kind, j in DENSE_ORDER]
        assert len(FIRST_UNITS) == MOE_UNIT

        def wait_lo(engine, n):
            by_dve, by_pool = lo_counts(n)
            engine.wait_ge(w_lo_ready, by_dve)
            if by_pool:
                engine.wait_ge(w_lo_by_pool, by_pool)

        block = ctx.enter_context(nc.Block())

        @block.sync
        def _(sp):
            def load_small():
                sp.dma_start(cst[:, first:], consts[:, first:]).then_inc(consts_loaded, 16)
                sp.dma_start(rows[R_DW:R_DW + 62], conf_dw.rearrange("l j (h c) -> (j h) l c", h=2)).then_inc(rows_loaded, 16)
                sp.dma_start(rows[R_SW:R_SW + 6], sconv_w.rearrange("l j (h c) -> (j h) l c", h=2)).then_inc(rows_loaded, 16)
                for r, m in ((R_PS, pool_scale), (R_LG, conf_ln_g), (R_LB, conf_ln_b)):
                    sp.dma_start(rows[r:r + 2], m.rearrange("l (h c) -> h l c", h=2)).then_inc(rows_loaded, 16)
                for b in range(2):
                    sp.dma_start(rows[R_SG:R_SG + 1, :, 64 * b:64 * b + 64], diff_subln_g.rearrange("(a l) n -> a l n", a=1)).then_inc(rows_loaded, 16)
                sp.dma_start(a_mix[:, 0:DEPTH * 128], diff_lambda.rearrange("l a n -> (l a n)").partition_broadcast(P)).then_inc(lam_loaded, 16)
                sp.dma_start(router_raw[:], router_w[0].rearrange("(k p) e -> p k e", p=P)).then_inc(router_loaded, 16)

            first = CONST_AT["first"][1]
            sp.dma_start(cst[:, 0:first], consts[:, 0:first]).then_inc(first_loaded, 16)
            for n, (src, k) in enumerate(FIRST_UNITS):
                if n == 1:
                    for t in range(TT):
                        sp.dma_start(xs[:, t, :], x[0, t * P:(t + 1) * P, :]).then_inc(x_loaded[t], 16)
                if n == SPLIT_SLOTS:
                    load_small()
                if n >= RAW_SLOTS:
                    wait_lo(sp, n - RAW_SLOTS)
                sp.dma_start(tiles(raw[:, n % RAW_SLOTS, :], k), src).then_inc(raw_loaded[n % RAW_SLOTS], 16)

            def load_item(e, item, count=NU, skip=None):
                for i, (kind, ch, half) in enumerate(MOE_ORDER[:count]):
                    if item is None and i == RAW_SLOTS:
                        sp.wait_ge(y_lo, DEPTH * NWO)
                        k = 2 if MOE_ORDER[SPARE_POS][0] == "d" else 4
                        for j, expert in enumerate(SPARE_ITEMS):
                            sp.dma_start(tiles(spare[:, j, :], k), moe_src(expert, *MOE_ORDER[SPARE_POS])).then_inc(spare_loaded, 16)
                    if i == skip:
                        continue
                    n = MOE_UNIT + i
                    back = i + 1 - RAW_SLOTS
                    if item is None:
                        if back <= 0:
                            wait_lo(sp, MOE_UNIT + back - 1)
                        else:
                            sp.wait_ge(w_lo_ready, LO_BASE + PARTS * back)
                    else:
                        sp.wait_ge(w_lo_ready, item * (PARTS * NU) + (LO_BASE + PARTS * back))
                    sp.dma_start(tiles(raw[:, n % RAW_SLOTS, :], 2 if kind == "d" else 4),
                                 moe_src(e, kind, ch, half)).then_inc(raw_loaded[n % RAW_SLOTS], 16)

            load_item(0, None)
            sp.wait_ge(routed, 1)
            items = sp.value_load(item_int[0:1, 12:13], min_val=NE, max_val=MAX_ITEMS)
            with sp.Fori(1, SPARE_ITEMS[0]) as item:
                load_item(item, item)
            with sp.Fori(SPARE_ITEMS[0], SPARE_ITEMS[-1] + 1) as item:
                load_item(item, item, skip=SPARE_POS)
            with sp.Fori(SPARE_ITEMS[-1] + 1, items) as item:
                e = sp.value_load(item_int[0:1, bass.ds(item, 1)], min_val=0, max_val=NE - 1)
                load_item(e, item)
            load_item(0, items, AHEAD)
            for t in range(TT):
                for h in range(2):
                    sp.wait_ge(x_ready, 3 * XQ + 2 * t + h + 1)
                    half = slice(512 * h, 512 * h + 512)
                    sp.dma_start(out[0, t * P:(t + 1) * P, half], xs[:, t, half]).then_inc(stored, 16)
            sp.wait_ge(stored, 16 * XQ)

        @block.gpsimd
        def _(pool):
            steps = [0]

            def step(ins):
                steps[0] += 1
                ins.then_inc(pool_step, 1)
                pool.wait_ge(pool_step, steps[0])

            nc.gpsimd.memset(conf_u[:, :, 0:CPAD], 0.0).then_inc(pads_zeroed, 1)
            nc.gpsimd.memset(pool_h[:, :, 0:PPAD], 0.0).then_inc(pads_zeroed, 1)
            nc.gpsimd.memset(sconv_u[:, :, 0:SPAD], 0.0).then_inc(pads_zeroed, 1)
            step(nc.gpsimd.memset(pool_mat[:], 0.0))
            for l in range(DEPTH):
                for h in range(2):
                    for b in range(2):
                        pool.dma_start(pool_mat[64 * b:64 * b + 64, l, h, 64 * b:64 * b + 64],
                                       pool_w[l, 2 * h + b]).then_inc(pool_loaded, 16)

            def short_window(l):
                pool.wait_ge(z_ready, NZ * l + Z_ORDER.index(SH_G) + 1)
                step(nc.gpsimd.tensor_tensor(sconv_u[:, :, SPAD:], z[SCG_G], z[SH_G], ALU.mult))
                for h in range(2):
                    for j in range(SCONV_K):
                        to = s_acc if j == 0 else s_tmp
                        tap = cols[:, l, R_SW + 2 * j + h:R_SW + 2 * j + h + 1]
                        step(nc.gpsimd.tensor_scalar(to[:, h, :], sconv_u[:, h, j:j + SEQ], tap, None, ALU.mult))
                        if j:
                            step(nc.gpsimd.tensor_tensor(s_acc[:, h, :], s_acc[:, h, :], s_tmp[:, h, :], ALU.add))
                pool.wait_ge(z_ready, NZ * l + Z_ORDER.index(SB_G) + 1)
                nc.gpsimd.tensor_tensor(y32[:, 2:4, :], s_acc, z[SB_G], ALU.mult).then_inc(sconv_y, 1)

            def window_sums(l):
                pool.wait_ge(z_ready, NZ * l + Z_ORDER.index(POOL_G) + 1)
                src, first = pool_h, 1
                for n, width in enumerate(WINDOWS):
                    dst = pool_s[n % 2]
                    step(nc.gpsimd.tensor_tensor(dst[:, :, first:], src[:, :, first:],
                                                 src[:, :, first - width // 2:SEQ + PPAD - width // 2], ALU.add))
                    h, lo = n // 2, 64 * (n % 2)
                    step(nc.gpsimd.tensor_tensor(y32[lo:lo + 64, h, :], dst[lo:lo + 64, h, PPAD:],
                                                 c("rcount")[lo:lo + 64, h * SEQ:(h + 1) * SEQ], ALU.mult))
                    src, first = dst, first + width
                nc.gpsimd.tensor_tensor(y32[:, 0:2, :], y32[:, 0:2, :], pool_h[:, :, PPAD:], ALU.subtract).then_inc(pool_diff, 1)

            def inverse_roots(n):
                for t in range(TT):
                    pool.wait_ge(ln_var, TT * n + t + 1)
                    step(nc.gpsimd.tensor_scalar(rstd[:, t:t + 1], mean_var[:, t, 1:2], EPS, None, ALU.add))
                    nc.gpsimd.tensor_tensor(rstd[:, t:t + 1], rstd[:, t:t + 1], c("minus_half")[:, 0:1], ALU.pow).then_inc(ln_rstd, 1)

            def lo_of_unit(n):
                pool.wait_ge(w_hi_ready, n + 1)
                s = n % SPLIT_SLOTS
                nc.gpsimd.tensor_tensor(w_lo[:, s, :], raw[:, n % RAW_SLOTS, :], w_hi[:, s, :].bitcast(F32),
                                        ALU.subtract).then_inc(w_lo_by_pool, 1)

            for l in range(DEPTH):
                for n, g in enumerate((Q_G, K_G)):
                    if n == 1:
                        lo_of_unit(Z_UNIT[l] + 5)
                    pool.wait_ge(z_ready, NZ * l + Z_ORDER.index(g) + 1)
                    cos = rope_cs[:, 1:2, :].broadcast_to((P, 2, SEQ))
                    if l == 0 and n == 0:
                        pool.wait_ge(rope_ready, 1)
                        pool.wait_ge(cols_ready, DEPTH)
                    nc.gpsimd.tensor_tensor(rope_qc[:, n], z[g], cos, ALU.mult).then_inc(rope_scaled, 1)
                lo_of_unit(Z_UNIT[l] + 7)
                short_window(l)
                window_sums(l)
                pool.wait_ge(o_ms, l + 1)
                minus_half = c("minus_half").rearrange("p (a h) -> p a h", a=1).broadcast_to((P, TT, HEADS))
                nc.gpsimd.tensor_tensor(head_ms[:], head_ms[:], minus_half, ALU.pow).then_inc(o_rstd, 1)
                lo_of_unit(Z_UNIT[l] + NZ + NWO - 1)
                inverse_roots(2 * l)
                if l == DEPTH - 1:
                    pool.wait_ge(x_ready, XQ * 3)
                    nc.gpsimd.tensor_scalar(acc, xs[:], ALPHA, None, ALU.mult).then_inc(acc_ready, 1)
                if l == DEPTH - 1:
                    pool.wait_ge(spare_loaded, 16 * len(SPARE_ITEMS))
                    slot = (MOE_UNIT + SPARE_POS) % RAW_SLOTS
                    for j, item in enumerate(SPARE_ITEMS):
                        pool.wait_ge(w_lo_ready, LO_BASE + PARTS * (item * NU + SPARE_POS + 1 - RAW_SLOTS))
                        nc.gpsimd.tensor_copy(raw[:, slot, :], spare[:, j, :]).then_inc(raw_loaded[slot], 16)
                inverse_roots(2 * l + 1)

        @block.scalar
        def _(act):
            act.dma_start(pos_int, positions[0].partition_broadcast(P)).then_inc(pos_loaded, 16)

            units = [0]

            def hi_of_unit(count=1):
                for _ in range(count):
                    n = units[0]
                    units[0] += 1
                    act.wait_ge(raw_loaded[n % RAW_SLOTS], 16 * (n // RAW_SLOTS + 1))
                    if n >= SPLIT_SLOTS:
                        act.wait_ge(w_used, n - SPLIT_SLOTS + 1)
                    nc.scalar.activation(w_hi[:, n % SPLIT_SLOTS, :], raw[:, n % RAW_SLOTS, :], ACT.Copy).then_inc(w_hi_ready, 1)

            def hi_of_moe(unit, item):
                n = MOE_UNIT + MOE_POS[unit]
                ahead = 0 if item is None else item * (16 * NU // RAW_SLOTS)
                act.wait_ge(raw_loaded[n % RAW_SLOTS], ahead + 16 * (n // RAW_SLOTS + 1))
                for s in range(PARTS):
                    if item is None:
                        act.wait_ge(w_used, n - SPLIT_SLOTS + 1)
                    else:
                        act.wait_ge(w_used, item * (PARTS * NU) + (MOE_UNIT + PARTS * (n - MOE_UNIT - SPLIT_SLOTS) + s + 1))
                    part = slice(s * PART, (s + 1) * PART)
                    nc.scalar.activation(w_hi[:, n % SPLIT_SLOTS, part], raw[:, n % RAW_SLOTS, part], ACT.Copy).then_inc(w_hi_ready, 1)

            def load_ln(n):
                if n:
                    act.wait_ge(x_ready, XQ * n)
                g, b = ((ln1_g, ln1_b), (ln2_g, ln2_b))[n % 2]
                for j, m in enumerate((g, b)):
                    act.dma_start(ln_gb[:, j, :], m[n // 2].partition_broadcast(P)).then_inc(ln_loaded, 16)

            def hi_of_x(n):
                for q in range(4):
                    t, k = q // 2, 4 * (q % 2)
                    act.wait_ge(xt_psum, 4 * n + q + 1)
                    nc.scalar.activation(a_hi[:, k:k + 4, t * P:(t + 1) * P], tiles(bank[q][:], 4), ACT.Copy).then_inc(xt_hi, 1)

            def z_out(l, i):
                g = Z_ORDER[i]
                act.wait_ge(w_used, Z_UNIT[l] + i + 1)
                to = pool_h[:, :, PPAD:] if g == POOL_G else z[g]
                nc.scalar.activation(to, tiles(bank[Z_BANKS[i % 3]][:], 2), ACT.Sigmoid if g == CG_G else ACT.Copy).then_inc(z_ready, 1)

            def probs(l, q):
                width = P * (q + 1)
                act.wait_ge(scores_max, 2 * l + q + 1)
                if l or q:
                    act.wait_ge(mixed, 2 * l + q)
                view = sc[:, 0:MAPS * width].rearrange("p (m k) -> p m k", m=MAPS)
                for m in range(MAPS):
                    nc.scalar.activation(view[:, m, :], bank[m % 4][:, (m // 4) * width:(m // 4 + 1) * width], ACT.Exp,
                                         bias=row_max[:, q, m:m + 1], scale=SCALE,
                                         accum_out=row_sum[:, q, m:m + 1]).then_inc(probs_ready, 1)

            def aT_out(l, q):
                for n, b in enumerate(([7], [0, 1])[q]):
                    act.wait_ge(aT_psum, 3 * l + q + n + 1)
                    nc.scalar.activation(aT[q][:, 512 * n:512 * n + 512], bank[b][:], ACT.Copy).then_inc(aT_ready, 1)

            def hi_of_y(l, n):
                pair = WO_ORDER[n]
                act.wait_ge((pool_y, sconv_y, o_y, conf_y)[pair], l + 1)
                act.wait_ge(w_used, WO_UNIT[l])
                nc.scalar.activation(a_hi[:, 2 * pair:2 * pair + 2, :], y32[:, 2 * pair:2 * pair + 2, :], ACT.Copy).then_inc(y_hi, 1)

            for l in range(DEPTH):
                if l == 0:
                    hi_of_unit(1)
                    hi_of_x(0)
                    hi_of_unit(2)
                else:
                    hi_of_x(2)
                    load_ln(2)
                    hi_of_unit(1)
                for i in range(NZ):
                    z_out(l, i)
                    hi_of_unit(1)
                    if l == 0 and i == 0:
                        act.wait_ge(angles_ready, 1)
                        nc.scalar.activation(rope_cs[:], trig, ACT.Sin).then_inc(sines_ready, 1)
                        load_ln(0)
                    if l == 0 and i == 1:
                        for k in range(DEPTH):
                            act.wait_ge(cols_psum, k + 1)
                            nc.scalar.activation(cols[:, k, :], bank[2 + k][:, 0:NR], ACT.Copy).then_inc(cols_ready, 1)
                        act.wait_ge(lam_summed, 1)
                        nc.scalar.activation(lam_exp.rearrange("p l n -> p (l n)"), lam_sum, ACT.Exp).then_inc(lam_exped, 1)
                        act.wait_ge(router_loaded, 16)
                        nc.scalar.activation(router_hi[:], router_raw[:], ACT.Copy).then_inc(router_split, 1)
                    if i == 5:
                        probs(l, 0)
                    if i == 6:
                        probs(l, 1)
                    if i == 7:
                        aT_out(l, 0)
                aT_out(l, 1)
                hi_of_y(l, 0)
                hi_of_y(l, 1)
                hi_of_unit(1)
                hi_of_y(l, 2)
                act.wait_ge(conf_var, l + 1)
                nc.scalar.activation(xsq[:, 0, :], bank[1][:, 256:512], ACT.Sqrt, bias=c("eps")).then_inc(conf_std, 1)
                act.wait_ge(conf_normed, l + 1)
                for h in range(2):
                    last = nc.scalar.activation(y32[:, 6 + h, :], xc[:, h, :], ACT.Silu, bias=cols[:, l, R_LB + h:R_LB + h + 1],
                                                scale=cols[:, l, R_LG + h:R_LG + h + 1])
                last.then_inc(conf_y, 1)
                hi_of_y(l, 3)
                if l == 0:
                    hi_of_unit(2)
                else:
                    hi_of_moe(MOE_ORDER[0], None)
                    hi_of_moe(MOE_ORDER[1], None)
                hi_of_x(2 * l + 1)
                load_ln(2 * l + 1)
                if l == 0:
                    hi_of_unit(1)
                    for j in range(FP + 1):
                        if 0 < j < FP:
                            hi_of_unit(1)
                        if j:
                            act.wait_ge(h_ready, j)
                            nc.scalar.activation(h_hi[:, (j - 1) % 2, :], d_h[:, (j - 1) % 2, :], ACT.Copy).then_inc(h_hi_ready, 1)
                        if 0 < j < FP:
                            hi_of_unit(1)
                        if j < FP:
                            act.wait_ge(w_used, dense_unit("g", j) + 1)
                            nc.scalar.activation(d_act[:, j % 2, :], bank[2 * (j % 2)][:], ACT.Silu).then_inc(g_act, 1)
                        if 0 < j < FP:
                            hi_of_unit(1)
                    hi_of_unit(2)
            assert units[0] == MOE_UNIT, (units, MOE_UNIT)

            act.wait_ge(logits_off, 1)
            nc.scalar.activation(expl, expl, ACT.Exp).then_inc(logits_exp, 1)

            def hi_of_item(before):
                for h, b in enumerate((1, 3)):
                    act.wait_ge(gather_psum, before * 2 + (h + 1))
                    nc.scalar.activation(a_hi[:, 4 * h:4 * h + 4, 0:P], tiles(bank[b][:], 4), ACT.Copy).then_inc(item_hi, 1)

            def y_out(before):
                act.wait_ge(w_used, before * (PARTS * NU) + MOE_UNIT)
                for h in range(2):
                    nc.scalar.activation(y_sb[:, 512 * h:512 * h + 512], bank[5 + h][:], ACT.Copy).then_inc(my_ready, 1)

            y_out(0)
            hi_of_moe(MOE_ORDER[2], None)
            hi_of_item(0)
            act.wait_ge(routed, 1)
            items = act.value_load(item_int[0:1, 12:13], min_val=NE, max_val=MAX_ITEMS)
            with act.Fori(0, items) as item:
                for ch in range(NC + 1):
                    if ch < NC:
                        if ch:
                            hi_of_moe(("g", ch, 0), item)
                            hi_of_moe(("g", ch, 1), item)
                            hi_of_moe(("u", ch, 0), item)
                        hi_of_moe(("u", ch, 1), item)
                    else:
                        hi_of_moe(("d", ch - 1, 0), item)
                    if ch:
                        act.wait_ge(mhT_psum, item * NC + ch)
                        nc.scalar.activation(h_hi[:, 0, :], bank[4][:], ACT.Copy).then_inc(mh_hi, 1)
                    if ch == NC:
                        hi_of_moe(("d", ch - 1, 1), item)
                    if ch < NC:
                        act.wait_ge(w_used, item * (PARTS * NU) + (MOE_UNIT + PARTS * (MOE_POS["g", ch, 1] + 1)))
                        nc.scalar.activation(m_act[:, ch % 2, :], bank[ch % 2][:], ACT.Silu).then_inc(mg_act, 1)
                    if ch == 3:
                        act.wait_ge(gT_psum, item + 1)
                        nc.scalar.activation(gatedT, bank[7][:, 0:256], ACT.Copy).then_inc(gT_ready, 1)
                    if 0 < ch < NC:
                        hi_of_moe(("d", ch - 1, 0), item)
                        hi_of_moe(("d", ch - 1, 1), item)
                hi_of_moe(MOE_ORDER[0], item + 1)
                hi_of_item(item + 1)
                hi_of_moe(MOE_ORDER[1], item + 1)
                y_out(item + 1)
                hi_of_moe(MOE_ORDER[2], item + 1)

        @block.vector
        def _(dve):
            steps, units = [0], [0]
            ident = c("ident")

            def step(ins):
                steps[0] += 1
                ins.then_inc(dve_step, 1)
                dve.wait_ge(dve_step, steps[0])

            def lo_of_unit(count=1):
                for _ in range(count):
                    n = units[0]
                    units[0] += 1
                    if n in POOL_UNITS:
                        continue
                    dve.wait_ge(w_hi_ready, n + 1)
                    s = n % SPLIT_SLOTS
                    nc.vector.tensor_tensor(w_lo[:, s, :], raw[:, n % RAW_SLOTS, :], w_hi[:, s, :].bitcast(F32),
                                            ALU.subtract).then_inc(w_lo_ready, 1)

            def lo_of_moe(unit, item):
                n = MOE_UNIT + MOE_POS[unit]
                slot = n % SPLIT_SLOTS
                ahead = 0 if item is None else item * (PARTS * NU)
                for s in range(PARTS):
                    dve.wait_ge(w_hi_ready, ahead + (MOE_UNIT + PARTS * MOE_POS[unit] + s + 1))
                    part = slice(s * PART, (s + 1) * PART)
                    nc.vector.tensor_tensor(w_lo[:, slot, part], raw[:, n % RAW_SLOTS, part], w_hi[:, slot, part].bitcast(F32),
                                            ALU.subtract).then_inc(w_lo_ready, 1)

            def lo_of_x(n):
                for q in range(4):
                    t, k = q // 2, 4 * (q % 2)
                    dve.wait_ge(xt_hi, 4 * n + q + 1)
                    at = (slice(None), slice(k, k + 4), slice(t * P, (t + 1) * P))
                    nc.vector.tensor_tensor(a_lo[at], tiles(bank[q][:], 4), a_hi[at].bitcast(F32), ALU.subtract).then_inc(xt_lo, 1)

            def lo_of_y(l, n):
                pair = WO_ORDER[n]
                dve.wait_ge(y_hi, NWO * l + n + 1)
                at = (slice(None), slice(2 * pair, 2 * pair + 2))
                nc.vector.tensor_tensor(a_lo[at], y32[at], a_hi[at].bitcast(F32), ALU.subtract).then_inc(y_lo, 1)

            def layer_norm(n, ready, source):
                dve.wait_ge(ln_loaded, 32 * (n + 1))
                for t in range(TT):
                    ready(t)
                    for h in range(2):
                        ins = nc.vector.bn_stats(stats[:, t, h, :], source(t, h))
                    step(ins)
                    nc.vector.bn_aggr(mean_var[:, t, :], stats[:, t].rearrange("p h n -> p (h n)")).then_inc(ln_var, 1)
                    dve.wait_ge(ln_var, TT * n + t + 1)
                    for h in range(2):
                        half = slice(512 * h, 512 * h + 512)
                        ins = nc.vector.scalar_tensor_tensor(xs[:, t, half], source(t, h), mean_var[:, t, 0:1], ln_gb[:, 0, half],
                                                             ALU.subtract, ALU.mult)
                    step(ins)
                    dve.wait_ge(ln_rstd, TT * n + t + 1)
                    for h in range(2):
                        half = slice(512 * h, 512 * h + 512)
                        nc.vector.scalar_tensor_tensor(xs[:, t, half], xs[:, t, half], rstd[:, t:t + 1], ln_gb[:, 1, half],
                                                       ALU.mult, ALU.add).then_inc(x_ready, 1)

            taps = [(h, j) for j in range(CONF_K) for h in range(2)]
            tap_at = [0]

            def conv_taps(l, count):
                for _ in range(count):
                    h, j = taps[tap_at[0] % len(taps)]
                    tap_at[0] += 1
                    tap = cols[:, l, R_DW + 2 * j + h:R_DW + 2 * j + h + 1]
                    window = conf_u[:, h, j:j + SEQ]
                    if j == 0:
                        ins = nc.vector.tensor_scalar(conf_acc[:, h, :], window, tap, None, ALU.mult)
                    else:
                        dve.wait_ge(conf_conv, tap_at[0] - 2)
                        ins = nc.vector.scalar_tensor_tensor(conf_acc[:, h, :], window, tap, conf_acc[:, h, :], ALU.mult, ALU.add)
                    ins.then_inc(conf_conv, 1)

            def rope(l, n):
                dve.wait_ge(rot_psum, 2 * l + n + 1)
                if l == 0 and n == 0:
                    dve.wait_ge(rope_ready, 1)
                sin = rope_cs[:, 0:1, :].broadcast_to((P, 2, SEQ))
                step(nc.vector.tensor_tensor(rope_rs[:, n], tiles(bank[n][:], 2), sin, ALU.mult))
                dve.wait_ge(rope_scaled, 2 * l + n + 1)
                nc.vector.tensor_tensor(z[(Q_G, K_G)[n]], rope_rs[:, n], rope_qc[:, n], ALU.add).then_inc(roped, 1)

            def score_rows(l, q):
                width = P * (q + 1)
                maxima = row_max[:, q, :].rearrange("p (t j) -> p t j", t=2)
                dve.wait_ge(scores_psum, 2 * l + q + 1)
                for j in range(4):
                    ins = nc.vector.tensor_reduce(maxima[:, :, j], bank[j][:, 0:2 * width].rearrange("p (t k) -> p t k", t=2),
                                                  AX_X, ALU.max)
                step(ins)
                nc.vector.tensor_scalar(row_max[:, q, :], row_max[:, q, :], -SCALE, None, ALU.mult).then_inc(scores_max, 1)

            def mix_maps(l, q):
                width = P * (q + 1)
                maps = sc[:, 0:MAPS * width].rearrange("p (m k) -> p m k", m=MAPS)
                dve.wait_ge(probs_ready, MAPS * (2 * l + q + 1))
                step(nc.vector.reciprocal(row_inv[:, q, :], row_sum[:, q, :]))
                second = row_inv[:, q, :].rearrange("p (h m) -> p h m", m=2)[:, :, 1]
                first_sum = row_sum[:, q, :].rearrange("p (h m) -> p h m", m=2)[:, :, 0]
                step(nc.vector.scalar_tensor_tensor(second, second, neg_lam[:, l:l + 1], first_sum, ALU.mult, ALU.mult))
                if q:
                    dve.wait_ge(aT_psum, 3 * l + 1)
                for hd in range(HEADS):
                    m = 2 * hd
                    ins = nc.vector.scalar_tensor_tensor(a_mix[:, hd * width:(hd + 1) * width], maps[:, m + 1, :],
                                                         row_inv[:, q, m + 1:m + 2], maps[:, m, :], ALU.mult, ALU.add)
                ins.then_inc(mixed, 1)

            for l in range(DEPTH):
                if l == 0:
                    lo_of_unit(1)
                    lo_of_x(0)
                    lo_of_unit(1)
                    dve.wait_ge(first_loaded, 16)
                    dve.wait_ge(pos_loaded, 16)
                    step(nc.vector.tensor_copy(angle, pos_int))
                    step(nc.vector.tensor_scalar(angle, angle, c("inv"), None, ALU.mult))
                    for h in range(2):
                        ins = nc.vector.tensor_scalar(turns[:, h, :], angle, 1.0 / TWO_PI, 0.25 * h, ALU.mult, ALU.add)
                    step(ins)
                    step(nc.vector.tensor_scalar(turns, turns, MAGIC, -MAGIC, ALU.add, ALU.add))
                    for j, piece in enumerate(TURN):
                        source = angle.rearrange("p (a t) -> p a t", a=1).broadcast_to((P, 2, SEQ)) if j == 0 else trig
                        step(nc.vector.scalar_tensor_tensor(trig, turns, -piece, source, ALU.mult, ALU.add))
                    step(nc.vector.tensor_scalar(trig[:, 1, :], trig[:, 1, :], 0.5 * np.pi, None, ALU.add))
                    nc.vector.tensor_scalar(trig, trig, PI_IN, -PI_IN, ALU.min, ALU.max).then_inc(angles_ready, 1)
                    lo_of_unit(1)
                else:
                    lo_of_x(2)
                    lo_of_unit(2)
                for i in range(NZ):
                    if l == 0 and i == 1:
                        lo_of_unit(1)
                        dve.wait_ge(lam_exped, 1)
                        step(nc.vector.tensor_tensor(neg_lam[:], lam_exp[:, :, 1], lam_exp[:, :, 0], ALU.subtract))
                        for k in range(DEPTH):
                            ins = nc.vector.tensor_scalar(neg_lam[:, k:k + 1], neg_lam[:, k:k + 1], -LAM_INIT[k], None, ALU.add)
                        step(ins)
                        dve.wait_ge(cols_ready, DEPTH)
                        for k in range(DEPTH):
                            ins = nc.vector.tensor_scalar(cols[:, k, R_SG:R_SG + 1], cols[:, k, R_SG:R_SG + 1], 1.0 - LAM_INIT[k],
                                                          None, ALU.mult)
                        step(ins)
                        dve.wait_ge(router_split, 1)
                        nc.vector.tensor_tensor(router_lo[:], router_raw[:], router_hi[:].bitcast(F32),
                                                ALU.subtract).then_inc(router_split, 1)
                        dve.wait_ge(pads_zeroed, 3)
                    if i == 1:
                        dve.wait_ge(z_ready, NZ * l + 2)
                        step(nc.vector.tensor_tensor(conf_u[:, :, CPAD:], z[CA_G], z[CG_G], ALU.mult))
                    if i == 3:
                        rope(l, 0)
                    if i == 4:
                        rope(l, 1)
                    if i == 5:
                        score_rows(l, 0)
                    if i == 6:
                        mix_maps(l, 0)
                    if i == 7:
                        mix_maps(l, 1)
                    if not (l == 0 and i == 1):
                        lo_of_unit(1)
                    if i == 6:
                        score_rows(l, 1)
                    if l == 0 and i == 0:
                        dve.wait_ge(sines_ready, 1)
                        nc.vector.tensor_scalar(rope_cs[:, 1, :], rope_cs[:, 1, :], c("roped"), c("unroped"), ALU.mult,
                                                ALU.add).then_inc(rope_ready, 1)
                        dve.wait_ge(consts_loaded, 16)
                        nc.vector.tensor_copy(ident_b[:], ident)
                        nc.vector.tensor_copy(causal_b[:], c("causal")).then_inc(tables_ready, 1)
                        dve.wait_ge(lam_loaded, 16)
                        step(nc.vector.tensor_tensor(lam_prod, lam_in[:, :, 0, :], lam_in[:, :, 1, :], ALU.mult))
                        nc.vector.tensor_reduce(lam_sum, lam_prod, AX_X, ALU.add).then_inc(lam_summed, 1)
                    conv_taps(l, (0, 6, 7, 3, 15, 4, 10, 0, 0)[i])
                lo_of_y(l, 0)
                conv_taps(l, 2)
                dve.wait_ge(o_psum, l + 1)
                first_inv = row_inv.rearrange("p q (h m) -> p q h m", m=2)[:, :, :, 0:1].broadcast_to((P, TT, HEADS, VD))
                step(nc.vector.tensor_tensor(o_sb, bank[2].rearrange("p (q h e) -> p q h e", q=TT, h=HEADS), first_inv, ALU.mult))
                step(nc.vector.tensor_tensor(o_sq, o_sb, o_sb, ALU.mult))
                step(nc.vector.tensor_reduce(head_ms[:], o_sq, AX_X, ALU.add))
                nc.vector.tensor_scalar(head_ms[:], head_ms[:], 1.0 / VD, EPS, ALU.mult, ALU.add).then_inc(o_ms, 1)
                dve.wait_ge(pool_psum, l + 1)
                for h in range(2):
                    ins = nc.vector.tensor_scalar(y32[:, h, :], bank[3][:, 256 * h:256 * h + 256],
                                                  cols[:, l, R_PS + h:R_PS + h + 1], None, ALU.mult)
                ins.then_inc(pool_y, 1)
                conv_taps(l, 2)
                lo_of_y(l, 1)
                dve.wait_ge(o_rstd, l + 1)
                scale = head_ms.rearrange("p q (h a) -> p q h a", a=1).broadcast_to((P, TT, HEADS, VD))
                nc.vector.tensor_tensor(o_sq, o_sb, scale, ALU.mult).then_inc(o_normed, 1)
                conv_taps(l, len(taps) - 45 - 4)
                dve.wait_ge(oT_psum, l + 1)
                nc.vector.tensor_scalar(y32[:, 4:6, :], tiles(bank[0][:], 2), cols[:, l, R_SG:R_SG + 1], None, ALU.mult).then_inc(o_y, 1)
                dve.wait_ge(conf_mean, l + 1)
                mean = bank[1][:, 0:256].rearrange("p (a t) -> p a t", a=1).broadcast_to((P, 2, SEQ))
                step(nc.vector.tensor_tensor(xc, conf_acc, mean, ALU.subtract))
                nc.vector.tensor_tensor(xsq, xc, xc, ALU.mult).then_inc(conf_sq, 1)
                lo_of_unit(1)
                lo_of_y(l, 2)
                dve.wait_ge(conf_std, l + 1)
                step(nc.vector.reciprocal(xsq[:, 1, :], xsq[:, 0, :]))
                inv_std = xsq[:, 1:2, :].broadcast_to((P, 2, SEQ))
                nc.vector.tensor_tensor(xc, xc, inv_std, ALU.mult).then_inc(conf_normed, 1)
                lo_of_y(l, 3)
                if l == 0:
                    lo_of_unit(1)
                else:
                    lo_of_moe(MOE_ORDER[0], None)

                def mixers_ready(t):
                    if t == 0:
                        dve.wait_ge(wo_psum, l + 1)
                    else:
                        dve.wait_ge(w_used, WO_UNIT[l] + NWO)

                layer_norm(2 * l, mixers_ready, lambda t, h: bank[4 + 2 * t + h][:])
                lo_of_x(2 * l + 1)
                if l == 0:
                    lo_of_unit(2)
                    for j in range(1, FP + 1):
                        b = 2 * ((j - 1) % 2)
                        dve.wait_ge(g_act, j)
                        dve.wait_ge(w_used, dense_unit("u", j - 1) + 1)
                        nc.vector.tensor_tensor(d_h[:, (j - 1) % 2, :], d_act[:, (j - 1) % 2, :], bank[b + 1][:],
                                                ALU.mult).then_inc(h_ready, 1)
                        if j < FP:
                            lo_of_unit(1)
                        dve.wait_ge(h_hi_ready, j)
                        nc.vector.tensor_tensor(h_lo[:, (j - 1) % 2, :], d_h[:, (j - 1) % 2, :],
                                                h_hi[:, (j - 1) % 2, :].bitcast(F32), ALU.subtract).then_inc(h_lo_ready, 1)
                        if j < FP:
                            lo_of_unit(2)
                    lo_of_unit(1)

                    def dense_ready(t):
                        if t == 0:
                            dve.wait_ge(ffn_psum, 1)
                        else:
                            dve.wait_ge(w_used, Z_UNIT[1])

                    layer_norm(1, dense_ready, lambda t, h: bank[4 + 2 * t + h][:])
            assert units[0] == MOE_UNIT, (units, MOE_UNIT)

            def hot(column):
                for t in range(TT):
                    ins = nc.vector.tensor_scalar(one_hot[:, t, :], c("iota"), slot_of[:, t, column], None, ALU.is_equal)
                ins.then_inc(hot_ready, 1)

            nc.vector.memset(gatedT, 0.0).then_inc(gT_ready, 1)
            for table in ("tri", "ones"):
                nc.vector.tensor_copy(count_b[table], c(table))
            nc.vector.memset(bank[5][:], 0.0)
            nc.vector.memset(bank[6][:], 0.0)
            nc.vector.memset(slot_of[:], -1.0)
            nc.vector.memset(gate_of[:], 0.0)
            step(nc.vector.memset(item_tab[:], 0.0))
            step(nc.vector.tensor_copy(item_tab[:, 0:NE], c("experts")))
            dve.wait_ge(logits_psum, 1)
            nc.vector.tensor_copy(logitsT, bank[7][0:NE, 256:512]).then_inc(logitsT_ready, 1)
            dve.wait_ge(logits_psum, 2)
            step(nc.vector.tensor_copy(logits, tiles(bank[7][:, 0:16], 2)))
            above = pairs.rearrange("p (t e f) -> p t e f", t=TT, e=NE)
            level = pairs2.rearrange("p (t e f) -> p t e f", t=TT, e=NE)
            other = logits.rearrange("p t (a e) -> p t a e", a=1).broadcast_to((P, TT, NE, NE))
            own = logits.rearrange("p t (e a) -> p t e a", a=1).broadcast_to((P, TT, NE, NE))
            nc.vector.tensor_tensor(above, other, own, ALU.is_gt)
            step(nc.vector.tensor_tensor(level, other, own, ALU.is_equal))
            before = c("before").rearrange("p (a n) -> p a n", a=1).broadcast_to((P, TT, NE * NE))
            step(nc.vector.tensor_tensor(tiles(pairs2, TT), tiles(pairs2, TT), before, ALU.mult))
            step(nc.vector.tensor_tensor(pairs, pairs, pairs2, ALU.add))
            step(nc.vector.tensor_reduce(rank, above, AX_X, ALU.add))
            nc.vector.tensor_scalar(mask_b, rank, 1.5, None, ALU.is_lt).then_inc(mask_ready, 1)
            nc.vector.tensor_scalar(mask, rank, 1.5, None, ALU.is_lt).then_inc(mask_ready, 1)
            step(nc.vector.tensor_reduce(top, logits, AX_X, ALU.max))

            def over_experts(v):
                return v.rearrange("p (t a) -> p t a", a=1).broadcast_to((P, TT, NE))

            nc.vector.tensor_tensor(expl, logits, over_experts(top), ALU.subtract).then_inc(logits_off, 1)
            dve.wait_ge(mask_ready, 2)
            dve.wait_ge(ranks_psum, 1)
            step(nc.vector.tensor_tensor(rank_in, tiles(bank[7][:, 64:80], 2), mask, ALU.mult))
            step(nc.vector.tensor_scalar(slot_of[:, :, 0:NE], rank_in, -1.0, None, ALU.add))
            hot(slice(0, 1))
            lo_of_moe(MOE_ORDER[1], None)
            dve.wait_ge(logits_exp, 1)
            step(nc.vector.tensor_tensor(expl, expl, mask, ALU.mult))
            step(nc.vector.tensor_reduce(denom, expl, AX_X, ALU.add))
            step(nc.vector.reciprocal(rdenom, denom))
            gates = gate_of[:, :, 0:NE]
            slots = slot_of[:, :, 0:NE]
            nc.vector.tensor_tensor(gates, expl, over_experts(rdenom), ALU.mult)
            step(nc.vector.tensor_scalar(over, bank[7][:, 80:88], P + 0.5, None, ALU.is_gt))
            over_all = over.rearrange("p (a e) -> p a e", a=1).broadcast_to((P, NE, NE))
            step(nc.vector.tensor_tensor(above[:, 0], over_all, c("upto").rearrange("p (e f) -> p e f", e=NE), ALU.mult))
            step(nc.vector.tensor_reduce(cum_over, above[:, 0], AX_X, ALU.add))

            def thrice(v):
                return v.rearrange("p (a e) -> p a e", a=1).broadcast_to((P, 3, NE))

            step(nc.vector.tensor_tensor(chosen, thrice(cum_over), c("spill").rearrange("p (j e) -> p j e", j=3), ALU.is_equal))
            step(nc.vector.tensor_tensor(chosen, chosen, thrice(over), ALU.mult))
            chosen_t = chosen.rearrange("p (a j) e -> p a j e", a=1).broadcast_to((P, TT, 3, NE))

            def over_items(v):
                return v.rearrange("p t (a e) -> p t a e", a=1).broadcast_to((P, TT, 3, NE))

            nc.vector.tensor_tensor(picked, chosen_t, over_items(slots), ALU.mult)
            nc.vector.tensor_tensor(picked_gate, chosen_t, over_items(gates), ALU.mult)
            nc.vector.tensor_tensor(picked_expert, chosen, thrice(c("experts")), ALU.mult)
            step(nc.vector.tensor_reduce(item_tab[:, 12:13], over, AX_X, ALU.add))
            nc.vector.tensor_reduce(slot_of[:, :, NE:NE + 3], picked, AX_X, ALU.add)
            nc.vector.tensor_reduce(gate_of[:, :, NE:NE + 3], picked_gate, AX_X, ALU.add)
            nc.vector.tensor_reduce(item_tab[:, NE:NE + 3], picked_expert, AX_X, ALU.add)
            step(nc.vector.tensor_scalar(item_tab[:, 12:13], item_tab[:, 12:13], float(NE), None, ALU.add))
            nc.vector.tensor_scalar(slot_of[:, :, NE:NE + 3], slot_of[:, :, NE:NE + 3], -float(P), None, ALU.add)
            nc.vector.tensor_copy(item_int[:, 0:13], item_tab[:, 0:13]).then_inc(routed, 1)

            def lo_of_item(before):
                for h, b in enumerate((1, 3)):
                    dve.wait_ge(item_hi, before * 2 + (h + 1))
                    at = (slice(None), slice(4 * h, 4 * h + 4), slice(0, P))
                    nc.vector.tensor_tensor(a_lo[at], tiles(bank[b][:], 4), a_hi[at].bitcast(F32), ALU.subtract).then_inc(item_lo, 1)

            def add_up(before, t):
                dve.wait_ge(acc_ready, before * 4 + 1 + 2 * t)
                for h in range(2):
                    q = 2 * t + h
                    dve.wait_ge(comb_psum, before * 4 + (q + 1))
                    ah = acc[:, t, 512 * h:512 * h + 512]
                    nc.vector.tensor_tensor(ah, ah, bank[COMB_BANKS[q]][:], ALU.add).then_inc(acc_ready, 1)

            lo_of_item(0)
            dve.wait_ge(routed, 1)
            items = dve.value_load(item_int[0:1, 12:13], min_val=NE, max_val=MAX_ITEMS)
            with dve.Fori(0, items) as item:
                for ch in range(NC + 1):
                    if ch:
                        dve.wait_ge(mg_act, item * NC + ch)
                        dve.wait_ge(w_used, item * (PARTS * NU) + (MOE_UNIT + PARTS * (MOE_POS["u", ch - 1, 1] + 1)))
                        nc.vector.tensor_tensor(m_h[:, (ch - 1) % 2, :], m_act[:, (ch - 1) % 2, :], bank[2 + (ch - 1) % 2][:],
                                                ALU.mult).then_inc(mh_ready, 1)
                    if ch < NC:
                        if ch:
                            lo_of_moe(("g", ch, 0), item)
                            lo_of_moe(("g", ch, 1), item)
                        if ch == 1:
                            add_up(item, 0)
                        lo_of_moe(("u", ch, 0), item)
                        if ch == 1:
                            add_up(item, 1)
                        lo_of_moe(("u", ch, 1), item)
                    else:
                        lo_of_moe(("d", ch - 1, 0), item)
                    if ch:
                        dve.wait_ge(mh_hi, item * NC + ch)
                        nc.vector.tensor_tensor(h_lo[:, 0, :], bank[4][:], h_hi[:, 0, :].bitcast(F32), ALU.subtract).then_inc(mh_lo, 1)
                    if ch == NC:
                        lo_of_moe(("d", ch - 1, 1), item)
                    if 0 < ch < NC:
                        lo_of_moe(("d", ch - 1, 0), item)
                        lo_of_moe(("d", ch - 1, 1), item)
                    if ch == 1:
                        for t in range(TT):
                            ins = nc.vector.tensor_scalar(gated[:, t, :], c("iota"), slot_of[:, t, bass.ds(item, 1)],
                                                          gate_of[:, t, bass.ds(item, 1)], ALU.is_equal, ALU.mult)
                        ins.then_inc(gated_ready, 1)
                    if ch == 3:
                        hot(bass.ds(item + 1, 1))
                lo_of_moe(MOE_ORDER[0], item + 1)
                lo_of_item(item + 1)
                lo_of_moe(MOE_ORDER[1], item + 1)

            def sums_ready(t):
                add_up(items, t)
                dve.wait_ge(acc_ready, items * 4 + (2 * t + 3))

            layer_norm(3, sums_ready, lambda t, h: acc[:, t, 512 * h:512 * h + 512])

        @block.tensor
        def _(pe):
            units = [0]
            ident = c("ident")

            def product(target, stationary, moving, first, last):
                (s_hi, s_lo), (m_hi, m_lo) = stationary, moving
                nc.tensor.matmul(target, s_hi, m_hi, start=first, stop=False)
                nc.tensor.matmul(target, s_hi, m_lo, start=False, stop=False)
                return nc.tensor.matmul(target, s_lo, m_hi, start=False, stop=last)

            def next_unit(k):
                n = units[0]
                units[0] += 1
                wait_lo(pe, n)
                return split_pair(n, k)

            def transpose_x(n, t):
                for q in (2 * t, 2 * t + 1):
                    k0 = 4 * (q % 2)
                    if n:
                        pe.wait_ge(x_ready, XQ * (n - 1) + q + 1)
                    for k in range(k0, k0 + 4):
                        last = nc.tensor.transpose(bank[q][:, (k - k0) * P:(k - k0 + 1) * P], xs[:, t, k * P:(k + 1) * P], ident)
                    last.then_inc(xt_psum, 1)

            def project(l, i):
                if i == 0:
                    pe.wait_ge(xt_lo, 4 * (2 * l + 1))
                if i >= 3:
                    pe.wait_ge(z_ready, NZ * l + i - 2)
                m_hi, m_lo = next_unit(KT)
                for h in range(2):
                    to = bank[Z_BANKS[i % 3]][:, 256 * h:256 * h + 256]
                    for k in range(KT):
                        if Z_ORDER[i] == V_G:
                            tokens = slice(h * P, (h + 1) * P)
                            last = product(to, (a_hi[:, k, tokens], a_lo[:, k, tokens]), (m_hi[:, k, :], m_lo[:, k, :]),
                                           k == 0, k == KT - 1)
                        else:
                            channels = slice(h * P, (h + 1) * P)
                            last = product(to, (m_hi[:, k, channels], m_lo[:, k, channels]), (a_hi[:, k, :], a_lo[:, k, :]),
                                           k == 0, k == KT - 1)
                last.then_inc(w_used, 1)

            def scores(l, q):
                width = P * (q + 1)
                pe.wait_ge(roped, 2 * l + 2)
                pe.wait_ge(tables_ready, 1)
                if q:
                    pe.wait_ge(probs_ready, MAPS * (2 * l + 1))
                for t in range(2):
                    for j in range(4):
                        to = bank[j][:, t * width:(t + 1) * width]
                        nc.tensor.matmul(to, ident_b[:], causal_b[:, SEQ - width:], start=True, stop=False)
                        last = nc.tensor.matmul(to, z[Q_G][32 * j:32 * j + 32, t, q * P:(q + 1) * P],
                                                z[K_G][32 * j:32 * j + 32, t, 0:width], start=False, stop=True)
                last.then_inc(scores_psum, 1)

            def transpose_probs(l, q):
                pe.wait_ge(mixed, 2 * l + q + 1)
                if q:
                    pe.wait_ge(probs_ready, MAPS * (2 * l + 2))
                for n, b in enumerate(([7], [0, 1])[q]):
                    for k in range(4):
                        at = (4 * n + k) * P
                        last = nc.tensor.transpose(bank[b][:, k * P:(k + 1) * P], a_mix[:, at:at + P], ident)
                    last.then_inc(aT_psum, 1)

            def attend(l, q):
                pe.wait_ge(aT_ready, 3 * l + 1 + 2 * q)
                for hd in range(HEADS):
                    for kb in range(q + 1):
                        at = (hd * (q + 1) + kb) * P
                        last = nc.tensor.matmul(bank[2][:, 256 * q + VD * hd:256 * q + VD * hd + VD], aT[q][:, at:at + P],
                                                z[V_G][:, kb, VD * hd:VD * hd + VD], start=(kb == 0), stop=(kb == q))
                if q:
                    last.then_inc(o_psum, 1)

            def residual(n, tiles_=range(TT)):
                for t in tiles_:
                    if n:
                        pe.wait_ge(x_ready, XQ * (n - 1) + 2 * t + 2)
                    for h in range(2):
                        nc.tensor.matmul(bank[4 + 2 * t + h][:], c("alpha"), xs[:, t, 512 * h:512 * h + 512], start=True, stop=False)

            def down_tile(t, unit, k0, hi, lo, final):
                m_hi, m_lo = unit
                tokens = slice(t * P, (t + 1) * P)
                for k in range(2):
                    for h in range(2):
                        half = slice(512 * h, 512 * h + 512)
                        last = product(bank[4 + 2 * t + h][:], (hi[:, k0 + k, tokens], lo[:, k0 + k, tokens]),
                                       (m_hi[:, k, half], m_lo[:, k, half]), False, final and k == 1)
                return last

            def down(k0, hi, lo, tile0_done=None):
                unit, final = next_unit(2), tile0_done is not None
                last = down_tile(0, unit, k0, hi, lo, final)
                if final:
                    last.then_inc(tile0_done, 1)
                down_tile(1, unit, k0, hi, lo, final).then_inc(w_used, 1)

            def mix_out(l, n):
                pe.wait_ge(y_lo, NWO * l + n + 1)
                down(2 * WO_ORDER[n], a_hi, a_lo, wo_psum if n == NWO - 1 else None)

            def dense_in(kind, j):
                b = 2 * (j % 2) + (kind == "u")
                if j == 0:
                    pe.wait_ge(xt_lo, 8)
                if j > 1:
                    pe.wait_ge(h_ready, j - 1)
                m_hi, m_lo = next_unit(KT)
                for f in range(2):
                    hidden = slice(f * P, (f + 1) * P)
                    for k in range(KT):
                        last = product(bank[b][:, 256 * f:256 * f + 256], (m_hi[:, k, hidden], m_lo[:, k, hidden]),
                                       (a_hi[:, k, :], a_lo[:, k, :]), k == 0, k == KT - 1)
                last.then_inc(w_used, 1)

            h_hi_t = h_hi[:].rearrange("p b (f t) -> p (b f) t", f=2)
            h_lo_t = h_lo[:].rearrange("p b (f t) -> p (b f) t", f=2)

            pe.wait_ge(first_loaded, 16)
            for l in range(DEPTH):
                for t in range(TT):
                    if l == 0:
                        pe.wait_ge(x_loaded[t], 16)
                    transpose_x(2 * l, t)
                for i in range(NZ):
                    project(l, i)
                    if l == 0 and i == 1:
                        pe.wait_ge(rows_loaded, 16 * 7)
                        for k in range(DEPTH):
                            nc.tensor.transpose(bank[2 + k][:, 0:NR], rows[0:NR, k, :], ident[0:NR, 0:NR]).then_inc(cols_psum, 1)
                    if i in (3, 4):
                        if i == 3:
                            pe.wait_ge(consts_loaded, 16)
                        n, g = ((0, Q_G), (1, K_G))[i - 3]
                        pe.wait_ge(z_ready, NZ * l + i)
                        nc.tensor.matmul(bank[n][:], c("rot"), z[g].rearrange("p h t -> p (h t)"), start=True, stop=True).then_inc(rot_psum, 1)
                    if i == 5:
                        if l == 0:
                            pe.wait_ge(cols_ready, DEPTH)
                        scores(l, 0)
                    if i == 6:
                        scores(l, 1)
                    if i == 7:
                        transpose_probs(l, 0)
                transpose_probs(l, 1)
                pe.wait_ge(aT_ready, 3 * l + 1)
                pe.wait_ge(z_ready, NZ * (l + 1))
                residual(2 * l)
                attend(l, 0)
                attend(l, 1)
                pe.wait_ge(pool_diff, l + 1)
                pe.wait_ge(pool_loaded, 16 * 4 * DEPTH)
                for h in range(2):
                    last = nc.tensor.matmul(bank[3][:, 256 * h:256 * h + 256], pool_mat[:, l, h, :], y32[:, h, :], start=True, stop=True)
                last.then_inc(pool_psum, 1)
                mix_out(l, 0)
                pe.wait_ge(o_normed, l + 1)
                for ct in range(2):
                    for q in range(TT):
                        last = nc.tensor.transpose(bank[0][:, ct * SEQ + q * P:ct * SEQ + (q + 1) * P],
                                                   o_sq[:, q].rearrange("p h e -> p (h e)")[:, ct * P:(ct + 1) * P], ident)
                last.then_inc(oT_psum, 1)
                mix_out(l, 1)
                pe.wait_ge(conf_conv, (l + 1) * 2 * CONF_K)
                for h in range(2):
                    last = nc.tensor.matmul(bank[1][:, 0:256], c("mean"), conf_acc[:, h, :], start=(h == 0), stop=(h == 1))
                last.then_inc(conf_mean, 1)
                pe.wait_ge(conf_sq, l + 1)
                for h in range(2):
                    last = nc.tensor.matmul(bank[1][:, 256:512], c("mean"), xsq[:, h, :], start=(h == 0), stop=(h == 1))
                last.then_inc(conf_var, 1)
                mix_out(l, 2)
                mix_out(l, 3)
                for t in range(TT):
                    transpose_x(2 * l + 1, t)
                    if l == 0:
                        residual(1, (t,))
                if l == 0:
                    for kind, j in DENSE_ORDER[:-2]:
                        if kind == "d":
                            pe.wait_ge(h_lo_ready, j + 1)
                            down(2 * (j % 2), h_hi_t, h_lo_t)
                        else:
                            dense_in(kind, j)
                    last_units = []
                    for t in range(TT):
                        for n, j in enumerate((FP - 2, FP - 1)):
                            if t == 0:
                                pe.wait_ge(h_lo_ready, j + 1)
                                last_units.append(next_unit(2))
                            last = down_tile(t, last_units[n], 2 * (j % 2), h_hi_t, h_lo_t, n == 1)
                            if t == 1:
                                last.then_inc(w_used, 1)
                        if t == 0:
                            last.then_inc(ffn_psum, 1)
            assert units[0] == MOE_UNIT, (units, MOE_UNIT)

            pe.wait_ge(xt_lo, 16)
            pe.wait_ge(router_split, 2)
            for k in range(KT):
                last = product(bank[7][0:NE, 256:512], (router_hi[:, k, :], router_lo[:, k, :]), (a_hi[:, k, :], a_lo[:, k, :]),
                               k == 0, k == KT - 1)
            last.then_inc(logits_psum, 1)
            pe.wait_ge(logitsT_ready, 1)
            for t in range(TT):
                last = nc.tensor.transpose(bank[7][:, NE * t:NE * t + NE], logitsT[:, t * P:(t + 1) * P], ident[0:NE, 0:NE])
            last.then_inc(logits_psum, 1)
            pe.wait_ge(mask_ready, 1)
            for at, pieces in ((64, (("tri", 0),)), (72, (("ones", 0), ("tri", 1))), (80, (("ones", 0), ("ones", 1)))):
                for n, (table, t) in enumerate(pieces):
                    last = nc.tensor.matmul(bank[7][:, at:at + NE], count_b[table], mask_b[:, t, :], start=(n == 0), stop=(n == len(pieces) - 1))
            last.then_inc(ranks_psum, 1)

            def gather(before):
                pe.wait_ge(hot_ready, before + 1)
                for k in range(KT):
                    for t in range(TT):
                        last = nc.tensor.matmul(bank[1 + 2 * (k // 4)][:, (k % 4) * P:(k % 4 + 1) * P], xs[:, t, k * P:(k + 1) * P],
                                                one_hot[:, t, :], start=(t == 0), stop=(t == TT - 1))
                    if k % 4 == 3:
                        last.then_inc(gather_psum, 1)

            def moe_unit(unit, item):
                kind, ch, half = unit
                n = MOE_UNIT + MOE_POS[unit]

                def part_ready(s):
                    pe.wait_ge(w_lo_ready, item * (PARTS * NU) + (LO_BASE + PARTS * MOE_POS[unit] + s + 1))

                if kind == "d":
                    m_hi, m_lo = split_pair(n, 2)
                    for k in range(2):
                        part_ready(k)
                        tile = slice((2 * half + k) * P, (2 * half + k + 1) * P)
                        for h in range(2):
                            cols_ = slice(512 * h, 512 * h + 512)
                            last = product(bank[5 + h][:], (h_hi[:, 0, tile], h_lo[:, 0, tile]), (m_hi[:, k, cols_], m_lo[:, k, cols_]),
                                           ch == 0 and half == 0 and k == 0, ch == NC - 1 and half == 1 and k == 1)
                        last.then_inc(w_used, 1)
                else:
                    m_hi, m_lo = split_pair(n, 4)
                    b = ch % 2 + 2 * (kind == "u")
                    for k in range(4):
                        if k % 2 == 0:
                            part_ready(k // 2)
                        last = product(bank[b][:], (a_hi[:, 4 * half + k, 0:P], a_lo[:, 4 * half + k, 0:P]), (m_hi[:, k, :], m_lo[:, k, :]),
                                       half == 0 and k == 0, half == 1 and k == 3)
                        if k % 2:
                            last.then_inc(w_used, 1)

            def transpose_h(ch, item):
                pe.wait_ge(mh_ready, item * NC + (ch + 1))
                for f in range(4):
                    last = nc.tensor.transpose(bank[4][:, f * P:(f + 1) * P], m_h[:, ch % 2, f * P:(f + 1) * P], ident)
                last.then_inc(mhT_psum, 1)

            def combine(before):
                pe.wait_ge(gT_ready, before + 1)
                for q in range(4):
                    t, h = q // 2, q % 2
                    if t == 0:
                        pe.wait_ge(my_ready, before * 2 + (h + 1))
                    nc.tensor.matmul(bank[COMB_BANKS[q]][:], gatedT[:, t * P:(t + 1) * P], y_sb[:, 512 * h:512 * h + 512],
                                     start=True, stop=True).then_inc(comb_psum, 1)

            gather(0)
            pe.wait_ge(routed, 1)
            items = pe.value_load(item_int[0:1, 12:13], min_val=NE, max_val=MAX_ITEMS)
            with pe.Fori(0, items) as item:
                for ch in range(NC + 1):
                    if ch < NC:
                        if ch == 0:
                            pe.wait_ge(item_lo, item * 2 + 1)
                        moe_unit(("g", ch, 0), item)
                        if ch == 0:
                            pe.wait_ge(item_lo, item * 2 + 2)
                        moe_unit(("g", ch, 1), item)
                    if ch:
                        if ch == 1:
                            pe.wait_ge(acc_ready, item * 4 + 2)
                        transpose_h(ch - 1, item)
                    if ch < NC:
                        moe_unit(("u", ch, 0), item)
                        moe_unit(("u", ch, 1), item)
                    if ch == 0:
                        combine(item)
                    if ch == 2:
                        pe.wait_ge(gated_ready, item + 1)
                        for t in range(TT):
                            last = nc.tensor.transpose(bank[7][:, t * P:(t + 1) * P], gated[:, t, :], ident)
                        last.then_inc(gT_psum, 1)
                    if ch == NC:
                        gather(item + 1)
                    if ch == 1:
                        pe.wait_ge(acc_ready, item * 4 + 5)
                    if ch:
                        pe.wait_ge(mh_lo, item * NC + ch)
                        moe_unit(("d", ch - 1, 0), item)
                        moe_unit(("d", ch - 1, 1), item)
            combine(items)


_INS = ["x", "positions", "w_in", "w_o", "pool_w", "pool_scale", "sconv_w", "diff_lambda", "diff_subln_g",
        "conf_dw", "conf_ln_g", "conf_ln_b", "ln1_g", "ln1_b", "ln2_g", "ln2_b", "ffn_wg", "ffn_wu", "ffn_wd",
        "router_w", "moe_wg", "moe_wu", "moe_wd"]


def kernel(**inputs):
    import concourse.bacc as _bacc
    from concourse.bass_utils import run_bass_kernel_spmd as _run

    nc = _bacc.Bacc("TRN2", target_bir_lowering=False, num_devices=1)
    arrays, args = {}, []
    for name, a in [("constants", CONSTANTS)] + [(n, np.ascontiguousarray(inputs[n])) for n in _INS]:
        arrays[f"in_{name}_dram"] = a
        args.append(nc.dram_tensor(f"in_{name}_dram", a.shape, mybir.dt.from_np(a.dtype), kind="ExternalInput").ap())
    args.append(nc.dram_tensor("out_0_dram", (1, SEQ, D), F32, kind="ExternalOutput").ap())
    hybrid_trunk(nc, *args)
    r = _run(nc, [arrays], core_ids=[0])
    return r.results[0]["out_0_dram"]
```
